# Optimizing a Trainium2 kernel written in Bass

```python
import math
import jax, jax.numpy as jnp
from jax import lax
import numpy as np

D_MODEL = 1024
BATCH = 1
SEQ = 512
DEPTH = 1

CHUNK = 64
Q_BLOCK = 128
EPS = 1e-6
D_MIX = D_MODEL
M_HEADS = 4
M_WIDTH = D_MIX // 2
M_HEAD_DIM = M_WIDTH // M_HEADS
CONV_WIDTH = 4
A_HEADS = 4
A_WIDTH = D_MIX - M_WIDTH
A_HEAD_DIM = A_WIDTH // A_HEADS
A_QK_DIM = A_HEAD_DIM // 2
IN_SIZES = (2 * M_WIDTH, M_WIDTH, M_WIDTH, M_HEADS, M_HEADS, A_WIDTH, A_WIDTH, A_WIDTH)
IN_COLS = sum(IN_SIZES)
IN_SPLITS = tuple(int(s) for s in np.cumsum(IN_SIZES)[:-1])
N_GROUPS = 4
EXPERTS_PER_GROUP = 8
N_EXPERTS = N_GROUPS * EXPERTS_PER_GROUP
TOP_K = 2
D_EXPERT = D_MODEL // 2
MOE_BLOCK = 256


def rms_norm(x, w):
    xf = x.astype(jnp.float32)
    y = xf * lax.rsqrt(jnp.mean(xf * xf, axis=-1, keepdims=True) + EPS)
    return (y * w.astype(jnp.float32)).astype(x.dtype)

def causal_conv(x, w, b):
    S = x.shape[1]
    xp = jnp.pad(x, ((0, 0), (CONV_WIDTH - 1, 0), (0, 0)))
    out = b
    for j in range(CONV_WIDTH):
        out = out + xp[:, j:j + S] * w[j]
    return out

def mlstm_chunkwise(q, k, v, i_pre, f_pre):
    Bn, S, H, Dh = q.shape
    NC = S // CHUNK

    def to_chunks(t):
        t = t.astype(jnp.float32).reshape((Bn, NC, CHUNK) + t.shape[2:])
        return jnp.moveaxis(jnp.moveaxis(t, 1, 0), 3, 2)

    qc = to_chunks(q)
    kc = to_chunks(k) * (Dh ** -0.5)
    vc = to_chunks(v)
    ic = to_chunks(i_pre)
    fc = jax.nn.log_sigmoid(to_chunks(f_pre))
    causal = jnp.tril(jnp.ones((CHUNK, CHUNK), dtype=bool))

    def step(carry, inp):
        C, n, m = carry
        q_c, k_c, v_c, i_c, lf_c = inp
        b = jnp.cumsum(lf_c, axis=-1)
        log_d = jnp.where(causal, b[..., :, None] - b[..., None, :] + i_c[..., None, :], -jnp.inf)
        log_inter = b + m[..., None]
        m_t = jnp.maximum(log_inter, jnp.max(log_d, axis=-1))
        d = jnp.exp(log_d - m_t[..., None])
        inter = jnp.exp(log_inter - m_t)
        s = jnp.einsum('bhtd,bhsd->bhts', q_c, k_c) * d
        num = jnp.einsum('bhts,bhse->bhte', s, v_c) + inter[..., None] * jnp.einsum('bhtd,bhde->bhte', q_c, C)
        den = jnp.sum(s, axis=-1) + inter * jnp.einsum('bhtd,bhd->bht', q_c, n)
        h = num / jnp.maximum(jnp.abs(den), jnp.exp(-m_t))[..., None]
        b_end = b[..., -1]
        log_w = b_end[..., None] - b + i_c
        m_new = jnp.maximum(b_end + m, jnp.max(log_w, axis=-1))
        w = jnp.exp(log_w - m_new[..., None])
        decay = jnp.exp(b_end + m - m_new)
        C_new = decay[..., None, None] * C + jnp.einsum('bhs,bhsd,bhse->bhde', w, k_c, v_c)
        n_new = decay[..., None] * n + jnp.einsum('bhs,bhsd->bhd', w, k_c)
        return (C_new, n_new, m_new), h

    init = (jnp.zeros((Bn, H, Dh, Dh), jnp.float32),
            jnp.zeros((Bn, H, Dh), jnp.float32),
            jnp.zeros((Bn, H), jnp.float32))
    _, h = lax.scan(step, init, (qc, kc, vc, ic, fc))
    h = jnp.moveaxis(jnp.moveaxis(h, 0, 1), 2, 3)
    return h.reshape(Bn, S, H, Dh)

def diff_attention(q, k, v, q_norm_w, k_norm_w, lq1, lk1, lq2, lk2, a_norm_w, lambda_init):
    Bn, S = q.shape[:2]
    NQ = S // Q_BLOCK
    q = rms_norm(q, q_norm_w)
    k = rms_norm(k, k_norm_w)
    f32 = jnp.float32
    lam = (jnp.exp(jnp.sum(lq1.astype(f32) * lk1.astype(f32)))
           - jnp.exp(jnp.sum(lq2.astype(f32) * lk2.astype(f32))) + lambda_init)
    kt = jnp.transpose(k, (0, 2, 3, 1, 4))
    vt = jnp.transpose(v, (0, 2, 1, 3))
    qb = q.reshape(Bn, NQ, Q_BLOCK, A_HEADS, 2, A_QK_DIM).transpose(1, 0, 3, 4, 2, 5)
    key_chunk = jnp.arange(S) // CHUNK
    scale = A_QK_DIM ** -0.5

    def block(args):
        q_blk, idx = args
        q_chunk = (idx * Q_BLOCK + jnp.arange(Q_BLOCK)) // CHUNK
        mask = key_chunk[None, :] <= q_chunk[:, None]
        s = jnp.einsum('bhcqd,bhcsd->bhcqs', q_blk, kt).astype(f32) * scale
        p = jax.nn.softmax(jnp.where(mask, s, -jnp.inf), axis=-1)
        attn = p[:, :, 0] - lam * p[:, :, 1]
        return jnp.einsum('bhqs,bhsd->bhqd', attn.astype(v.dtype), vt)

    o = lax.map(block, (qb, jnp.arange(NQ)))
    o = o.transpose(1, 0, 3, 2, 4).reshape(Bn, S, A_HEADS, A_HEAD_DIM)
    o = rms_norm(o, a_norm_w) * (1.0 - lambda_init)
    return o.reshape(Bn, S, A_WIDTH)

def hybrid_mixer(h, w_in, b_igate, b_fgate, conv_w, conv_b, m_norm_w, q_norm_w, k_norm_w,
                 lq1, lk1, lq2, lk2, a_norm_w, w_out, lambda_init):
    Bn, S, _ = h.shape
    proj = h @ w_in
    mqk, mv, mo, mi, mf, aq, ak, av = jnp.split(proj, IN_SPLITS, axis=-1)
    qk = jax.nn.silu(causal_conv(mqk, conv_w, conv_b))
    mq, mk = jnp.split(qk, 2, axis=-1)
    shp = (Bn, S, M_HEADS, M_HEAD_DIM)
    hm = mlstm_chunkwise(mq.reshape(shp), mk.reshape(shp), mv.reshape(shp), mi + b_igate, mf + b_fgate)
    hm = jax.nn.sigmoid(mo).reshape(shp) * hm.astype(h.dtype)
    hm = rms_norm(hm, m_norm_w).reshape(Bn, S, M_WIDTH)
    ha = diff_attention(aq.reshape(Bn, S, A_HEADS, 2, A_QK_DIM), ak.reshape(Bn, S, A_HEADS, 2, A_QK_DIM),
                        av.reshape(Bn, S, A_HEADS, A_HEAD_DIM), q_norm_w, k_norm_w,
                        lq1, lk1, lq2, lk2, a_norm_w, lambda_init)
    return jnp.concatenate([hm, ha], axis=-1) @ w_out

def hierarchical_moe(h, w_group, b_group, w_expert, b_expert, w_gate, w_up, w_down):
    Bn, S, D = h.shape
    T = Bn * S
    xt = h.reshape(T, D)
    f32 = jnp.float32
    g_logits = (xt @ w_group).astype(f32) + b_group.astype(f32)
    g_prob = jax.nn.softmax(g_logits, axis=-1)
    g_sel = jnp.argmax(g_logits, axis=-1)
    g_w = jnp.take_along_axis(g_prob, g_sel[:, None], axis=1)[:, 0]
    e_logits = ((xt @ w_expert).astype(f32) + b_expert.astype(f32)).reshape(T, N_GROUPS, EXPERTS_PER_GROUP)
    e_in = jnp.take_along_axis(e_logits, g_sel[:, None, None], axis=1)[:, 0]
    top_vals, top_idx = lax.top_k(e_in, TOP_K)
    weights = g_w[:, None] * jax.nn.softmax(top_vals, axis=-1)
    eid = (g_sel[:, None] * EXPERTS_PER_GROUP + top_idx).reshape(-1)
    A = T * TOP_K
    tok = jnp.arange(A) // TOP_K
    counts = jax.ops.segment_sum(jnp.ones_like(eid), eid, num_segments=N_EXPERTS)
    padded = ((counts + MOE_BLOCK - 1) // MOE_BLOCK) * MOE_BLOCK
    pad_end = jnp.cumsum(padded)
    pad_start = pad_end - padded
    start = jnp.cumsum(counts) - counts
    order = jnp.argsort(eid)
    eid_sorted = eid[order]
    dest_sorted = pad_start[eid_sorted] + (jnp.arange(A) - start[eid_sorted])
    dest = jnp.zeros((A,), jnp.int32).at[order].set(dest_sorted.astype(jnp.int32))
    P = ((A + MOE_BLOCK - 1) // MOE_BLOCK) * MOE_BLOCK + N_EXPERTS * MOE_BLOCK
    NB = P // MOE_BLOCK
    block_start = jnp.arange(NB) * MOE_BLOCK
    block_expert = jnp.minimum(jnp.sum(pad_end[None, :] <= block_start[:, None], axis=1), N_EXPERTS - 1)
    x_buf = jnp.zeros((P, D), h.dtype).at[dest].set(xt[tok])

    def expert_block(args):
        xb, e = args
        hid = jax.nn.silu(xb @ w_gate[e]) * (xb @ w_up[e])
        return hid @ w_down[e]

    y_buf = lax.map(expert_block, (x_buf.reshape(NB, MOE_BLOCK, D), block_expert)).reshape(P, D)
    y = jnp.sum(y_buf[dest].reshape(T, TOP_K, D) * weights[..., None].astype(h.dtype), axis=1)
    return y.reshape(Bn, S, D)

def first_inputs(seed: int = 0) -> dict:
    key = jax.random.key(seed)
    ks = jax.random.split(key, 24)
    nrm = jax.random.normal
    f32 = jnp.float32
    L = DEPTH
    gain = lambda k, n: 1.0 + 0.01 * nrm(k, (L, n), f32)
    return {
        'x': nrm(ks[0], (BATCH, SEQ, D_MODEL), f32),
        'norm1_w': gain(ks[1], D_MODEL),
        'w_in': nrm(ks[2], (L, D_MODEL, IN_COLS), f32) * D_MODEL ** -0.5,
        'b_igate': 0.1 * nrm(ks[3], (L, M_HEADS), f32),
        'b_fgate': jnp.linspace(3.0, 6.0, M_HEADS, dtype=f32)[None, :] + 0.1 * nrm(ks[4], (L, M_HEADS), f32),
        'conv_w': nrm(ks[5], (L, CONV_WIDTH, 2 * M_WIDTH), f32) * CONV_WIDTH ** -0.5,
        'conv_b': 0.01 * nrm(ks[6], (L, 2 * M_WIDTH), f32),
        'm_norm_w': gain(ks[7], M_HEAD_DIM),
        'q_norm_w': gain(ks[8], A_QK_DIM),
        'k_norm_w': gain(ks[9], A_QK_DIM),
        'lambda_q1': 0.1 * nrm(ks[10], (L, A_QK_DIM), f32),
        'lambda_k1': 0.1 * nrm(ks[11], (L, A_QK_DIM), f32),
        'lambda_q2': 0.1 * nrm(ks[12], (L, A_QK_DIM), f32),
        'lambda_k2': 0.1 * nrm(ks[13], (L, A_QK_DIM), f32),
        'a_norm_w': gain(ks[14], A_HEAD_DIM),
        'w_out': nrm(ks[15], (L, D_MIX, D_MODEL), f32) * D_MIX ** -0.5,
        'norm2_w': gain(ks[16], D_MODEL),
        'w_group': nrm(ks[17], (L, D_MODEL, N_GROUPS), f32) * D_MODEL ** -0.5,
        'b_group': 0.01 * nrm(ks[18], (L, N_GROUPS), f32),
        'w_expert': nrm(ks[19], (L, D_MODEL, N_EXPERTS), f32) * D_MODEL ** -0.5,
        'b_expert': 0.01 * nrm(ks[20], (L, N_EXPERTS), f32),
        'w_gate': nrm(ks[21], (L, N_EXPERTS, D_MODEL, D_EXPERT), f32) * D_MODEL ** -0.5,
        'w_up': nrm(ks[22], (L, N_EXPERTS, D_MODEL, D_EXPERT), f32) * D_MODEL ** -0.5,
        'w_down': nrm(ks[23], (L, N_EXPERTS, D_EXPERT, D_MODEL), f32) * D_EXPERT ** -0.5,
    }

def first_block(x, norm1_w, w_in, b_igate, b_fgate, conv_w, conv_b, m_norm_w, q_norm_w, k_norm_w,
              lambda_q1, lambda_k1, lambda_q2, lambda_k2, a_norm_w, w_out, norm2_w,
              w_group, b_group, w_expert, b_expert, w_gate, w_up, w_down):
    for l in range(DEPTH):
        lambda_init = 0.8 - 0.6 * math.exp(-0.3 * l)
        h = rms_norm(x, norm1_w[l])
        x = x + hybrid_mixer(h, w_in[l], b_igate[l], b_fgate[l], conv_w[l], conv_b[l], m_norm_w[l],
                             q_norm_w[l], k_norm_w[l], lambda_q1[l], lambda_k1[l], lambda_q2[l],
                             lambda_k2[l], a_norm_w[l], w_out[l], lambda_init)
        h = rms_norm(x, norm2_w[l])
        x = x + hierarchical_moe(h, w_group[l], b_group[l], w_expert[l], b_expert[l],
                                 w_gate[l], w_up[l], w_down[l])
    return x


PLE_DIM = 256
MIX_WIDTH = D_MODEL
POOL_WIDTH = MIX_WIDTH // 2
POOL_WINDOWS = (2, 4, 8, 16)
N_POOL_GROUPS = len(POOL_WINDOWS)
POOL_GROUP = POOL_WIDTH // N_POOL_GROUPS
HEAD_DIM = 64
ATTN_WIDTH = MIX_WIDTH - POOL_WIDTH
N_Q_HEADS = ATTN_WIDTH // HEAD_DIM
N_KV_HEADS = 2
GQA_GROUP = N_Q_HEADS // N_KV_HEADS
KV_WIDTH = N_KV_HEADS * HEAD_DIM
IN_WIDTH = POOL_WIDTH + ATTN_WIDTH + 2 * KV_WIDTH
WINDOW = 128
BLOCK = 128
D_FF = 4 * D_MODEL
LN_EPS = 1e-5
DEEPNORM_ALPHA = (2 * DEPTH) ** 0.25
DEEPNORM_BETA = (8 * DEPTH) ** -0.25
NEG_INF = -1e30


def layer_norm(x, g, b):
    xf = x.astype(jnp.float32)
    mu = jnp.mean(xf, axis=-1, keepdims=True)
    xc = xf - mu
    var = jnp.mean(xc * xc, axis=-1, keepdims=True)
    y = xc * lax.rsqrt(var + LN_EPS) * g.astype(jnp.float32) + b.astype(jnp.float32)
    return y.astype(x.dtype)

def alibi_slopes(n_heads):
    h = jnp.arange(1, n_heads + 1, dtype=jnp.float32)
    return jnp.exp2(-8.0 * h / n_heads)

def pool_mixer(u, w_pool, pool_scale):
    B, S, _ = u.shape
    uf = u.astype(jnp.float32)
    cs = jnp.pad(jnp.cumsum(uf, axis=1), ((0, 0), (1, 0), (0, 0)))
    t = jnp.arange(S)
    outs = []
    for g, w in enumerate(POOL_WINDOWS):
        sl = slice(g * POOL_GROUP, (g + 1) * POOL_GROUP)
        c = cs[..., sl]
        lo = jnp.maximum(t + 1 - w, 0)
        win_sum = c[:, 1:] - c[:, lo]
        count = (t + 1 - lo).astype(jnp.float32)[None, :, None]
        outs.append(win_sum / count - uf[..., sl])
    d = jnp.stack(outs, axis=2).astype(u.dtype)
    y = jnp.einsum('bsgc,gcd->bsgd', d, w_pool).reshape(B, S, POOL_WIDTH)
    return y * pool_scale

def sliding_window_attention(q, k, v, sinks):
    B, S = q.shape[:2]
    nb = S // BLOCK
    qb = q.reshape(B, nb, BLOCK, N_KV_HEADS, GQA_GROUP, HEAD_DIM)

    def band(a):
        ab = a.reshape(B, nb, BLOCK, N_KV_HEADS, HEAD_DIM)
        prev = jnp.pad(ab, ((0, 0), (1, 0), (0, 0), (0, 0), (0, 0)))[:, :-1]
        return jnp.concatenate([prev, ab], axis=2)

    kb, vb = band(k), band(v)
    scale = 1.0 / math.sqrt(HEAD_DIM)
    scores = jnp.einsum('bnqkgd,bnjkd->bnkgqj', qb, kb).astype(jnp.float32) * scale

    qi = jnp.arange(BLOCK)
    kj = jnp.arange(2 * BLOCK)
    dist = (qi[:, None] + BLOCK - kj[None, :])
    in_band = (dist >= 0) & (dist < WINDOW)
    key_pos = jnp.arange(nb)[:, None] * BLOCK - BLOCK + kj[None, :]
    mask = in_band[None] & (key_pos >= 0)[:, None, :]

    slopes = alibi_slopes(N_Q_HEADS).reshape(N_KV_HEADS, GQA_GROUP)
    bias = -slopes[:, :, None, None] * dist.astype(jnp.float32)[None, None]
    scores = jnp.where(mask[None, :, None, None], scores + bias[None, None], NEG_INF)

    sink = sinks.astype(jnp.float32).reshape(1, 1, N_KV_HEADS, GQA_GROUP, 1, 1)
    m = jnp.maximum(jnp.max(scores, axis=-1, keepdims=True), sink)
    e = jnp.exp(scores - m)
    denom = jnp.sum(e, axis=-1, keepdims=True) + jnp.exp(sink - m)
    probs = (e / denom).astype(v.dtype)
    out = jnp.einsum('bnkgqj,bnjkd->bnqkgd', probs, vb)
    return out.reshape(B, S, ATTN_WIDTH)

def second_inputs(seed: int = 0) -> dict:
    key = jax.random.key(seed)
    ks = jax.random.split(key, 16)
    f32 = jnp.float32

    def nrm(k, shape, std):
        return jax.random.normal(k, shape, f32) * std

    return {
        "x": nrm(ks[0], (BATCH, SEQ, D_MODEL), 1.0),
        "p": nrm(ks[1], (DEPTH, BATCH, SEQ, PLE_DIM), 1.0),
        "w_in": nrm(ks[2], (DEPTH, D_MODEL, IN_WIDTH), D_MODEL ** -0.5),
        "w_pool": nrm(ks[3], (DEPTH, N_POOL_GROUPS, POOL_GROUP, POOL_GROUP), POOL_GROUP ** -0.5),
        "pool_scale": 1.0 + nrm(ks[4], (DEPTH, POOL_WIDTH), 0.1),
        "attn_sinks": nrm(ks[5], (DEPTH, N_Q_HEADS), 0.5),
        "w_out": nrm(ks[6], (DEPTH, MIX_WIDTH, D_MODEL), MIX_WIDTH ** -0.5 * DEEPNORM_BETA),
        "ln1_g": 1.0 + nrm(ks[7], (DEPTH, D_MODEL), 0.05),
        "ln1_b": nrm(ks[8], (DEPTH, D_MODEL), 0.02),
        "w_ff1": nrm(ks[9], (DEPTH, D_MODEL, D_FF), D_MODEL ** -0.5),
        "w_ff2": nrm(ks[10], (DEPTH, D_FF, D_MODEL), D_FF ** -0.5 * DEEPNORM_BETA),
        "ln2_g": 1.0 + nrm(ks[11], (DEPTH, D_MODEL), 0.05),
        "ln2_b": nrm(ks[12], (DEPTH, D_MODEL), 0.02),
        "w_ple": nrm(ks[13], (DEPTH, PLE_DIM, D_MODEL), PLE_DIM ** -0.5),
        "w_ple_gate": nrm(ks[14], (DEPTH, D_MODEL, D_MODEL), D_MODEL ** -0.5),
        "b_ple_gate": nrm(ks[15], (DEPTH, D_MODEL), 0.02),
    }

def second_block(x, p, w_in, w_pool, pool_scale, attn_sinks, w_out, ln1_g, ln1_b,
              w_ff1, w_ff2, ln2_g, ln2_b, w_ple, w_ple_gate, b_ple_gate):
    B, S, _ = x.shape
    h = x
    for i in range(DEPTH):
        z = h @ w_in[i]
        u_pool = z[..., :POOL_WIDTH]
        q = z[..., POOL_WIDTH:POOL_WIDTH + ATTN_WIDTH].reshape(B, S, N_Q_HEADS, HEAD_DIM)
        k = z[..., POOL_WIDTH + ATTN_WIDTH:POOL_WIDTH + ATTN_WIDTH + KV_WIDTH].reshape(B, S, N_KV_HEADS, HEAD_DIM)
        v = z[..., POOL_WIDTH + ATTN_WIDTH + KV_WIDTH:].reshape(B, S, N_KV_HEADS, HEAD_DIM)

        y_pool = pool_mixer(u_pool, w_pool[i], pool_scale[i])
        y_attn = sliding_window_attention(q, k, v, attn_sinks[i])
        mix = jnp.concatenate([y_pool, y_attn], axis=-1) @ w_out[i]
        h = layer_norm(DEEPNORM_ALPHA * h + mix, ln1_g[i], ln1_b[i])

        ff = jnp.square(jax.nn.relu(h @ w_ff1[i])) @ w_ff2[i]
        h = layer_norm(DEEPNORM_ALPHA * h + ff, ln2_g[i], ln2_b[i])

        gate = jax.nn.sigmoid(h @ w_ple_gate[i] + b_ple_gate[i])
        h = h + gate * (p[i] @ w_ple[i])
    return h


def setup_inputs(seed=0):
    out = dict(first_inputs(seed))
    for name, value in second_inputs(seed + 1).items():
        if name != "x":
            out[name + "_2"] = value
    return out


def reference(
    x, norm1_w, w_in, b_igate, b_fgate, conv_w, conv_b, m_norm_w, q_norm_w, k_norm_w, lambda_q1,
    lambda_k1, lambda_q2, lambda_k2, a_norm_w, w_out, norm2_w, w_group, b_group, w_expert,
    b_expert, w_gate, w_up, w_down, p_2, w_in_2, w_pool_2, pool_scale_2, attn_sinks_2, w_out_2,
    ln1_g_2, ln1_b_2, w_ff1_2, w_ff2_2, ln2_g_2, ln2_b_2, w_ple_2, w_ple_gate_2, b_ple_gate_2,
):
    x = first_block(
        x, norm1_w, w_in, b_igate, b_fgate, conv_w, conv_b, m_norm_w, q_norm_w, k_norm_w,
        lambda_q1, lambda_k1, lambda_q2, lambda_k2, a_norm_w, w_out, norm2_w, w_group, b_group,
        w_expert, b_expert, w_gate, w_up, w_down,
    )
    return second_block(
        x, p_2, w_in_2, w_pool_2, pool_scale_2, attn_sinks_2, w_out_2, ln1_g_2, ln1_b_2,
        w_ff1_2, w_ff2_2, ln2_g_2, ln2_b_2, w_ple_2, w_ple_gate_2, b_ple_gate_2,
    )


_drawn_inputs = setup_inputs


def setup_inputs(seed=0):
    import zlib

    import numpy as np

    out = dict(_drawn_inputs(seed))
    spreads = {}
    factors = {'norm1_w': 2.843,
     'b_igate': 64.0,
     'conv_b': 4.494,
     'm_norm_w': 3.349,
     'q_norm_w': 5.755,
     'k_norm_w': 4.75,
     'lambda_q1': 5.272,
     'a_norm_w': 3.881,
     'norm2_w': 3.847,
     'b_group': 6.177,
     'b_expert': 4.472,
     'attn_sinks_2': 200.0,
     'ln1_b_2': 2.889,
     'ln2_b_2': 3.154,
     'b_ple_gate_2': 8.0}
    for name, (base, spread) in spreads.items():
        noise = np.random.default_rng([zlib.crc32(name.encode()), seed]).standard_normal(out[name].shape)
        drawn = base * np.exp(spread * noise) if base else spread * noise
        out[name] = __import__('jax').numpy.asarray(drawn.astype(out[name].dtype))
    for name, factor in factors.items():
        out[name] = (out[name] * factor).astype(out[name].dtype)
    return out
```

```python
from contextlib import ExitStack

import numpy as np

import concourse.bass as bass
from concourse import mybir

F32 = mybir.dt.float32
BF16 = mybir.dt.bfloat16
I32 = mybir.dt.int32
ALU = mybir.AluOpType
ACT = mybir.ActivationFunctionType
AX = mybir.AxisListType.X

P = 128
T = 512
D = 1024
TT = T // P
DT = D // P
RING = 6
UNIT = 4096
NEG = -1e30
EPS = 1e-6
LN_EPS = 1e-5
HEADS = 4
HD = 128
QK = 64
LAMBDA_INIT = 0.8 - 0.6
NE = 32
NG = 4
EG = NE // NG
FT = 4
BLK = 96
PER_EXPERT_MAX = -(-T // BLK)
BLOCKS_MAX = 2 * T // BLK + NE
BLOCKS_HELD = BLOCKS_MAX + PER_EXPERT_MAX
SLOTS = BLOCKS_HELD * BLK
NO_ROW = 2 * T
W2_HEADS = 8
PAIRS = W2_HEADS // 2
WINDOW = 128
FFT = 4 * D // P
POOL_WINDOWS = (2, 4, 8, 16)
ALPHA = 2.0 ** 0.25

C_MQ, C_MK, C_MV, C_MO, C_GATES, C_AQ, C_AK, C_AV = 0, 512, 1024, 1536, 2048, 2056, 2568, 3080
R_N1, R_N2, R_CB, R_CW, R_MN, R_AN, R_PS, R_QN, R_KN = 0, 8, 16, 24, 56, 57, 58, 62, 63
N_PARAMS = 64
N_SMALL = 17
N_CONSTS = 19

UNITS_1 = ["mq", "mk", "mo", "aq", "ak", "av", "mv", "out0", "out1"]
UNITS_2 = (["q2", "kv2", "pool2", "mix0", "mix1"] + [f"up{n}" for n in range(8)]
           + [f"down{n}" for n in range(8)] + ["ple", "gate0", "gate1"])
DMAS_OF = {"q2": 8, "mix0": 3, "mix1": 3}
SECOND = len(UNITS_1) + 3 * NE

ROOTS = ([("n1", t) for t in range(TT)] + [("aq", t) for t in range(TT)]
         + [("ak", t) for t in range(TT)]
         + [(k, t) for t in range(TT) for k in ("fd", "fm")] + [("n2", t) for t in range(TT)]
         + [("l1", t) for t in range(TT)] + [("l2", t) for t in range(TT)])

ITEMS = [(i, h, kind) for i in range(TT) for h in range(HEADS) for kind in "dm"]
FIN_STEP = 13
BANKS = {"d": (2, 3, 6, 7), "m": (4, 5, 1, 0)}


def build(nc, A, out):
    ctx = ExitStack()

    def sb(name, shape, dt=F32):
        return ctx.enter_context(nc.sbuf_tensor(name, shape, dt))

    def sem(name):
        return ctx.enter_context(nc.semaphore(name))

    with ctx:
        ring = sb("ring", [P, RING, UNIT])
        X = sb("X", [P, TT, D])
        HT = sb("HT", [P, DT, T])
        M = sb("M", [P, 17920])
        ident = sb("ident", [P, P])
        identb = sb("identb", [P, P], BF16)
        maskc = sb("maskc", [P, P], BF16)
        maskk = sb("maskk", [P, P], BF16)
        ones = sb("ones", [P, P])
        headsel = sb("headsel", [HEADS, HEADS, P])
        wrow = sb("wrow", [HEADS, T])
        prm = sb("prm", [P, N_PARAMS])
        wgates = sb("wgates", [P, DT, 8])
        msv = sb("msv", [P, len(ROOTS), 8])
        rsv = sb("rsv", [P, len(ROOTS), 8])
        half = sb("half", [P, 8])
        st = sb("st", [P, 96])
        cols = sb("cols", [P, 2, TT, HEADS])
        rg = sb("rg", [HEADS, 12])
        lamc = sb("lamc", [P, 4])
        wts = sb("wts", [P, 2, TT])
        dest = sb("dest", [P, 2, TT], I32)
        tokid = sb("tokid", [P, 2, TT, 2], I32)
        tab = sb("tab", [1, 2, NE], I32)
        idx = sb("idx", [BLK, 2, 2], I32)
        sink = sb("sink", [P, W2_HEADS])
        bn = sb("bn", [P, 2, 6])
        inv16 = sb("inv16", [P, 16])

        def m(a, *shape):
            v = M[:, a:a + int(np.prod(shape))]
            if len(shape) == 2:
                v = v.rearrange("p (a b) -> p a b", a=shape[0])
            if len(shape) == 3:
                v = v.rearrange("p (a b c) -> p a b c", a=shape[0], b=shape[1])
            return v

        MV, MO = m(0, TT, 512), m(2048, TT, 512)
        QA, KA, AV = m(4096, HEADS, T), m(6144, HEADS, T), m(8192, TT, 512)
        MIXA = m(10240, HEADS, T)
        JUNK3 = m(15872, 2, D)
        JUNK2 = m(0, 2, D)
        PROWS = m(12288, P)[0:N_PARAMS]
        EE = m(12288, 2, 512)
        AD, ATD = m(13312, 512), m(13824, 512)
        DD, AM, ATM = m(14336, 512), m(14848, 512), m(15360, 512)
        ND, SQD, NM, SQM = m(15872, 512), m(16384, 512), m(16896, 512), m(17408, 512)
        RI, RF, RT, RB, RR, RM, REM = (m(14336 + 512 * k, T)[0:HEADS] for k in range(7))
        GTOK = m(13312, TT, 8)
        LAMIN = m(13376, 4, QK)[0:1]
        LAMP = m(13632, 2 * QK)[0:1]
        unheld = m(17408, 2 * BLOCKS_HELD)[0:BLK].bitcast(I32).rearrange("p (n o) -> p n o", o=2)
        QKM = X[:, :, :].rearrange("p t d -> p (t d)").rearrange("p (c t) -> p c t", c=8)
        HN = m(4096, TT, D)
        WR = m(8192, DT, NG + NE)
        BR = m(8480, NG + NE)
        SQS = (SQD, SQM)
        UPPER, LG = m(8576, P), m(8704, TT, NG + NE)
        OHG, D4, EXPG = m(8848, TT, NG), m(8864, TT, NG), m(8880, TT, NG)
        E8, C8, H8, OH1, OH2 = (m(8896 + 32 * k, TT, EG) for k in range(5))
        T32, O1, O2 = (m(9056 + 128 * k, TT, NG, EG) for k in range(3))
        OHS = m(9440, TT, NE)
        NB, BEF = m(9568, NE), m(9600, NE)
        TH = m(9632, NE * (PER_EXPERT_MAX - 1))
        IOG, IO8 = m(9856, TT * NG), m(9872, TT * EG)
        IOG4, IO88 = m(9856, TT, NG), m(9872, TT, EG)
        RS = m(9904, 8, TT)
        P2, DM = m(9936, TT), m(9940, TT)
        RANK = m(9952, TT + 1, NE)
        XG, XT = m(0, D)[0:BLK], m(1024, DT, BLK)
        SG, HID, YB = m(1792, FT, BLK), m(2176, FT, BLK), m(2560, 2, 512)[0:BLK]
        YG = m(4096, 2, TT, D)
        BM = m(12288, W2_HEADS, 2 * P)
        DISTI = m(14336, 2 * P)
        Q2, K2, V2, U2, DP = m(0, PAIRS, T), m(2048, T), m(2560, TT, P), m(3072, 4, T), m(5120, 4, T)
        MIX2 = m(7168, DT, T)
        PW = m(11264, 2, T)
        SC2 = m(14336, 2, 2, 2 * P)
        PT2 = m(15360, 2, 512)
        AT = m(0, FFT, T)
        LNB1, LNG1 = m(0, D), m(16384, D)
        WP2 = m(16384, 4, P)
        LNG2, LNB2, BG = (HT[:, 2 * k:2 * k + 2, :].rearrange("p a b -> p (a b)") for k in range(3))
        PIN = HT[:, 6:8, :].rearrange("p a b -> p (a b)").rearrange("p (t c) -> p t c", t=TT)
        PET = m(16384, 2, T)
        H5T = m(0, DT, T)
        GT = m(4096, 2, 512)
        OUT2 = m(8192, TT, D)

        ps = ctx.enter_context(nc.psum_tensor("ps", [P, 8, 512], F32))
        h_rows = nc.dram_tensor("h_rows", [T, D], F32, kind="Internal").ap()
        slot_tokens = nc.dram_tensor("slot_tokens", [SLOTS, 2], I32, kind="Internal").ap()
        results = nc.dram_tensor("results", [NO_ROW, D], F32, kind="Internal").ap()

        full = [sem(f"bank_full{b}") for b in range(8)]
        empty = [sem(f"bank_empty{b}") for b in range(8)]
        slot_in = [sem(f"slot_in{s}") for s in range(RING)]
        unit_used = sem("unit_used")
        experts_done = sem("experts_done")
        x_in = [sem(f"x_in{t}") for t in range(TT)]
        small_in = sem("small_in")
        wgates_in = sem("wgates_in")
        sink_in = sem("sink_in")
        router_in = sem("router_in")
        consts = sem("consts")
        sumsq = sem("sumsq")
        ms_ready = sem("ms_ready")
        root_done = sem("root_done")
        xn_ready = sem("xn_ready")
        dve_step = sem("dve_step")
        silu_done = sem("silu_done")
        row_dve = sem("row_dve")
        row_act = sem("row_act")
        rows_done = sem("rows_done")
        lam_prod = sem("lam_prod")
        nmax_ready = sem("nmax_ready")
        ad_ready = sem("ad_ready")
        w_ready = sem("w_ready")
        fin_sq = sem("fin_sq")
        fin_in = sem("fin_in")
        fin_ready = sem("fin_ready")
        hn_ready = sem("hn_ready")
        h_out = sem("h_out")
        r_dve = sem("r_dve")
        r_act = sem("r_act")
        oh_ready = sem("oh_ready")
        tab_ready = sem("tab_ready")
        ids_out = sem("ids_out")
        table_in = sem("table_in")
        idx_kept = sem("idx_kept")
        waits_met = sem("waits_met")
        idx_in = sem("idx_in")
        rows_in = sem("rows_in")
        xt_full = sem("xt_full")
        xt_left = sem("xt_left")
        gu_full = sem("gu_full")
        g_left = sem("g_left")
        u_left = sem("u_left")
        y_full = sem("y_full")
        y_left = sem("y_left")
        y_out = sem("y_out")
        yg_in = [sem(f"yg_in{t}") for t in range(TT)]
        x3_ready = sem("x3_ready")
        consts2 = sem("consts2")
        dest_ready = sem("dest_ready")
        pool_step = sem("pool_step")
        wp_in = sem("wp_in")
        pool_ready = sem("pool_ready")
        nmax2 = sem("nmax2")
        exp2 = sem("exp2")
        pr2_ready = sem("pr2_ready")
        ln_in = sem("ln_in")
        ln_ready = sem("ln_ready")
        at_ready = sem("at_ready")
        late_in = sem("late_in")
        gate_act = sem("gate_act")
        out_ready = sem("out_ready")
        stored = sem("stored")

        turn, turns_of = {}, [0] * 8
        last_turn = {}

        def open_turn(pe, key, bank):
            turn[key] = (bank, turns_of[bank])
            if turns_of[bank]:
                pe.wait_ge(empty[bank], turns_of[bank])
            turns_of[bank] += 1
            return ps[:, bank, :]

        def fill_turn(ins, key):
            ins.then_inc(full[turn[key][0]], 1)

        def filled(eng, key):
            eng.wait_ge(full[turn[key][0]], turn[key][1] + 1)
            return ps[:, turn[key][0], :]

        def leave(ins, key):
            ins.then_inc(empty[turn[key][0]], 1)

        def left(eng, key):
            eng.wait_ge(empty[turn[key][0]], turn[key][1] + 1)

        place, slot_total = {}, [0] * RING
        for n, u in enumerate(UNITS_1):
            slot_total[n % RING] += 16 * DMAS_OF.get(u, 1)
            place[u] = (n % RING, slot_total[n % RING])
        expert_base = list(slot_total)
        slot_total = [c + 16 * NE // 2 for c in slot_total]
        for n, u in enumerate(UNITS_2):
            s = (SECOND + n) % RING
            slot_total[s] += 16 * DMAS_OF.get(u, 1)
            place[u] = (s, slot_total[s])

        def unit(pe, u):
            pe.wait_ge(slot_in[place[u][0]], place[u][1])
            return ring[:, place[u][0], :]

        def expert_slots(odd):
            return [(len(UNITS_1) + 3 * odd + k) % RING for k in range(3)]

        def root(name, t):
            return ROOTS.index((name, t))

        def until(eng, s, value):
            eng.wait_ge(s, value)
            eng.sem_inc(waits_met, 1)

        block = ctx.enter_context(nc.Block())

        @block.tensor
        def _(pe):
            def transposes(key, bank, src, n, width=P, idn=None):
                o = open_turn(pe, key, bank)
                idn = ident[:, :] if idn is None else idn
                for c in range(n):
                    ins = pe.transpose(o[:, c * width:(c + 1) * width], src[:, c * P:(c + 1) * P], idn)
                fill_turn(ins, key)

            pe.wait_ge(consts, N_CONSTS)
            pe.wait_ge(small_in, 16 * N_SMALL)
            transposes("prm", 7, PROWS, 1, N_PARAMS, ident[0:N_PARAMS, 0:N_PARAMS])
            for t in range(TT):
                pe.wait_ge(xn_ready, t + 1)
                for c in range(2):
                    transposes(("h", t, c), 2 + (2 * t + c) % 4, X[:, t, c * 512:(c + 1) * 512], 4)

            pe.wait_ge(wgates_in, 16)
            o = open_turn(pe, "gates", 6)
            for t in range(TT):
                left(pe, ("h", t, 0))
                left(pe, ("h", t, 1))
                for k in range(DT):
                    ins = pe.matmul(o[:, t * 8:t * 8 + 8], HT[:, k, t * P:(t + 1) * P],
                                    wgates[:, k, :], start=(k == 0), stop=(k == DT - 1))
            fill_turn(ins, "gates")
            pe.wait_ge(lam_prod, 1)
            o = open_turn(pe, "lam", 7)
            fill_turn(pe.matmul(o[:, 0:2], ones[0:1, :], LAMP[:, 0:2], start=True, stop=True), "lam")

            jobs = [0]

            def project(u, n, key, channel_major):
                w = unit(pe, u).rearrange("p (k c) -> p k c", k=DT)
                o = open_turn(pe, key, jobs[0] % 2)
                jobs[0] += 1
                for k in range(DT):
                    a, b = w[:, k, n * P:(n + 1) * P], HT[:, k, :]
                    if not channel_major:
                        a, b = HT[:, k, n * P:(n + 1) * P], w[:, k, :]
                    ins = pe.matmul(o, a, b, start=(k == 0), stop=(k == DT - 1))
                fill_turn(ins, key)
                last_turn[u] = key

            for n in range(4):
                project("mq", n, ("mq", n), True)
                if n == 0:
                    left(pe, "gates")
                    for g, bank in ((0, 4), (1, 5)):
                        o = open_turn(pe, ("grow", g), bank)
                        for t in range(TT):
                            ins = pe.transpose(o[0:HEADS, t * P:(t + 1) * P],
                                               GTOK[:, t, g * HEADS:(g + 1) * HEADS], ident[:, :])
                        fill_turn(ins, ("grow", g))
            for n in range(4):
                project("mk", n, ("mk", n), True)
            for n in range(4):
                project("mo", n, ("mo", n), False)
            pe.wait_ge(rows_done, 1)
            o = open_turn(pe, "gcols", 4)
            for g, src in ((0, RR), (1, REM)):
                for t in range(TT):
                    ins = pe.transpose(o[:, (g * TT + t) * HEADS:(g * TT + t + 1) * HEADS],
                                       src[:, t * P:(t + 1) * P], ident[0:HEADS, 0:HEADS])
            fill_turn(ins, "gcols")
            names = [(u, n) for u in ("aq", "ak", "av", "mv") for n in range(4)]
            for k, (u, n) in enumerate(names):
                project(u, n, (u, n), False)
                if 1 <= k <= 8:
                    left(pe, names[k - 1])
                    transposes(("T",) + names[k - 1], 6 + k % 2, (ND, NM)[(k - 1) % 2], HEADS)

            def scores(n):
                i, h, kind = ITEMS[n]
                W = (i + 1) * P
                b0, b1, _, _ = BANKS[kind]
                if kind == "d":
                    if h == 0:
                        left(pe, ("T", "aq", i))
                        left(pe, ("T", "ak", i))
                    for c, bank in ((0, b0), (1, b1)):
                        r = slice(c * QK, (c + 1) * QK)
                        o = open_turn(pe, ("S", n, c), bank)
                        pe.matmul(o[:, 0:W], QA[r, h, i * P:W], KA[r, h, 0:W], start=True, stop=False)
                        fill_turn(pe.matmul(o[:, i * P:W], identb[:, :], maskk[:, :],
                                            start=False, stop=True), ("S", n, c))
                else:
                    if h == 0 and i:
                        pe.wait_ge(w_ready, i)
                    o = open_turn(pe, ("S", n, 0), b0)
                    pe.matmul(o[:, 0:W], headsel[:, h, :], wrow[:, 0:W], start=True, stop=False)
                    fill_turn(pe.matmul(o[:, i * P:W], identb[:, :], maskc[:, :],
                                        start=False, stop=True), ("S", n, 0))
                    if n == 1:
                        pe.wait_ge(silu_done, 8)
                    o = open_turn(pe, ("S", n, 1), b1)
                    fill_turn(pe.matmul(o[:, 0:W], QKM[:, h, i * P:W], QKM[:, HEADS + h, 0:W],
                                        start=True, stop=True), ("S", n, 1))

            def turned(n):
                i, h, kind = ITEMS[n]
                if kind == "d":
                    pe.wait_ge(ad_ready, n // 2 + 1)
                else:
                    left(pe, ("S", n, 1))
                transposes(("AT", n), BANKS[kind][2], AD if kind == "d" else AM, i + 1)

            def outputs(n):
                i, h, kind = ITEMS[n]
                left(pe, ("AT", n))
                a, v = (ATD, AV) if kind == "d" else (ATM, MV)
                if n < 2:
                    for t in range(TT):
                        left(pe, ("av" if kind == "d" else "mv", t))
                if h == 0:
                    open_turn(pe, ("O", i, kind), BANKS[kind][3])
                o = ps[:, BANKS[kind][3], :]
                for j in range(i + 1):
                    ins = pe.matmul(o[:, h * P:(h + 1) * P], a[:, j * P:(j + 1) * P],
                                    v[:, j, h * P:(h + 1) * P], start=(j == 0), stop=(j == i))
                if h == HEADS - 1:
                    fill_turn(ins, ("O", i, kind))

            def final(i):
                left(pe, ("O", i, "d"))
                pe.wait_ge(fin_ready, i + 1)
                for kind in "dm":
                    transposes(("F", i, kind), BANKS[kind][2], ND if kind == "d" else NM, HEADS)

            for n in range(len(ITEMS) + 2):
                if n < len(ITEMS):
                    scores(n)
                if 1 <= n <= len(ITEMS):
                    turned(n - 1)
                if n >= 2:
                    outputs(n - 2)
                if n >= FIN_STEP and (n - FIN_STEP) % 8 == 0:
                    final((n - FIN_STEP) // 8)
            final(TT - 1)

            for i in range(TT):
                for kind in "dm":
                    left(pe, ("F", i, kind))
            for c in range(2):
                w = unit(pe, f"out{c}").rearrange("p (k c) -> p k c", k=DT)
                for t in range(TT):
                    key = ("o", c, t)
                    o = open_turn(pe, key, 2 + (c * TT + t) % 4)
                    for k in range(DT):
                        a = HT[:, k, t * P:(t + 1) * P] if k < HEADS else MIXA[:, k - HEADS, t * P:(t + 1) * P]
                        ins = pe.matmul(o, a, w[:, k, :], start=(k == 0), stop=(k == DT - 1))
                    fill_turn(ins, key)
                last_turn[f"out{c}"] = key

            for t in range(TT):
                pe.wait_ge(hn_ready, t + 1)
                for c in range(2):
                    transposes(("h2", t, c), 2 + (2 * t + c) % 4, HN[:, t, c * 512:(c + 1) * 512], 4)
            pe.wait_ge(router_in, 64)
            o = open_turn(pe, "route", 7)
            E = NG + NE
            for t in range(TT):
                left(pe, ("h2", t, 0))
                left(pe, ("h2", t, 1))
                for k in range(DT):
                    ins = pe.matmul(o[:, t * E:(t + 1) * E], HT[:, k, t * P:(t + 1) * P], WR[:, k, :],
                                    start=(k == 0), stop=(k == DT - 1))
            fill_turn(ins, "route")
            pe.wait_ge(oh_ready, 1)
            o = open_turn(pe, "rank", 6)
            for t in range(TT + 1):
                for j in range(min(t + 1, TT)):
                    ins = pe.matmul(o[:, t * NE:(t + 1) * NE], UPPER if j == t else ones[:, :],
                                    OHS[:, j, :], start=(j == 0), stop=(j == min(t, TT - 1)))
            fill_turn(ins, "rank")

            pe.wait_ge(tab_ready, 1)
            with pe.Fori(0, NE // 2) as ii:
                for odd in range(2):
                    sg, su, sd = expert_slots(odd)
                    wg, wu = (ring[:, s, :].rearrange("p (k c) -> p k c", k=DT) for s in (sg, su))
                    wd = ring[:, sd, :].rearrange("p (k c) -> p k c", k=FT)
                    blocks = pe.value_load(tab[0:1, 0, bass.ds(2 * ii + odd, 1)], min_val=1, max_val=PER_EXPERT_MAX)
                    before = pe.value_load(tab[0:1, 1, bass.ds(2 * ii + odd, 1)], min_val=0, max_val=BLOCKS_MAX)
                    for s in (sg, su, sd):
                        until(pe, slot_in[s], ii * 16 + (expert_base[s] + 16))
                    with pe.Fori(0, blocks) as j:
                        g = before + j
                        until(pe, rows_in, g * 16 + 16)
                        for k in range(DT):
                            kk = k % 4
                            ins = pe.transpose(ps[:, 6 + k // 4, kk * BLK:(kk + 1) * BLK], XG[:, k * P:(k + 1) * P],
                                               ident[0:BLK, 0:BLK])
                        ins.then_inc(xt_full, 1)
                        pe.wait_ge(xt_left, g + 1)
                        for f in range(FT):
                            for w, bank in ((wg, 2 * (f % 2)), (wu, 2 * (f % 2) + 1)):
                                if f >= 2:
                                    pe.wait_ge(g_left if w is wg else u_left, g * FT + (f - 1))
                                for k in range(DT):
                                    ins = pe.matmul(ps[:, bank, 0:BLK], w[:, k, f * P:(f + 1) * P],
                                                    XT[:, k, :], start=(k == 0), stop=(k == DT - 1))
                                ins.then_inc(gu_full, 1)
                        pe.wait_ge(u_left, g * FT + FT)
                        pe.wait_ge(y_left, g * 2 + 1)
                        for c in range(2):
                            for f in range(FT):
                                ins = pe.matmul(ps[0:BLK, 4 + c, :], HID[:, f, :],
                                                wd[:, f, c * 512:(c + 1) * 512],
                                                start=(f == 0), stop=(f == FT - 1))
                            ins.then_inc(y_full, 1)
                    pe.drain().then_inc(experts_done, 1)

            for t in range(TT):
                pe.wait_ge(x3_ready, t + 1)
                for c in range(2):
                    transposes(("x3", t, c), 2 + (2 * t + c) % 4, X[:, t, c * 512:(c + 1) * 512], 4)
            for t in range(TT):
                left(pe, ("x3", t, 0))
                left(pe, ("x3", t, 1))

            w = unit(pe, "q2").rearrange("p (k c) -> p k c", k=DT)
            for n in range(PAIRS):
                o = open_turn(pe, ("q2", n), n % 2)
                for k in range(DT):
                    ins = pe.matmul(o, w[:, k, n * P:(n + 1) * P], HT[:, k, :], start=(k == 0), stop=(k == DT - 1))
                fill_turn(ins, ("q2", n))
            last_turn["q2"] = ("q2", 3)
            w = unit(pe, "kv2")[:, 0:DT * 2 * P].rearrange("p (k c) -> p k c", k=DT)
            o = open_turn(pe, "k2", 0)
            for k in range(DT):
                ins = pe.matmul(o, w[:, k, 0:P], HT[:, k, :], start=(k == 0), stop=(k == DT - 1))
            fill_turn(ins, "k2")
            o = open_turn(pe, "v2", 1)
            for t in range(TT):
                for k in range(DT):
                    ins = pe.matmul(o[:, t * P:(t + 1) * P], HT[:, k, t * P:(t + 1) * P], w[:, k, P:2 * P],
                                    start=(k == 0), stop=(k == DT - 1))
            fill_turn(ins, "v2")
            last_turn["kv2"] = "v2"
            w = unit(pe, "pool2").rearrange("p (k c) -> p k c", k=DT)
            for n in range(4):
                o = open_turn(pe, ("u2", n), n % 2)
                for k in range(DT):
                    ins = pe.matmul(o, w[:, k, n * P:(n + 1) * P], HT[:, k, :], start=(k == 0), stop=(k == DT - 1))
                fill_turn(ins, ("u2", n))
            last_turn["pool2"] = ("u2", 3)

            def scores2(n):
                i, j = divmod(n, PAIRS)
                lo = P if i == 0 else 0
                for a in range(2):
                    r = slice(a * QK, (a + 1) * QK)
                    o = open_turn(pe, ("S2", n, a), 2 + 2 * (n % 2) + a)
                    fill_turn(pe.matmul(o[:, lo:2 * P], Q2[r, j, i * P:(i + 1) * P],
                                        K2[r, (i - 1) * P + lo:(i + 1) * P], start=True, stop=True),
                              ("S2", n, a))

            def turned2(n):
                i, j = divmod(n, PAIRS)
                pe.wait_ge(pr2_ready, 2 * n + 2)
                o = open_turn(pe, ("PT", n), 6)
                for a in range(2):
                    for b in range(1 if i == 0 else 0, 2):
                        ins = pe.transpose(o[:, (2 * a + b) * P:(2 * a + b + 1) * P],
                                           SC2[:, n % 2, a, b * P:(b + 1) * P], ident[:, :])
                fill_turn(ins, ("PT", n))

            def outputs2(n):
                i, j = divmod(n, PAIRS)
                left(pe, ("PT", n))
                if n == 0:
                    left(pe, "v2")
                if j == 0:
                    open_turn(pe, ("O2", i), 7)
                b0 = 1 if i == 0 else 0
                for a in range(2):
                    for b in range(b0, 2):
                        ins = pe.matmul(ps[a * QK:(a + 1) * QK, 7, j * P:(j + 1) * P],
                                        V2[:, i - 1 + b, a * QK:(a + 1) * QK],
                                        PT2[:, n % 2, (2 * a + b) * P:(2 * a + b + 1) * P],
                                        start=(b == b0), stop=(b == 1))
                if j == PAIRS - 1:
                    fill_turn(ins, ("O2", i))

            left(pe, ("q2", 3))
            left(pe, ("q2", 2))
            left(pe, "k2")
            for n in range(18):
                if n < 16:
                    scores2(n)
                if 1 <= n <= 16:
                    turned2(n - 1)
                if n >= 2:
                    outputs2(n - 2)
            pe.wait_ge(wp_in, 16)
            for g in range(4):
                pe.wait_ge(pool_ready, g + 1)
                o = open_turn(pe, ("pw", g), g % 2)
                fill_turn(pe.matmul(o, WP2[:, g, :], DP[:, g, :], start=True, stop=True), ("pw", g))
            for g in range(2, 4):
                left(pe, ("pw", g))
            left(pe, ("O2", 3))
            for c in range(2):
                w = unit(pe, f"mix{c}").rearrange("p (k c) -> p k c", k=DT)
                for t in range(TT):
                    key = ("o2", c, t)
                    o = open_turn(pe, key, 2 + (c * TT + t) % 4)
                    for k in range(DT):
                        ins = pe.matmul(o, MIX2[:, k, t * P:(t + 1) * P], w[:, k, :],
                                        start=(k == 0), stop=(k == DT - 1))
                    fill_turn(ins, key)
                last_turn[f"mix{c}"] = key

            for t in range(TT):
                pe.wait_ge(ln_ready, t + 1)
                for c in range(2):
                    transposes(("h1", t, c), 2 + (2 * t + c) % 4, X[:, t, c * 512:(c + 1) * 512], 4)
            for t in range(TT):
                left(pe, ("h1", t, 0))
                left(pe, ("h1", t, 1))
            for n in range(8):
                w = unit(pe, f"up{n}").rearrange("p (k c) -> p k c", k=DT)
                for f in range(4):
                    key = ("up", 4 * n + f)
                    o = open_turn(pe, key, (4 * n + f) % 4)
                    for k in range(DT):
                        ins = pe.matmul(o, w[:, k, f * P:(f + 1) * P], HT[:, k, :],
                                        start=(k == 0), stop=(k == DT - 1))
                    fill_turn(ins, key)
                last_turn[f"up{n}"] = key
            pe.wait_ge(late_in, 64)
            for t in range(TT):
                transposes(("pt", t), 4 + t % 4, PIN[:, t, :], 2)
            for t in range(TT):
                for c in range(2):
                    open_turn(pe, ("dn", t, c), 2 * t + c)
            pe.wait_ge(at_ready, FFT)
            for n in range(8):
                w = unit(pe, f"down{n}").rearrange("p (k c) -> p k c", k=4)

                def product(k, t, c):
                    return pe.matmul(ps[:, 2 * t + c, :], AT[:, 4 * n + k, t * P:(t + 1) * P],
                                     w[:, k, c * 512:(c + 1) * 512], start=(n == 0 and k == 0),
                                     stop=(n == 7 and k == 3))
                if n < 7:
                    for k in range(4):
                        for t in range(TT):
                            for c in range(2):
                                ins = product(k, t, c)
                    pe.drain().then_inc(unit_used, 1)
                else:
                    for t in range(TT):
                        for c in range(2):
                            for k in range(4):
                                ins = product(k, t, c)
                            fill_turn(ins, ("dn", t, c))
                    last_turn["down7"] = ("dn", TT - 1, 1)
            for t in range(TT):
                pe.wait_ge(ln_ready, TT + t + 1)
                for c in range(2):
                    transposes(("h5", t, c), 2 * t + c, X[:, t, c * 512:(c + 1) * 512], 4)
            for t in range(TT):
                left(pe, ("pt", t))
                left(pe, ("h5", t, 0))
                left(pe, ("h5", t, 1))
            wl = unit(pe, "ple")[:, 0:2 * D].rearrange("p (k c) -> p k c", k=2)
            for c in range(2):
                w = unit(pe, f"gate{c}").rearrange("p (k c) -> p k c", k=DT)
                for t in range(TT):
                    n = c * TT + t
                    o = open_turn(pe, ("gt", n), n % 4)
                    for k in range(DT):
                        ins = pe.matmul(o, H5T[:, k, t * P:(t + 1) * P], w[:, k, :],
                                        start=(k == 0), stop=(k == DT - 1))
                    fill_turn(ins, ("gt", n))
                    o = open_turn(pe, ("pl", n), 4 + n % 4)
                    for k in range(2):
                        ins = pe.matmul(o, PET[:, k, t * P:(t + 1) * P], wl[:, k, c * 512:(c + 1) * 512],
                                        start=(k == 0), stop=(k == 1))
                    fill_turn(ins, ("pl", n))

        @block.sync
        def _(sp):
            W1, W2, RT_ = A["w_in"][0], A["w_in_2"][0], None
            cols_of = {"mq": C_MQ, "mk": C_MK, "mo": C_MO, "aq": C_AQ, "ak": C_AK, "av": C_AV, "mv": C_MV}

            def load(u):
                s = place[u][0]
                dst = ring[:, s, :]
                k8 = dst.rearrange("p (k c) -> p k c", k=DT)

                def put(d, src):
                    sp.dma_start(d, src).then_inc(slot_in[s], 16)

                def columns(w, a, n):
                    return w[:, a:a + n].rearrange("(k p) c -> p k c", p=P)

                if u in cols_of:
                    put(k8, columns(W1, cols_of[u], 512))
                elif u.startswith("out"):
                    put(k8, columns(A["w_out"][0], 512 * int(u[3]), 512))
                elif u == "q2":
                    for h in range(W2_HEADS):
                        c = P * (h % PAIRS) + QK * (h // PAIRS)
                        put(k8[:, :, c:c + QK], columns(W2, 512 + QK * h, QK))
                elif u == "kv2":
                    put(dst[:, 0:DT * 2 * P].rearrange("p (k c) -> p k c", k=DT), columns(W2, 1024, 256))
                elif u == "pool2":
                    put(k8, columns(W2, 0, 512))
                elif u.startswith("mix"):
                    w = A["w_out_2"][0][:, 512 * int(u[3]):512 * int(u[3]) + 512]
                    put(k8[:, 0:4, :], w[0:512].rearrange("(k p) c -> p k c", p=P))
                    for a in range(2):
                        rows_ = w[512 + 256 * a:768 + 256 * a].rearrange("(j d) c -> d j c", d=QK)
                        put(k8[a * QK:(a + 1) * QK, 4:8, :], rows_)
                elif u.startswith("up"):
                    put(k8, columns(A["w_ff1_2"][0], 512 * int(u[2:]), 512))
                elif u.startswith("down"):
                    n = int(u[4:])
                    put(dst.rearrange("p (k c) -> p k c", k=4),
                        A["w_ff2_2"][0][512 * n:512 * n + 512].rearrange("(k p) c -> p k c", p=P))
                elif u == "ple":
                    put(dst[:, 0:2 * D].rearrange("p (k c) -> p k c", k=2),
                        A["w_ple_2"][0].rearrange("(k p) c -> p k c", p=P))
                else:
                    put(k8, columns(A["w_ple_gate_2"][0], 512 * int(u[4]), 512))

            def used_up(u):
                if u in last_turn:
                    filled(sp, last_turn[u])
                else:
                    sp.wait_ge(unit_used, int(u[4:]) + 1)

            def load_expert(e, odd):
                for s, w, k in zip(expert_slots(odd), ("w_gate", "w_up", "w_down"), (DT, DT, FT)):
                    src = A[w][0, bass.ds(e, 1)].rearrange("e (k p) c -> p (e k) c", p=P)
                    yield s, ring[:, s, :].rearrange("p (k c) -> p k c", k=k), src

            for n, u in enumerate(UNITS_1):
                if n >= RING:
                    used_up(UNITS_1[n - RING])
                load(u)
            for odd in range(2):
                for k, (s, dst, src) in enumerate(load_expert(odd, odd)):
                    used_up(UNITS_1[len(UNITS_1) - RING + 3 * odd + k])
                    sp.dma_start(dst, src).then_inc(slot_in[s], 16)
            with sp.Fori(1, NE // 2) as ii:
                for odd in range(2):
                    sp.wait_ge(experts_done, 2 * ii + (odd - 1))
                    for s, dst, src in load_expert(2 * ii + odd, odd):
                        sp.dma_start(dst, src).then_inc(slot_in[s], 16)
            for n, u in enumerate(UNITS_2):
                if n < RING:
                    sp.wait_ge(experts_done, NE - 1 + n // 3)
                else:
                    used_up(UNITS_2[n - RING])
                load(u)
            res = out[0].rearrange("(t p) c -> p t c", p=P)
            for n in range(2 * TT):
                c, t = divmod(n, TT)
                sp.wait_ge(out_ready, n + 1)
                sp.dma_start(res[:, t, c * 512:(c + 1) * 512], OUT2[:, t, c * 512:(c + 1) * 512]).then_inc(stored, 16)
            sp.wait_ge(stored, 16 * 2 * TT)

        @block.gpsimd
        def _(pool):
            made = [0]

            def const(ins, wait=False):
                ins.then_inc(consts, 1)
                made[0] += 1
                if wait:
                    pool.wait_ge(consts, made[0])

            def select(t, pattern, base, mult, op, fill, wait=False):
                const(pool.affine_select(out=t, in_=t, pattern=pattern, base=base, channel_multiplier=mult,
                                         compare_op=op, fill=fill), wait)

            const(pool.memset(ident[:, :], 0.0))
            const(pool.memset(identb[:, :], 0.0))
            const(pool.memset(maskc[:, :], 0.0))
            const(pool.memset(headsel[:, :, :], 0.0))
            const(pool.memset(maskk[:, :], 0.0))
            const(pool.memset(ones[:, :], 1.0))
            const(pool.memset(half[:, :], -0.5))
            const(pool.memset(unheld[:, :, :], NO_ROW))
            const(pool.memset(idx[:, 1, :], NO_ROW))
            const(pool.iota(inv16[:, :], [[1, 16]], base=1, channel_multiplier=0,
                            allow_small_or_imprecise_dtypes=True))
            for k in range(2):
                const(pool.iota(tokid[:, k, :, 0], [[P, TT]], base=0, channel_multiplier=1))
                const(pool.iota(tokid[:, k, :, 1], [[P, TT]], base=k * T, channel_multiplier=1), k == 1)
            select(ident[:, :], [[-1, P]], 0, 1, ALU.not_equal, 1.0)
            select(identb[:, :], [[-1, P]], 0, 1, ALU.not_equal, 1.0)
            select(maskc[:, :], [[-1, P]], 0, 1, ALU.is_ge, NEG)
            select(headsel[:, :, :], [[-1, HEADS], [0, P]], 0, 1, ALU.not_equal, 1.0)
            const(pool.memset(maskk[0:QK, QK:P], NEG))
            assert made[0] == N_CONSTS

            def roots(names, width):
                for nm in names:
                    r = root(*nm)
                    pool.wait_ge(ms_ready, r + 1)
                    pool.tensor_tensor(rsv[:, r, 0:width], msv[:, r, 0:width], half[:, 0:width],
                                       ALU.pow).then_inc(root_done, 1)

            roots([("n1", t) for t in range(TT)], 1)
            roots([(u, t) for u in ("aq", "ak") for t in range(TT)], 8)
            roots([(k, t) for t in range(TT) for k in ("fd", "fm")], HEADS)

            filled(pool, ("O", TT - 1, "m"))
            filled(pool, ("F", TT - 1, "d"))
            pool.memset(XG, 0.0).then_inc(consts2, 1)
            pool.memset(YB, 0.0).then_inc(y_left, 1)
            pool.memset(UPPER, 1.0).then_inc(consts2, 1)
            pool.iota(DISTI, [[-1, 2 * P]], base=P, channel_multiplier=1,
                      allow_small_or_imprecise_dtypes=True).then_inc(consts2, 1)
            pool.iota(IOG, [[0, TT], [1, NG]], base=0, channel_multiplier=0,
                      allow_small_or_imprecise_dtypes=True).then_inc(consts2, 1)
            pool.iota(IO8, [[0, TT], [1, EG]], base=0, channel_multiplier=0,
                      allow_small_or_imprecise_dtypes=True).then_inc(consts2, 1)
            pool.iota(TH, [[0, NE], [BLK, PER_EXPERT_MAX - 1]], base=BLK, channel_multiplier=0,
                      allow_small_or_imprecise_dtypes=True).then_inc(consts2, 1)
            pool.wait_ge(consts2, 6)
            pool.affine_select(out=UPPER, in_=UPPER, pattern=[[1, P]], base=0, channel_multiplier=-1,
                               compare_op=ALU.is_gt, fill=0.0).then_inc(consts2, 1)
            roots([("n2", t) for t in range(TT)], 1)
            for h in range(W2_HEADS):
                pool.tensor_scalar(BM[:, h, :], DISTI, -(2.0 ** -(h + 1)), None, ALU.mult).then_inc(consts2, 1)
            pool.wait_ge(consts2, 7 + W2_HEADS)
            pool.affine_select(out=BM, in_=BM, pattern=[[0, W2_HEADS], [-1, 2 * P]], base=P, channel_multiplier=1,
                               compare_op=ALU.is_ge, fill=NEG).then_inc(consts2, 1)
            pool.wait_ge(consts2, 8 + W2_HEADS)
            pool.affine_select(out=BM, in_=BM, pattern=[[0, W2_HEADS], [1, 2 * P]], base=-1, channel_multiplier=-1,
                               compare_op=ALU.is_ge, fill=NEG).then_inc(consts2, 1)

            pool.wait_ge(table_in, 16)
            pool.wait_ge(dest_ready, 1)
            for k in range(2):
                for t in range(TT):
                    pool.indirect_dma_start(
                        out=slot_tokens, out_offset=bass.IndirectOffsetOnAxis(dest[:, k, t:t + 1], 0),
                        in_=tokid[:, k, t, :], in_offset=None).then_inc(ids_out, 16)
            pool.wait_ge(ids_out, 16 * 2 * TT)
            pool.wait_ge(h_out, 16 * TT)
            pool.wait_ge(tab_ready, 1)

            def scatter_results():
                pool.indirect_dma_start(
                    out=results, out_offset=bass.IndirectOffsetOnAxis(idx[:, 1, 1:2], 0),
                    in_=YB.rearrange("p c n -> p (c n)"), in_offset=None,
                    bounds_check=NO_ROW - 1, oob_is_err=False).then_inc(y_out, 16)

            with pool.Fori(0, NE) as e:
                blocks = pool.value_load(tab[0:1, 0, bass.ds(e, 1)], min_val=1, max_val=PER_EXPERT_MAX)
                before = pool.value_load(tab[0:1, 1, bass.ds(e, 1)], min_val=0, max_val=BLOCKS_MAX)
                with pool.Fori(0, blocks) as j:
                    g = before + j
                    pool.dma_start(idx[:, 0, :], slot_tokens[bass.ds(g * BLK, BLK), :]).then_inc(idx_in, 16)
                    until(pool, idx_in, g * 16 + 16)
                    pool.indirect_dma_start(
                        out=XG, out_offset=None, in_=h_rows,
                        in_offset=bass.IndirectOffsetOnAxis(idx[:, 0, 0:1], 0),
                        bounds_check=T - 1, oob_is_err=False).then_inc(rows_in, 16)
                    until(pool, xt_full, g + 1)
                    until(pool, y_left, g * 2 + 1)
                    scatter_results()
                    until(pool, y_out, g * 16 + 16)
                    pool.tensor_copy(idx[:, 1, :], idx[:, 0, :]).then_inc(idx_kept, 1)
                    until(pool, idx_kept, g + 1)
            last = pool.value_load(tab[0:1, 0, NE - 1:NE], min_val=1, max_val=PER_EXPERT_MAX)
            before = pool.value_load(tab[0:1, 1, NE - 1:NE], min_val=0, max_val=BLOCKS_MAX)
            until(pool, y_left, (before + last) * 2 + 1)
            scatter_results()

            done = [0]

            def step(ins, wait=True):
                ins.then_inc(pool_step, 1)
                done[0] += 1
                if wait:
                    pool.wait_ge(pool_step, done[0])

            for g, w in enumerate(POOL_WINDOWS):
                left(pool, ("u2", g))
                src, k, sh = U2[:, g, :], 0, 1
                while sh < w:
                    dst = PW[:, k, :]
                    step(pool.tensor_copy(dst[:, 0:sh], src[:, 0:sh]), False)
                    step(pool.tensor_tensor(dst[:, sh:T], src[:, sh:T], src[:, 0:T - sh], ALU.add))
                    src, k, sh = dst, 1 - k, 2 * sh
                dst = PW[:, k, :]
                step(pool.tensor_tensor(dst[:, 0:w], src[:, 0:w], inv16[:, 0:w], ALU.mult), False)
                step(pool.tensor_scalar(dst[:, w:T], src[:, w:T], 1.0 / w, None, ALU.mult))
                pool.tensor_tensor(DP[:, g, :], dst, U2[:, g, :], ALU.subtract).then_inc(pool_ready, 1)
                pool.wait_ge(pool_ready, g + 1)
            roots([("l1", t) for t in range(TT)] + [("l2", t) for t in range(TT)], 1)

        @block.scalar
        def _(act):
            xt = A["x"][0].rearrange("(t p) c -> p t c", p=P)

            def small(dst, src, s=small_in):
                act.dma_start(dst, src).then_inc(s, 16)

            def row(name, q):
                return A[name][0].rearrange("(q c) -> q c", q=q)

            for t in range(TT):
                act.dma_start(X[:, t, :], xt[:, t, :]).then_inc(x_in[t], 16)
            small(PROWS[R_N1:R_N1 + 8], row("norm1_w", 8))
            small(PROWS[R_N2:R_N2 + 8], row("norm2_w", 8))
            small(PROWS[R_CB:R_CB + 8], row("conv_b", 8))
            small(PROWS[R_CW:R_CW + 32], A["conv_w"][0].rearrange("w (c p) -> (w c) p", p=P))
            small(PROWS[R_MN:R_MN + 1], A["m_norm_w"])
            small(PROWS[R_AN:R_AN + 1], A["a_norm_w"])
            small(PROWS[R_PS:R_PS + 4], row("pool_scale_2", 4))
            for c in range(2):
                small(PROWS[R_QN:R_QN + 1, c * QK:(c + 1) * QK], A["q_norm_w"])
                small(PROWS[R_KN:R_KN + 1, c * QK:(c + 1) * QK], A["k_norm_w"])
            small(wgates[:, :, :], A["w_in"][0][:, C_GATES:C_GATES + 8].rearrange("(k p) c -> p k c", p=P), wgates_in)
            for k, nm in enumerate(("lambda_q1", "lambda_k1", "lambda_q2", "lambda_k2")):
                small(LAMIN[:, k, :], A[nm])
            small(rg[:, 0:1], A["b_igate"].rearrange("o h -> h o"))
            small(rg[:, 1:2], A["b_fgate"].rearrange("o h -> h o"))
            act.dma_start(sink[:, :], A["attn_sinks_2"].to_broadcast([P, W2_HEADS])).then_inc(sink_in, 16)
            act.wait_ge(consts, N_CONSTS)
            act.dma_start(slot_tokens.rearrange("(p n) o -> p (n o)", p=BLK),
                          unheld[:, :, :].rearrange("p n o -> p (n o)")).then_inc(table_in, 16)

            for t in range(TT):
                act.wait_ge(x_in[t], 16)
                if t >= 2:
                    act.wait_ge(sumsq, t - 1)
                act.activation(JUNK2[:, t % 2, :], X[:, t, :], ACT.Square, accum_out=st[:, t:t + 1]).then_inc(sumsq, 1)
            filled(act, "lam")
            leave(act.activation(lamc[:, 0:2], ps[:, 7, 0:2], ACT.Exp), "lam")

            def silu(c):
                left(act, ("mq", c) if c < 4 else ("mk", c - 4))
                act.activation(QKM[:, c, :], EE[:, c % 2, :], ACT.Silu).then_inc(silu_done, 1)

            silu(0)
            silu(1)
            act.wait_ge(row_dve, 1)
            act.activation(RT, RT, ACT.Exp).then_inc(row_act, 1)
            act.wait_ge(row_act, 1)
            act.activation(RT, RT, ACT.Ln, bias=1.0).then_inc(row_act, 1)
            silu(2)
            act.wait_ge(row_dve, 2)
            act.wait_ge(table_in, 16)
            act.activation(REM, RM, ACT.Exp, scale=-1.0).then_inc(row_act, 1)
            for c in range(3, 8):
                silu(c)
            for t in range(TT):
                leave(act.activation(MO[:, t, :], filled(act, ("mo", t)), ACT.Sigmoid), ("mo", t))
            names = [(u, n) for u in ("aq", "ak", "av", "mv") for n in range(4)]
            filled(act, "gcols")
            for k, nm in enumerate(names):
                p = filled(act, nm)
                if k < 8:
                    if k >= 2:
                        act.wait_ge(ms_ready, root(*names[k - 2]) + 1)
                    act.activation(SQS[k % 2], p, ACT.Square).then_inc(sumsq, 1)
                else:
                    leave(act.activation((AV if nm[0] == "av" else MV)[:, nm[1], :], p, ACT.Copy), nm)
                if 1 <= k <= 8:
                    u, n = names[k - 1]
                    key = ("T", u, n)
                    q = filled(act, key).rearrange("p (h t) -> p h t", h=HEADS)
                    dst, gain = (QA, R_QN) if u == "aq" else (KA, R_KN)
                    leave(act.activation(dst[:, :, n * P:(n + 1) * P], q, ACT.Copy, scale=prm[:, gain:gain + 1]), key)

            def exps(n):
                i, h, kind = ITEMS[n]
                k, W = n // 2, (i + 1) * P
                if kind == "d":
                    act.wait_ge(nmax_ready, k + 1)
                    if k:
                        act.wait_ge(ad_ready, k)
                    for c in range(2):
                        leave(act.activation(EE[:, c, 0:W], filled(act, ("S", n, c))[:, 0:W], ACT.Exp,
                                       bias=st[:, 18 + 8 * (k % 2) + c:19 + 8 * (k % 2) + c], scale=QK ** -0.5,
                                       accum_out=st[:, 20 + 8 * (k % 2) + c:21 + 8 * (k % 2) + c]), ("S", n, c))
                else:
                    p = filled(act, ("S", n, 0))
                    if k:
                        left(act, ("S", n - 2, 1))
                    if k == 0:
                        left(act, "gcols")
                    leave(act.activation(DD[:, 0:W], p[:, 0:W], ACT.Exp, bias=cols[:, 0, i, h:h + 1]), ("S", n, 0))

            def finals(i):
                act.activation(SQD, filled(act, ("O", i, "d")), ACT.Square).then_inc(fin_sq, 1)
                act.wait_ge(fin_in, i + 1)
                act.activation(SQM, NM, ACT.Square).then_inc(fin_sq, 1)

            def final_out(i):
                for kind, dst, gain in (("d", MIXA, R_AN), ("m", HT, R_MN)):
                    key = ("F", i, kind)
                    q = filled(act, key).rearrange("p (h t) -> p h t", h=HEADS)
                    leave(act.activation(dst[:, 0:HEADS, i * P:(i + 1) * P], q, ACT.Copy, scale=prm[:, gain:gain + 1]), key)

            for n in range(len(ITEMS) + 1):
                if n < len(ITEMS):
                    exps(n)
                if n >= 1 and ITEMS[n - 1][2] == "d":
                    key, W = ("AT", n - 1), (ITEMS[n - 1][0] + 1) * P
                    leave(act.activation(ATD[:, 0:W], filled(act, key)[:, 0:W], ACT.Copy), key)
                if n >= 9 and (n - 9) % 8 == 0:
                    finals((n - 9) // 8)
                if n >= FIN_STEP and (n - FIN_STEP) % 8 == 0:
                    final_out((n - FIN_STEP) // 8)
            finals(TT - 1)
            for t in range(TT):
                act.dma_start(X[:, t, :], xt[:, t, :]).then_inc(x_in[t], 16)
            final_out(TT - 1)
            small(WR[:, :, 0:NG], A["w_group"][0].rearrange("(k p) c -> p k c", p=P), router_in)
            small(WR[:, :, NG:NG + NE], A["w_expert"][0].rearrange("(k p) c -> p k c", p=P), router_in)
            small(BR[:, 0:NG], A["b_group"].to_broadcast([P, NG]), router_in)
            small(BR[:, NG:NG + NE], A["b_expert"].to_broadcast([P, NE]), router_in)
            for t in range(TT):
                left(act, ("o", 0, t))
                left(act, ("o", 1, t))
                if t >= 2:
                    act.wait_ge(sumsq, TT + 8 + t - 1)
                act.activation(JUNK3[:, t % 2, :], X[:, t, :], ACT.Square, accum_out=st[:, 4 + t:5 + t]).then_inc(sumsq, 1)
            for t in range(TT):
                act.wait_ge(hn_ready, t + 1)
                act.dma_start(h_rows[t * P:(t + 1) * P, :], HN[:, t, :]).then_inc(h_out, 16)
            act.wait_ge(r_dve, 1)
            act.activation(EXPG, D4, ACT.Exp).then_inc(r_act, 1)
            act.wait_ge(r_dve, 2)
            act.activation(P2, DM, ACT.Exp).then_inc(r_act, 1)

            act.wait_ge(tab_ready, 1)
            with act.Fori(0, NE) as e:
                blocks = act.value_load(tab[0:1, 0, bass.ds(e, 1)], min_val=1, max_val=PER_EXPERT_MAX)
                before = act.value_load(tab[0:1, 1, bass.ds(e, 1)], min_val=0, max_val=BLOCKS_MAX)
                with act.Fori(0, blocks) as j:
                    g = before + j
                    for f in range(FT):
                        act.wait_ge(gu_full, g * 2 * FT + (2 * f + 1))
                        act.activation(SG[:, f, :], ps[:, 2 * (f % 2), 0:BLK], ACT.Silu).then_inc(g_left, 1)
                    act.wait_ge(y_out, g * 16 + 16)
                    for c in range(2):
                        act.wait_ge(y_full, g * 2 + (c + 1))
                        act.activation(YB[:, c, :], ps[0:BLK, 4 + c, :], ACT.Copy).then_inc(y_left, 1)

            last = act.value_load(tab[0:1, 0, NE - 1:NE], min_val=1, max_val=PER_EXPERT_MAX)
            before = act.value_load(tab[0:1, 1, NE - 1:NE], min_val=0, max_val=BLOCKS_MAX)
            act.wait_ge(y_out, (before + last) * 16 + 16)
            for t in range(TT):
                for k in range(2):
                    act.dma_start(YG[:, k, t, :], results[k * T + t * P:k * T + (t + 1) * P, :]).then_inc(yg_in[t], 16)

            for t in range(TT):
                leave(act.activation(HT[:, 0:4, t * P:(t + 1) * P],
                                     filled(act, ("x3", t, 0)).rearrange("p (k t) -> p k t", k=4), ACT.Copy), ("x3", t, 0))
            act.dma_start(WP2, A["w_pool_2"][0].rearrange("g c d -> c g d")).then_inc(wp_in, 16)
            for n in range(PAIRS):
                leave(act.activation(Q2[:, n, :], filled(act, ("q2", n)), ACT.Copy), ("q2", n))
            leave(act.activation(K2, filled(act, "k2"), ACT.Copy), "k2")
            leave(act.activation(V2, filled(act, "v2").rearrange("p (t d) -> p t d", t=TT), ACT.Copy), "v2")
            for n in range(4):
                leave(act.activation(U2[:, n, :], filled(act, ("u2", n)), ACT.Copy), ("u2", n))

            def pt_out(n):
                lo = 1 if n < PAIRS else 0
                dst, src = (v.rearrange("p (a b q) -> p a b q", a=2, b=2)[:, :, lo:2, :]
                            for v in (PT2[:, n % 2, :], filled(act, ("PT", n))))
                leave(act.activation(dst, src, ACT.Copy), ("PT", n))

            for n in range(18):
                if n < 16:
                    lo = P if n < PAIRS else 0
                    b = 32 + 8 * (n % 2)
                    act.wait_ge(nmax2, n + 1)
                    for a in range(2):
                        act.activation(SC2[:, n % 2, a, lo:], SC2[:, n % 2, a, lo:], ACT.Exp,
                                       bias=st[:, b + 2 + a:b + 3 + a], accum_out=st[:, b + 4 + a:b + 5 + a]).then_inc(exp2, 1)
                    act.activation(st[:, b + 6:b + 8], st[:, b + 6:b + 8], ACT.Exp).then_inc(exp2, 1)
                if 1 <= n <= 16:
                    pt_out(n - 1)
                if n >= 5 and (n - 5) % 4 == 0:
                    i = (n - 5) // 4
                    leave(act.activation(MIX2[:, 4:8, i * P:(i + 1) * P],
                                         filled(act, ("O2", i)).rearrange("p (j q) -> p j q", j=PAIRS), ACT.Copy), ("O2", i))
            act.dma_start(LNB1, A["ln1_b_2"].to_broadcast([P, D])).then_inc(ln_in, 16)
            for g in range(4):
                leave(act.activation(MIX2[:, g, :], filled(act, ("pw", g)), ACT.Copy, scale=prm[:, R_PS + g:R_PS + g + 1]), ("pw", g))
            act.dma_start(LNG1, A["ln1_g_2"].to_broadcast([P, D])).then_inc(ln_in, 16)
            for t in range(TT):
                for c in range(2):
                    key = ("h1", t, c)
                    leave(act.activation(HT[:, 4 * c:4 * c + 4, t * P:(t + 1) * P],
                                         filled(act, key).rearrange("p (k t) -> p k t", k=4), ACT.Copy), key)
            for f in range(FFT):
                leave(act.activation(AT[:, f, :], filled(act, ("up", f)), ACT.Relu), ("up", f))
            for dst, nm in ((LNG2, "ln2_g_2"), (LNB2, "ln2_b_2"), (BG, "b_ple_gate_2")):
                act.dma_start(dst, A[nm].to_broadcast([P, D])).then_inc(late_in, 16)
            act.dma_start(PIN, A["p_2"][0, 0].rearrange("(t p) c -> p t c", p=P)).then_inc(late_in, 16)
            for t in range(TT):
                leave(act.activation(PET[:, :, t * P:(t + 1) * P],
                                     filled(act, ("pt", t))[:, 0:2 * P].rearrange("p (k t) -> p k t", k=2), ACT.Copy), ("pt", t))
            for t in range(TT):
                for c in range(2):
                    key = ("h5", t, c)
                    leave(act.activation(H5T[:, 4 * c:4 * c + 4, t * P:(t + 1) * P],
                                         filled(act, key).rearrange("p (k t) -> p k t", k=4), ACT.Copy), key)
            for n in range(2 * TT):
                left(act, ("gt", n))
                act.activation(GT[:, n % 2, :], GT[:, n % 2, :], ACT.Sigmoid).then_inc(gate_act, 1)

        @block.vector
        def _(vec):
            steps = [0]

            def step(ins):
                ins.then_inc(dve_step, 1)
                steps[0] += 1
                vec.wait_ge(dve_step, steps[0])

            def mean_square(r, src, n, width=1, eps=EPS):
                vec.tensor_scalar(msv[:, r, 0:width], src, 1.0 / n, eps, ALU.mult, ALU.add).then_inc(ms_ready, 1)

            def rooted(r):
                vec.wait_ge(root_done, r + 1)
                return rsv[:, r, :]

            vec.wait_ge(consts, N_CONSTS)
            step(vec.reciprocal(inv16[:, :], inv16[:, :]))

            def ms1(t):
                vec.wait_ge(sumsq, t + 1)
                mean_square(t, st[:, t:t + 1], D)

            ms1(0)
            for t in range(TT):
                if t + 1 < TT:
                    ms1(t + 1)
                vec.tensor_scalar(X[:, t, :], X[:, t, :], rooted(t)[:, 0:1], None, ALU.mult).then_inc(xn_ready, 1)
            vec.wait_ge(small_in, 16 * N_SMALL)
            leave(vec.tensor_copy(prm[:, :], filled(vec, "prm")[:, 0:N_PARAMS]), "prm")
            left(vec, "prm")
            step(vec.tensor_scalar(prm[:, R_AN:R_AN + 1], prm[:, R_AN:R_AN + 1], 1.0 - LAMBDA_INIT, None, ALU.mult))

            def gained(key, t, c, first):
                w = prm[:, first + 4 * c:first + 4 * c + 4].unsqueeze(2).to_broadcast([P, 4, P])
                leave(vec.tensor_tensor(HT[:, 4 * c:4 * c + 4, t * P:(t + 1) * P],
                                        filled(vec, key).rearrange("p (k t) -> p k t", k=4), w, ALU.mult), key)

            for t in range(TT):
                for c in range(2):
                    gained(("h", t, c), t, c, R_N1)
            for k in range(2):
                step(vec.tensor_tensor_reduce(LAMP[:, 2:2 + QK], LAMIN[:, 2 * k, :], LAMIN[:, 2 * k + 1, :], 1.0, 0.0,
                                              ALU.mult, ALU.add, LAMP[:, k:k + 1]))
            vec.tensor_copy(LAMP[:, 66:67], LAMP[:, 0:1]).then_inc(lam_prod, 1)
            leave(vec.tensor_copy(GTOK, filled(vec, "gates")[:, 0:TT * 8].rearrange("p (t g) -> p t g", t=TT)), "gates")
            left(vec, "lam")
            step(vec.tensor_tensor(lamc[:, 3:4], lamc[:, 1:2], lamc[:, 0:1], ALU.subtract))
            step(vec.tensor_scalar(lamc[:, 2:3], lamc[:, 3:4], -LAMBDA_INIT, None, ALU.add))

            def conv(c):
                key = ("mq", c) if c < 4 else ("mk", c - 4)
                p, e = filled(vec, key), EE[:, c % 2, :]
                if c >= 2:
                    vec.wait_ge(silu_done, c - 1)
                w = [prm[:, R_CW + 8 * j + c:R_CW + 8 * j + c + 1] for j in range(4)]
                step(vec.tensor_scalar(e, p, w[3], prm[:, R_CB + c:R_CB + c + 1], ALU.mult, ALU.add))
                for s in (1, 2, 3):
                    ins = vec.scalar_tensor_tensor(out=e[:, s:T], in0=p[:, 0:T - s], scalar=w[3 - s], in1=e[:, s:T],
                                                   op0=ALU.mult, op1=ALU.add)
                    step(ins) if s < 3 else leave(ins, key)

            conv(0)
            conv(1)
            leave(vec.tensor_scalar(RI, filled(vec, ("grow", 0))[0:HEADS], rg[:, 0:1], None, ALU.add), ("grow", 0))
            leave(vec.tensor_scalar(RF, filled(vec, ("grow", 1))[0:HEADS], rg[:, 1:2], None, ALU.add), ("grow", 1))
            left(vec, ("grow", 1))
            vec.scalar_tensor_tensor(out=RT, in0=RF, scalar=-1.0, in1=RF, op0=ALU.mult, op1=ALU.min).then_inc(row_dve, 1)
            conv(2)
            vec.wait_ge(row_act, 2)
            step(vec.scalar_tensor_tensor(out=RF, in0=RF, scalar=0.0, in1=RT, op0=ALU.min, op1=ALU.subtract))
            for j in range(TT):
                s = slice(j * P, (j + 1) * P)
                step(vec.tensor_tensor_scan(RB[:, s], ones[0:HEADS, :], RF[:, s], 0.0, ALU.mult, ALU.add))
            step(vec.tensor_copy(rg[:, 8:8 + TT], RB[:, P - 1:T:P]))
            step(vec.tensor_tensor(wrow[:, :], RI, RB, ALU.subtract))
            step(vec.memset(rg[:, 2:6], 0.0))
            for i in range(TT):
                s = slice(i * P, (i + 1) * P)
                if i:
                    e = rg[:, 7 + i:8 + i]
                    step(vec.tensor_reduce(rg[:, 4:5], wrow[:, (i - 1) * P:i * P], AX, ALU.max))
                    if i > 1:
                        step(vec.tensor_tensor(rg[:, 4:5], rg[:, 4:5], rg[:, 3:4], ALU.max))
                    step(vec.tensor_tensor(rg[:, 3:4], rg[:, 4:5], e, ALU.add))
                    step(vec.tensor_tensor(rg[:, 2:3], rg[:, 2:3], e, ALU.add))
                    step(vec.tensor_tensor(rg[:, 5:6], rg[:, 2:3], rg[:, 3:4], ALU.max))
                step(vec.tensor_tensor_scan(RR[:, s], wrow[:, s], wrow[:, s], rg[:, 5:6], ALU.max, ALU.max))
            vec.tensor_tensor(RM, RB, RR, ALU.add).then_inc(row_dve, 1)
            conv(3)
            vec.wait_ge(row_act, 3)
            vec.wait_ge(row_dve, 2)
            vec.tensor_scalar(RR, RR, -1.0, None, ALU.mult).then_inc(rows_done, 1)
            for c in range(4, 8):
                conv(c)
            leave(vec.tensor_copy(cols[:, :, :, :].rearrange("p a t h -> p (a t h)"), filled(vec, "gcols")[:, 0:2 * TT * HEADS]), "gcols")

            names = [(u, n) for u in ("aq", "ak") for n in range(4)]
            for k, nm in enumerate(names):
                vec.wait_ge(sumsq, TT + k + 1)
                p = filled(vec, nm).rearrange("p (g d) -> p g d", g=8)
                step(vec.tensor_reduce(st[:, 8:16], SQS[k % 2].rearrange("p (g d) -> p g d", g=8), AX, ALU.add))
                mean_square(root(*nm), st[:, 8:16], QK, 8)
                if k >= 2:
                    filled(vec, ("T",) + names[k - 2])
                r = rooted(root(*nm)).unsqueeze(2).to_broadcast([P, 8, QK])
                dst = (ND, NM)[k % 2].rearrange("p (g d) -> p g d", g=8)
                leave(vec.tensor_tensor(dst, p, r, ALU.mult), nm)

            def maximum(n):
                i, h, _ = ITEMS[n]
                k, W = n // 2, (i + 1) * P
                b = 16 + 8 * (k % 2)
                if h == 0 and i:
                    filled(vec, ("S", n - 1, 0))
                    vec.tensor_scalar(wrow[:, 0:i * P], wrow[:, 0:i * P], rg[:, 7 + i:8 + i], None, ALU.add).then_inc(w_ready, 1)
                filled(vec, ("S", n, 0))
                filled(vec, ("S", n, 1))
                step(vec.tensor_reduce(st[:, b:b + 2], ps[:, 2:4, 0:W], AX, ALU.max))
                vec.tensor_scalar(st[:, b + 2:b + 4], st[:, b:b + 2], -QK ** -0.5, None, ALU.mult).then_inc(nmax_ready, 1)

            def decayed(n):
                i, h, _ = ITEMS[n]
                W = (i + 1) * P
                left(vec, ("S", n, 0))
                if n >= 2:
                    filled(vec, ("AT", n - 2))
                d = 64 + 4 * (i % 2) + h
                leave(vec.tensor_tensor_reduce(AM[:, 0:W], filled(vec, ("S", n, 1))[:, 0:W], DD[:, 0:W], HD ** -0.5, 0.0,
                                               ALU.mult, ALU.add, st[:, d:d + 1]), ("S", n, 1))

            def mixed(n):
                i, h, _ = ITEMS[n]
                k, W = n // 2, (i + 1) * P
                b = 16 + 8 * (k % 2)
                for c in range(2):
                    left(vec, ("S", n, c))
                step(vec.reciprocal(st[:, b + 6:b + 8], st[:, b + 4:b + 6]))
                vec.tensor_scalar(EE[:, 0, 0:W], EE[:, 0, 0:W], st[:, b + 6:b + 7], None, ALU.mult).then_inc(dve_step, 1)
                steps[0] += 1
                step(vec.tensor_tensor(st[:, 81:82], st[:, b + 7:b + 8], lamc[:, 2:3], ALU.mult))
                if n >= 2:
                    filled(vec, ("AT", n - 2))
                vec.scalar_tensor_tensor(out=AD[:, 0:W], in0=EE[:, 1, 0:W], scalar=st[:, 81:82], in1=EE[:, 0, 0:W],
                                         op0=ALU.mult, op1=ALU.add).then_inc(ad_ready, 1)

            def at_out(n):
                key, W = ("AT", n), (ITEMS[n][0] + 1) * P
                leave(vec.tensor_copy(ATM[:, 0:W], filled(vec, key)[:, 0:W]), key)

            def heads_of(v):
                return v.rearrange("p (h d) -> p h d", h=HEADS)

            def final(i):
                d = 64 + 4 * (i % 2)
                step(vec.scalar_tensor_tensor(out=st[:, 72:76], in0=st[:, d:d + 4], scalar=-1.0, in1=st[:, d:d + 4],
                                              op0=ALU.mult, op1=ALU.max))
                step(vec.tensor_tensor(st[:, 72:76], st[:, 72:76], cols[:, 1, i, :], ALU.max))
                step(vec.reciprocal(st[:, 76:80], st[:, 72:76]))
                r = st[:, 76:80].unsqueeze(2).to_broadcast([P, HEADS, HD])
                p = filled(vec, ("O", i, "m"))
                if i:
                    filled(vec, ("F", i - 1, "m"))
                leave(vec.tensor_tensor(heads_of(NM), heads_of(p), r, ALU.mult), ("O", i, "m"))
                left(vec, ("O", i, "m"))
                left(vec, ("mo", i))
                vec.tensor_tensor(NM, NM, MO[:, i, :], ALU.mult).then_inc(fin_in, 1)
                for k, (kind, sq, dst) in enumerate((("d", SQD, ND), ("m", SQM, NM))):
                    r = root("f" + kind, i)
                    vec.wait_ge(fin_sq, 2 * i + k + 1)
                    step(vec.tensor_reduce(st[:, 84:88], heads_of(sq), AX, ALU.add))
                    mean_square(r, st[:, 84:88], HD, HEADS)
                    v = rooted(r)[:, 0:HEADS].unsqueeze(2).to_broadcast([P, HEADS, HD])
                    if kind == "d":
                        if i:
                            filled(vec, ("F", i - 1, "d"))
                        leave(vec.tensor_tensor(heads_of(ND), heads_of(filled(vec, ("O", i, "d"))), v, ALU.mult), ("O", i, "d"))
                    else:
                        vec.tensor_tensor(heads_of(NM), heads_of(NM), v, ALU.mult).then_inc(fin_ready, 1)

            for q in range(len(ITEMS) // 2):
                maximum(2 * q)
                if q:
                    at_out(2 * q - 1)
                decayed(2 * q + 1)
                mixed(2 * q)
                if q >= 4 and q % 4 == 0:
                    final(q // 4 - 1)
            at_out(len(ITEMS) - 1)
            final(TT - 1)

            for c in range(2):
                for t in range(TT):
                    vec.wait_ge(x_in[t], 32)
                    s = slice(c * 512, (c + 1) * 512)
                    leave(vec.tensor_tensor(X[:, t, s], X[:, t, s], filled(vec, ("o", c, t)), ALU.add), ("o", c, t))

            def ms2(t):
                vec.wait_ge(sumsq, TT + 8 + t + 1)
                mean_square(root("n2", t), st[:, 4 + t:5 + t], D)

            ms2(0)
            for t in range(TT):
                if t + 1 < TT:
                    ms2(t + 1)
                vec.tensor_scalar(HN[:, t, :], X[:, t, :], rooted(root("n2", t))[:, 0:1], None, ALU.mult).then_inc(hn_ready, 1)
            for t in range(TT):
                for c in range(2):
                    gained(("h2", t, c), t, c, R_N2)

            def over(v, *shape):
                return v.to_broadcast([P] + list(shape))

            E = NG + NE
            vec.wait_ge(router_in, 64)
            leave(vec.tensor_tensor(LG, filled(vec, "route")[:, 0:TT * E].rearrange("p (t e) -> p t e", t=TT),
                                    over(BR.unsqueeze(1), TT, E), ALU.add), "route")
            left(vec, "route")
            vec.wait_ge(consts2, 7)
            step(vec.tensor_reduce(RS[:, 0, :], LG[:, :, 0:NG], AX, ALU.max))
            vec.tensor_tensor(D4, LG[:, :, 0:NG], over(RS[:, 0, :].unsqueeze(2), TT, NG), ALU.subtract).then_inc(r_dve, 1)

            def first_of(dst, hit, iota, n):
                step(vec.scalar_tensor_tensor(out=C8[:, :, 0:n], in0=hit, scalar=-100.0, in1=iota, op0=ALU.mult, op1=ALU.add))
                step(vec.tensor_reduce(RS[:, 1, :], C8[:, :, 0:n], AX, ALU.min))
                step(vec.tensor_tensor(dst, C8[:, :, 0:n], over(RS[:, 1, :].unsqueeze(2), TT, n), ALU.is_equal))

            vec.wait_ge(r_dve, 1)
            step(vec.tensor_scalar(H8[:, :, 0:NG], D4, 0.0, None, ALU.is_equal))
            first_of(OHG, H8[:, :, 0:NG], IOG4, NG)
            le = LG[:, :, NG:E].rearrange("p t (g j) -> p t g j", g=NG)
            step(vec.tensor_tensor(T32, le, over(OHG.unsqueeze(3), TT, NG, EG), ALU.mult))
            step(vec.tensor_reduce(E8, T32.rearrange("p t g j -> p t j g"), AX, ALU.add))
            for k, oh in enumerate((OH1, OH2)):
                step(vec.tensor_reduce(RS[:, 2 + k, :], E8, AX, ALU.max))
                step(vec.tensor_tensor(H8, E8, over(RS[:, 2 + k, :].unsqueeze(2), TT, EG), ALU.is_equal))
                first_of(oh, H8, IO88, EG)
                if k == 0:
                    step(vec.scalar_tensor_tensor(out=E8, in0=oh, scalar=NEG, in1=E8, op0=ALU.mult, op1=ALU.add))
            for o, oh in ((O1, OH1), (O2, OH2)):
                step(vec.tensor_tensor(o, over(OHG.unsqueeze(3), TT, NG, EG), over(oh.unsqueeze(2), TT, NG, EG), ALU.mult))
            O1F, O2F = (o.rearrange("p t g j -> p t (g j)") for o in (O1, O2))
            vec.tensor_tensor(OHS, O1F, O2F, ALU.add).then_inc(oh_ready, 1)
            vec.tensor_tensor(DM, RS[:, 3, :], RS[:, 2, :], ALU.subtract).then_inc(r_dve, 1)
            vec.wait_ge(r_act, 2)
            step(vec.tensor_reduce(RS[:, 4, :], EXPG, AX, ALU.add))
            step(vec.scalar_tensor_tensor(out=RS[:, 5, :], in0=P2, scalar=1.0, in1=RS[:, 4, :], op0=ALU.add, op1=ALU.mult))
            step(vec.reciprocal(wts[:, 0, :], RS[:, 5, :]))
            step(vec.tensor_tensor(wts[:, 1, :], wts[:, 0, :], P2, ALU.mult))
            leave(vec.tensor_copy(RANK, filled(vec, "rank")[:, 0:(TT + 1) * NE].rearrange("p (t e) -> p t e", e=NE)), "rank")
            left(vec, "rank")
            th = TH.rearrange("p (e q) -> p e q", e=NE)
            q7 = PER_EXPERT_MAX - 1
            step(vec.tensor_tensor(th, over(RANK[:, TT, :].unsqueeze(2), NE, q7), th, ALU.is_gt))
            step(vec.tensor_reduce(NB, th, AX, ALU.add))
            step(vec.tensor_scalar(NB, NB, 1.0, None, ALU.add))
            step(vec.tensor_tensor_scan(BEF, ones[:, 0:NE], NB, 0.0, ALU.mult, ALU.add))
            step(vec.tensor_tensor(BEF, BEF, NB, ALU.subtract))
            step(vec.tensor_copy(tab[:, 0, :], NB[0:1]))
            vec.tensor_copy(tab[:, 1, :], BEF[0:1]).then_inc(tab_ready, 1)
            step(vec.tensor_scalar(NB, BEF, float(BLK), None, ALU.mult))
            step(vec.tensor_tensor(RANK[:, 0:TT, :], RANK[:, 0:TT, :], over(NB.unsqueeze(1), TT, NE), ALU.add))
            for k, o in enumerate((O1F, O2F)):
                step(vec.tensor_tensor(o, o, RANK[:, 0:TT, :], ALU.mult))
                step(vec.tensor_reduce(RS[:, 6 + k, :], o, AX, ALU.add))
            vec.tensor_copy(dest[:, :, :], RS[:, 6:8, :]).then_inc(dest_ready, 1)

            vec.wait_ge(tab_ready, 1)
            gain = prm[:, R_N2:R_N2 + DT].unsqueeze(2).to_broadcast([P, DT, BLK])
            with vec.Fori(0, NE) as e:
                blocks = vec.value_load(tab[0:1, 0, bass.ds(e, 1)], min_val=1, max_val=PER_EXPERT_MAX)
                before = vec.value_load(tab[0:1, 1, bass.ds(e, 1)], min_val=0, max_val=BLOCKS_MAX)
                with vec.Fori(0, blocks) as j:
                    g = before + j
                    vec.wait_ge(xt_full, g + 1)
                    turned = ps[:, 6:8, 0:4 * BLK].rearrange("p a (k b) -> p a k b", k=4)
                    vec.tensor_tensor(XT.rearrange("p (a k) b -> p a k b", a=2), turned,
                                      gain.rearrange("p (a k) b -> p a k b", a=2), ALU.mult).then_inc(xt_left, 1)
                    for f in range(FT):
                        vec.wait_ge(gu_full, g * 2 * FT + (2 * f + 2))
                        vec.wait_ge(g_left, g * FT + (f + 1))
                        vec.tensor_tensor(HID[:, f, :], SG[:, f, :], ps[:, 2 * (f % 2) + 1, 0:BLK], ALU.mult).then_inc(u_left, 1)

            for t in range(TT):
                vec.wait_ge(yg_in[t], 32)
                step(vec.scalar_tensor_tensor(out=X[:, t, :], in0=YG[:, 0, t, :], scalar=wts[:, 0, t:t + 1], in1=X[:, t, :],
                                              op0=ALU.mult, op1=ALU.add))
                vec.scalar_tensor_tensor(out=X[:, t, :], in0=YG[:, 1, t, :], scalar=wts[:, 1, t:t + 1], in1=X[:, t, :],
                                         op0=ALU.mult, op1=ALU.add).then_inc(x3_ready, 1)

            for t in range(TT):
                leave(vec.tensor_copy(HT[:, 4:8, t * P:(t + 1) * P],
                                      filled(vec, ("x3", t, 1)).rearrange("p (k t) -> p k t", k=4)), ("x3", t, 1))
            vec.wait_ge(sink_in, 16)
            vec.wait_ge(consts2, 9 + W2_HEADS)

            def biased(n):
                i, j = divmod(n, PAIRS)
                lo, b = (P if i == 0 else 0), 32 + 8 * (n % 2)
                if n >= 2:
                    filled(vec, ("PT", n - 2))
                for a in range(2):
                    leave(vec.scalar_tensor_tensor(out=SC2[:, n % 2, a, lo:], in0=filled(vec, ("S2", n, a))[:, lo:2 * P],
                                                   scalar=QK ** -0.5, in1=BM[:, j + PAIRS * a, lo:], op0=ALU.mult, op1=ALU.add),
                          ("S2", n, a))
                left(vec, ("S2", n, 0))
                left(vec, ("S2", n, 1))
                snk = sink[:, j:j + PAIRS + 1:PAIRS]
                step(vec.tensor_reduce(st[:, b:b + 2], SC2[:, n % 2, :, lo:], AX, ALU.max))
                step(vec.tensor_tensor(st[:, b:b + 2], st[:, b:b + 2], snk, ALU.max))
                step(vec.tensor_scalar(st[:, b + 2:b + 4], st[:, b:b + 2], -1.0, None, ALU.mult))
                vec.tensor_tensor(st[:, b + 6:b + 8], snk, st[:, b:b + 2], ALU.subtract).then_inc(nmax2, 1)

            def probabilities(n):
                lo, b = (P if n < PAIRS else 0), 32 + 8 * (n % 2)
                vec.wait_ge(exp2, 3 * n + 3)
                step(vec.tensor_tensor(st[:, b + 4:b + 6], st[:, b + 4:b + 6], st[:, b + 6:b + 8], ALU.add))
                step(vec.reciprocal(st[:, b + 4:b + 6], st[:, b + 4:b + 6]))
                for a in range(2):
                    vec.tensor_scalar(SC2[:, n % 2, a, lo:], SC2[:, n % 2, a, lo:], st[:, b + 4 + a:b + 5 + a], None,
                                      ALU.mult).then_inc(pr2_ready, 1)

            for n in range(17):
                if n < 16:
                    biased(n)
                if n:
                    probabilities(n - 1)

            def residual(c, t, key):
                s = slice(c * 512, (c + 1) * 512)
                leave(vec.scalar_tensor_tensor(out=X[:, t, s], in0=X[:, t, s], scalar=ALPHA, in1=filled(vec, key),
                                               op0=ALU.mult, op1=ALU.add), key)

            def ln_stats(name, t, key):
                b = 48 + 2 * t
                left(vec, (key, 0, t) if key == "o2" else (key, t, 0))
                left(vec, (key, 1, t) if key == "o2" else (key, t, 1))
                for c in range(2):
                    step(vec.bn_stats(bn[:, c, :], X[:, t, c * 512:(c + 1) * 512]))
                step(vec.bn_aggr(st[:, b:b + 2], bn[:, :, :].rearrange("p a b -> p (a b)")))
                mean_square(root(name, t), st[:, b + 1:b + 2], 1, 1, LN_EPS)

            def ln_apply(name, t, g, b_):
                b = 48 + 2 * t
                step(vec.tensor_scalar(X[:, t, :], X[:, t, :], st[:, b:b + 1], rooted(root(name, t))[:, 0:1],
                                       ALU.subtract, ALU.mult))
                step(vec.tensor_tensor(X[:, t, :], X[:, t, :], g, ALU.mult))
                vec.tensor_tensor(X[:, t, :], X[:, t, :], b_, ALU.add).then_inc(ln_ready, 1)

            for c in range(2):
                for t in range(TT):
                    residual(c, t, ("o2", c, t))
                    if c == 1:
                        ln_stats("l1", t, "o2")
            vec.wait_ge(ln_in, 32)
            for t in range(TT):
                ln_apply("l1", t, LNG1, LNB1)
            for f in range(FFT):
                left(vec, ("up", f))
                vec.tensor_tensor(AT[:, f, :], AT[:, f, :], AT[:, f, :], ALU.mult).then_inc(at_ready, 1)
            vec.wait_ge(late_in, 64)
            for t in range(TT):
                for c in range(2):
                    residual(c, t, ("dn", t, c))
                ln_stats("l2", t, "dn")
                ln_apply("l2", t, LNG2, LNB2)

            def gate_in_(n):
                c, t = divmod(n, TT)
                if n >= 2:
                    vec.wait_ge(out_ready, n - 1)
                leave(vec.tensor_tensor(GT[:, n % 2, :], filled(vec, ("gt", n)), BG[:, c * 512:(c + 1) * 512], ALU.add), ("gt", n))

            gate_in_(0)
            for n in range(2 * TT):
                c, t = divmod(n, TT)
                s = slice(c * 512, (c + 1) * 512)
                if n + 1 < 2 * TT:
                    gate_in_(n + 1)
                vec.wait_ge(gate_act, n + 1)
                leave(vec.tensor_tensor(GT[:, n % 2, :], GT[:, n % 2, :], filled(vec, ("pl", n)), ALU.mult), ("pl", n))
                left(vec, ("pl", n))
                vec.tensor_tensor(OUT2[:, t, s], GT[:, n % 2, :], X[:, t, s], ALU.add).then_inc(out_ready, 1)


_OUT = (1, T, D)


def kernel(**inputs):
    from concourse import bacc
    from concourse.bass_utils import run_bass_kernel_spmd

    nc = bacc.Bacc("TRN2", target_bir_lowering=False, num_devices=1)
    arrays, args = {}, {}
    for name, value in inputs.items():
        a = np.ascontiguousarray(value)
        arrays[f"in_{name}"] = a
        args[name] = nc.dram_tensor(f"in_{name}", a.shape, mybir.dt.from_np(a.dtype), kind="ExternalInput").ap()
    out = nc.dram_tensor("result", _OUT, F32, kind="ExternalOutput").ap()
    build(nc, args, out)
    r = run_bass_kernel_spmd(nc, [arrays], core_ids=[0])
    return r.results[0]["result"]
```

```python
from contextlib import ExitStack

import numpy as np

import concourse.bass as bass
from concourse import mybir

F32 = mybir.dt.float32
BF16 = mybir.dt.bfloat16
F32R = mybir.dt.float32r
I32 = mybir.dt.int32
ALU = mybir.AluOpType
ACT = mybir.ActivationFunctionType
AX = mybir.AxisListType.X

P = 128
T = 512
D = 1024
TT = T // P
DT = D // P
RING = 6
UNIT = 4096
NEG = -1e30
EPS = 1e-6
LN_EPS = 1e-5
HEADS = 4
HD = 128
QK = 64
LAMBDA_INIT = 0.8 - 0.6
NE = 32
NG = 4
EG = NE // NG
FT = 4
BLK = 64
PER_EXPERT_MAX = -(-T // BLK)
BLOCKS_MAX = 2 * T // BLK + NE
BLOCKS_HELD = BLOCKS_MAX + PER_EXPERT_MAX + 1
SLOTS = BLOCKS_HELD * BLK
NO_ROW = 2 * T
W2_HEADS = 8
PAIRS = W2_HEADS // 2
WINDOW = 128
FFT = 4 * D // P
POOL_WINDOWS = (2, 4, 8, 16)
ALPHA = 2.0 ** 0.25

C_MQ, C_MK, C_MV, C_MO, C_GATES, C_AQ, C_AK, C_AV = 0, 512, 1024, 1536, 2048, 2056, 2568, 3080
R_N1, R_N2, R_CB, R_CW, R_MN, R_AN, R_PS, R_QN, R_KN = 0, 8, 16, 24, 56, 57, 58, 62, 63
N_PARAMS = 64
N_CONSTS2 = 21
N_SMALL = 17
N_CONSTS = 20

UNITS_1 = ["mq", "mk", "mo", "aq", "ak", "av", "mv", "out0", "out1"]
UNITS_2 = (["q2", "kv2", "pool2", "mix0", "mix1"] + [f"up{n}" for n in range(8)]
           + [f"down{n}" for n in range(8)] + ["ple", "gate0", "gate1"])
DMAS_OF = {"q2": 8, "mix0": 3, "mix1": 3}
SECOND = len(UNITS_1) + 3 * NE

ROOTS = ([("n1", t) for t in range(TT)] + [("aq", t) for t in range(TT)]
         + [("ak", t) for t in range(TT)]
         + [(k, t) for t in range(TT) for k in ("fd", "fm")] + [("n2", t) for t in range(TT)]
         + [("l1", t) for t in range(TT)] + [("l2", t) for t in range(TT)])

ITEMS = [(i, h, kind) for i in range(TT) for h in range(HEADS) for kind in "dm"]
FIN_STEP = 13
BANKS = {"d": (2, 3, 6, 7), "m": (4, 5, 1, 0)}


def build(nc, A, out):
    ctx = ExitStack()

    def sb(name, shape, dt=F32):
        return ctx.enter_context(nc.sbuf_tensor(name, shape, dt))

    def sem(name):
        return ctx.enter_context(nc.semaphore(name))

    with ctx:
        base = -(-nc.sbuf_base // 32) * 32
        ring = sb("ring", [P, RING, UNIT])
        X = sb("X", [P, TT, D])
        HT = sb("HT", [P, DT, T])
        M = sb("M", [P, 17920])
        def as_r(name, a, *shape):
            return nc.alloc_sbuf_tensor_at(name, [P] + list(shape), F32R, offset=base + 4 * a)

        HT_AT = RING * UNIT + TT * D
        M_AT = HT_AT + DT * T
        ring_r = [as_r(f"ring_r{s}", s * UNIT, UNIT) for s in range(RING)]
        ident = sb("ident", [P, P])
        identb = sb("identb", [P, P], BF16)
        maskc = sb("maskc", [P, P], BF16)
        maskk = sb("maskk", [P, P], BF16)
        ones = sb("ones", [P, P])
        headsel = sb("headsel", [HEADS, HEADS, P])
        wrow = sb("wrow", [HEADS, T])
        prm = sb("prm", [P, N_PARAMS])
        wgates = sb("wgates", [P, DT, 8])
        msv = sb("msv", [P, len(ROOTS), 8])
        rsv = sb("rsv", [P, len(ROOTS), 8])
        half = sb("half", [P, 8])
        st = sb("st", [P, 96])
        cols = sb("cols", [P, 2, TT, HEADS])
        rg = sb("rg", [HEADS, 12])
        lamc = sb("lamc", [P, 4])
        wts = sb("wts", [P, 2, TT])
        dest = sb("dest", [P, 2, TT], I32)
        tokid = sb("tokid", [P, 2, TT, 2], I32)
        tab = sb("tab", [1, 2, NE + 1], I32)
        idx = sb("idx", [BLK, 2, 1], I32)
        sink = sb("sink", [P, W2_HEADS])
        bn = sb("bn", [P, 2, 6])
        inv16 = sb("inv16", [P, 16])

        def m(a, *shape):
            v = M[:, a:a + int(np.prod(shape))]
            if len(shape) == 2:
                v = v.rearrange("p (a b) -> p a b", a=shape[0])
            if len(shape) == 3:
                v = v.rearrange("p (a b c) -> p a b c", a=shape[0], b=shape[1])
            return v

        MV, MO = m(0, TT, 512), m(2048, TT, 512)
        QA, KA, AV = m(4096, HEADS, T), m(6144, HEADS, T), m(8192, TT, 512)
        MIXA = m(10240, HEADS, T)
        JUNK3 = m(15872, 2, D)
        JUNK2 = m(0, 2, D)
        PROWS = m(12288, P)[0:N_PARAMS]
        EE = m(12288, 2, 512)
        AD, ATD = m(13312, 512), m(13824, 512)
        DD, AM, ATM = m(14336, 512), m(14848, 512), m(15360, 512)
        ND, SQD, NM, SQM = m(15872, 512), m(16384, 512), m(16896, 512), m(17408, 512)
        RI, RF, RT, RB, RR, RM, REM = (m(14336 + 512 * k, T)[0:HEADS] for k in range(7))
        GTOK = m(13312, TT, 8)
        LAMIN = m(13376, 4, QK)[0:1]
        LAMP = m(13632, 2 * QK)[0:1]
        unheld = m(17408, 2 * BLOCKS_HELD)[0:BLK].bitcast(I32).rearrange("p (n o) -> p n o", o=2)
        QKM = X[:, :, :].rearrange("p t d -> p (t d)").rearrange("p (c t) -> p c t", c=8)
        HN = m(4096, TT, D)
        WR = m(8192, DT, NG + NE)
        BR = m(8480, NG + NE)
        SQS = (SQD, SQM)
        UPPER, LG = m(8576, P), m(8704, TT, NG + NE)
        OHG, D4, EXPG = m(8848, TT, NG), m(8864, TT, NG), m(8880, TT, NG)
        E8, C8, H8, OH1, OH2 = (m(8896 + 32 * k, TT, EG) for k in range(5))
        T32, O1, O2 = (m(9056 + 128 * k, TT, NG, EG) for k in range(3))
        OHS = m(9440, TT, NE)
        NB, BEF = m(9568, NE), m(9600, NE)
        TH = m(9632, NE * (PER_EXPERT_MAX - 1))
        IOG, IO8 = m(9856, TT * NG), m(9872, TT * EG)
        IOG4, IO88 = m(9856, TT, NG), m(9872, TT, EG)
        RS = m(9904, 8, TT)
        P2, DM = m(9936, TT), m(9940, TT)
        RANK = m(9952, TT + 1, NE)
        XG, XTG = m(0, D)[0:BLK], m(1024, DT, BLK)
        XTS = as_r("XTS", M_AT + 1536, DT, 2, BLK)
        YB = m(2560, 2, 512)[0:BLK]
        SG, HIDG = m(3584, FT, BLK), m(3840, FT, BLK)
        ids = m(15232, 2 * BLOCKS_HELD)[0:BLK].bitcast(I32).rearrange("p (n o) -> p n o", o=2)
        SUM2 = m(14592, 2 * BLK)
        HIDS = as_r("HIDS", M_AT + 14720, 2, FT, BLK)
        GUS = m(15872, 2, 512)
        HI = [as_r(f"hi{u}", a, UNIT) for u, a in enumerate((HT_AT, M_AT + UNIT, M_AT + 2 * UNIT))]
        YG = m(4096, 2, TT, D)
        BM = m(12288, W2_HEADS, 2 * P)
        DISTI = m(14336, 2 * P)
        Q2, K2, V2, U2, DP = m(0, PAIRS, T), m(2048, T), m(2560, TT, P), m(3072, 4, T), m(5120, 4, T)
        MIX2 = m(7168, DT, T)
        PW = m(11264, 2, T)
        SC2 = m(14336, 2, 2, 2 * P)
        PT2 = m(15360, 2, 512)
        AT = m(0, FFT, T)
        LNB1, LNG1 = m(0, D), m(16384, D)
        WP2 = m(16384, 4, P)
        LNG2, LNB2, BG = (HT[:, 2 * k:2 * k + 2, :].rearrange("p a b -> p (a b)") for k in range(3))
        PIN = HT[:, 6:8, :].rearrange("p a b -> p (a b)").rearrange("p (t c) -> p t c", t=TT)
        PET = m(16384, 2, T)
        H5T = m(0, DT, T)
        GT = m(4096, 2, 512)
        OUT2 = m(8192, TT, D)

        ps = ctx.enter_context(nc.psum_tensor("ps", [P, 8, 512], F32))
        h_rows = nc.dram_tensor("h_rows", [T, D], F32, kind="Internal").ap()
        slot_tokens = nc.dram_tensor("slot_tokens", [SLOTS, 2], I32, kind="Internal").ap()
        results = nc.dram_tensor("results", [NO_ROW, D], F32, kind="Internal").ap()

        full = [sem(f"bank_full{b}") for b in range(8)]
        empty = [sem(f"bank_empty{b}") for b in range(8)]
        slot_in = [sem(f"slot_in{s}") for s in range(RING)]
        unit_used = sem("unit_used")
        x_in = [sem(f"x_in{t}") for t in range(TT)]
        small_in = sem("small_in")
        wgates_in = sem("wgates_in")
        sink_in = sem("sink_in")
        router_in = sem("router_in")
        consts = sem("consts")
        sumsq = sem("sumsq")
        ms_ready = sem("ms_ready")
        root_done = sem("root_done")
        xn_ready = sem("xn_ready")
        dve_step = sem("dve_step")
        silu_done = sem("silu_done")
        row_dve = sem("row_dve")
        row_act = sem("row_act")
        rows_done = sem("rows_done")
        lam_prod = sem("lam_prod")
        nmax_ready = sem("nmax_ready")
        ad_ready = sem("ad_ready")
        w_ready = sem("w_ready")
        fin_sq = sem("fin_sq")
        fin_in = sem("fin_in")
        fin_ready = sem("fin_ready")
        hn_ready = sem("hn_ready")
        h_out = sem("h_out")
        r_dve = sem("r_dve")
        r_act = sem("r_act")
        oh_ready = sem("oh_ready")
        tab_ready = sem("tab_ready")
        ids_out = sem("ids_out")
        table_in = sem("table_in")
        idx_kept = [sem(f"idx_kept{k}") for k in range(2)]
        waits_met = sem("waits_met")
        idx_in = sem("idx_in")
        rows_in = sem("rows_in")
        xt_full = sem("xt_full")
        xt_gained = sem("xt_gained")
        xt_hi = sem("xt_hi")
        xt_lo = sem("xt_lo")
        w_hi = sem("w_hi")
        w_lo = sem("w_lo")
        gate_full = sem("gate_full")
        up_full = sem("up_full")
        gu_out = sem("gu_out")
        sum_full = sem("sum_full")
        sg_ready = sem("sg_ready")
        hid_gated = sem("hid_gated")
        hid_hi = sem("hid_hi")
        hid_ready = sem("hid_ready")
        y_full = sem("y_full")
        y_left = sem("y_left")
        y_out = sem("y_out")
        yg_in = [sem(f"yg_in{t}") for t in range(TT)]
        x3_ready = sem("x3_ready")
        consts2 = sem("consts2")
        dest_ready = sem("dest_ready")
        pool_step = sem("pool_step")
        wp_in = sem("wp_in")
        pool_ready = sem("pool_ready")
        nmax2 = sem("nmax2")
        exp2 = sem("exp2")
        pr2_ready = sem("pr2_ready")
        ln_in = sem("ln_in")
        ln_ready = sem("ln_ready")
        at_ready = sem("at_ready")
        late_in = sem("late_in")
        gate_act = sem("gate_act")
        out_ready = sem("out_ready")
        stored = sem("stored")

        turn, turns_of = {}, [0] * 8
        last_turn = {}

        def open_turn(pe, key, bank):
            turn[key] = (bank, turns_of[bank])
            if turns_of[bank]:
                pe.wait_ge(empty[bank], turns_of[bank])
            turns_of[bank] += 1
            return ps[:, bank, :]

        def fill_turn(ins, key):
            ins.then_inc(full[turn[key][0]], 1)

        def filled(eng, key):
            eng.wait_ge(full[turn[key][0]], turn[key][1] + 1)
            return ps[:, turn[key][0], :]

        def leave(ins, key):
            ins.then_inc(empty[turn[key][0]], 1)

        def left(eng, key):
            eng.wait_ge(empty[turn[key][0]], turn[key][1] + 1)

        place, slot_total = {}, [0] * RING
        for n, u in enumerate(UNITS_1):
            slot_total[n % RING] += 16 * DMAS_OF.get(u, 1)
            place[u] = (n % RING, slot_total[n % RING])
        expert_base = list(slot_total)
        slot_total = [c + 16 * NE // 2 for c in slot_total]
        for n, u in enumerate(UNITS_2):
            s = (SECOND + n) % RING
            slot_total[s] += 16 * DMAS_OF.get(u, 1)
            place[u] = (s, slot_total[s])

        def unit(pe, u):
            pe.wait_ge(slot_in[place[u][0]], place[u][1])
            return ring[:, place[u][0], :]

        def raw_loads(e, odd, s):
            return (e - odd) * 8 + (expert_base[s] + 16)

        def expert_slots(odd):
            return [(len(UNITS_1) + 3 * odd + k) % RING for k in range(3)]

        def each_expert(eng, work, start=None):
            def one(e, odd, ahead):
                before = eng.value_load(tab[0:1, 0, bass.ds(e, 1)], min_val=0, max_val=BLOCKS_MAX)
                extra = eng.value_load(tab[0:1, 1, bass.ds(e, 1)], min_val=0, max_val=PER_EXPERT_MAX - 1)
                if start:
                    start(e, odd)
                with eng.If(extra > 0):
                    with eng.Fori(0, extra) as j:
                        work(e, before + j, odd, False, False)
                work(e, before + extra, odd, True, ahead)

            with eng.Fori(0, NE // 2 - 1) as ii:
                for odd in range(2):
                    one(2 * ii + odd, odd, True)
            one(NE - 2, 0, True)
            one(NE - 1, 1, False)

        def root(name, t):
            return ROOTS.index((name, t))

        def until(eng, s, value):
            eng.wait_ge(s, value)
            eng.sem_inc(waits_met, 1)

        block = ctx.enter_context(nc.Block())

        @block.tensor
        def _(pe):
            def transposes(key, bank, src, n, width=P, idn=None):
                o = open_turn(pe, key, bank)
                idn = ident[:, :] if idn is None else idn
                for c in range(n):
                    ins = pe.transpose(o[:, c * width:(c + 1) * width], src[:, c * P:(c + 1) * P], idn)
                fill_turn(ins, key)

            pe.wait_ge(consts, N_CONSTS)
            pe.wait_ge(small_in, 16 * N_SMALL)
            transposes("prm", 7, PROWS, 1, N_PARAMS, ident[0:N_PARAMS, 0:N_PARAMS])
            for t in range(TT):
                pe.wait_ge(xn_ready, t + 1)
                for c in range(2):
                    transposes(("h", t, c), 2 + (2 * t + c) % 4, X[:, t, c * 512:(c + 1) * 512], 4)

            pe.wait_ge(wgates_in, 16)
            o = open_turn(pe, "gates", 6)
            for t in range(TT):
                left(pe, ("h", t, 0))
                left(pe, ("h", t, 1))
                for k in range(DT):
                    ins = pe.matmul(o[:, t * 8:t * 8 + 8], HT[:, k, t * P:(t + 1) * P],
                                    wgates[:, k, :], start=(k == 0), stop=(k == DT - 1))
            fill_turn(ins, "gates")
            pe.wait_ge(lam_prod, 1)
            o = open_turn(pe, "lam", 7)
            fill_turn(pe.matmul(o[:, 0:2], ones[0:1, :], LAMP[:, 0:2], start=True, stop=True), "lam")

            jobs = [0]

            def project(u, n, key, channel_major):
                w = unit(pe, u).rearrange("p (k c) -> p k c", k=DT)
                o = open_turn(pe, key, jobs[0] % 2)
                jobs[0] += 1
                for k in range(DT):
                    a, b = w[:, k, n * P:(n + 1) * P], HT[:, k, :]
                    if not channel_major:
                        a, b = HT[:, k, n * P:(n + 1) * P], w[:, k, :]
                    ins = pe.matmul(o, a, b, start=(k == 0), stop=(k == DT - 1))
                fill_turn(ins, key)
                last_turn[u] = key

            for n in range(4):
                project("mq", n, ("mq", n), True)
                if n == 0:
                    left(pe, "gates")
                    for g, bank in ((0, 4), (1, 5)):
                        o = open_turn(pe, ("grow", g), bank)
                        for t in range(TT):
                            ins = pe.transpose(o[0:HEADS, t * P:(t + 1) * P],
                                               GTOK[:, t, g * HEADS:(g + 1) * HEADS], ident[:, :])
                        fill_turn(ins, ("grow", g))
            for n in range(4):
                project("mk", n, ("mk", n), True)
            for n in range(4):
                project("mo", n, ("mo", n), False)
            pe.wait_ge(rows_done, 1)
            o = open_turn(pe, "gcols", 4)
            for g, src in ((0, RR), (1, REM)):
                for t in range(TT):
                    ins = pe.transpose(o[:, (g * TT + t) * HEADS:(g * TT + t + 1) * HEADS],
                                       src[:, t * P:(t + 1) * P], ident[0:HEADS, 0:HEADS])
            fill_turn(ins, "gcols")
            names = [(u, n) for u in ("aq", "ak", "av", "mv") for n in range(4)]
            for k, (u, n) in enumerate(names):
                project(u, n, (u, n), False)
                if 1 <= k <= 8:
                    left(pe, names[k - 1])
                    transposes(("T",) + names[k - 1], 6 + k % 2, (ND, NM)[(k - 1) % 2], HEADS)

            def scores(n):
                i, h, kind = ITEMS[n]
                W = (i + 1) * P
                b0, b1, _, _ = BANKS[kind]
                if kind == "d":
                    if h == 0:
                        left(pe, ("T", "aq", i))
                        left(pe, ("T", "ak", i))
                    for c, bank in ((0, b0), (1, b1)):
                        r = slice(c * QK, (c + 1) * QK)
                        o = open_turn(pe, ("S", n, c), bank)
                        pe.matmul(o[:, 0:W], QA[r, h, i * P:W], KA[r, h, 0:W], start=True, stop=False)
                        fill_turn(pe.matmul(o[:, i * P:W], identb[:, :], maskk[:, :],
                                            start=False, stop=True), ("S", n, c))
                else:
                    if h == 0 and i:
                        pe.wait_ge(w_ready, i)
                    o = open_turn(pe, ("S", n, 0), b0)
                    pe.matmul(o[:, 0:W], headsel[:, h, :], wrow[:, 0:W], start=True, stop=False)
                    fill_turn(pe.matmul(o[:, i * P:W], identb[:, :], maskc[:, :],
                                        start=False, stop=True), ("S", n, 0))
                    if n == 1:
                        pe.wait_ge(silu_done, 8)
                    o = open_turn(pe, ("S", n, 1), b1)
                    fill_turn(pe.matmul(o[:, 0:W], QKM[:, h, i * P:W], QKM[:, HEADS + h, 0:W],
                                        start=True, stop=True), ("S", n, 1))

            def turned(n):
                i, h, kind = ITEMS[n]
                if kind == "d":
                    pe.wait_ge(ad_ready, n // 2 + 1)
                else:
                    left(pe, ("S", n, 1))
                transposes(("AT", n), BANKS[kind][2], AD if kind == "d" else AM, i + 1)

            def outputs(n):
                i, h, kind = ITEMS[n]
                left(pe, ("AT", n))
                a, v = (ATD, AV) if kind == "d" else (ATM, MV)
                if n < 2:
                    for t in range(TT):
                        left(pe, ("av" if kind == "d" else "mv", t))
                if h == 0:
                    open_turn(pe, ("O", i, kind), BANKS[kind][3])
                o = ps[:, BANKS[kind][3], :]
                for j in range(i + 1):
                    ins = pe.matmul(o[:, h * P:(h + 1) * P], a[:, j * P:(j + 1) * P],
                                    v[:, j, h * P:(h + 1) * P], start=(j == 0), stop=(j == i))
                if h == HEADS - 1:
                    fill_turn(ins, ("O", i, kind))

            def final(i):
                left(pe, ("O", i, "d"))
                pe.wait_ge(fin_ready, i + 1)
                for kind in "dm":
                    transposes(("F", i, kind), BANKS[kind][2], ND if kind == "d" else NM, HEADS)

            for n in range(len(ITEMS) + 2):
                if n < len(ITEMS):
                    scores(n)
                if 1 <= n <= len(ITEMS):
                    turned(n - 1)
                if n >= 2:
                    outputs(n - 2)
                if n >= FIN_STEP and (n - FIN_STEP) % 8 == 0:
                    final((n - FIN_STEP) // 8)
            final(TT - 1)

            for i in range(TT):
                for kind in "dm":
                    left(pe, ("F", i, kind))
            for c in range(2):
                w = unit(pe, f"out{c}").rearrange("p (k c) -> p k c", k=DT)
                for t in range(TT):
                    key = ("o", c, t)
                    o = open_turn(pe, key, 2 + (c * TT + t) % 4)
                    for k in range(DT):
                        a = HT[:, k, t * P:(t + 1) * P] if k < HEADS else MIXA[:, k - HEADS, t * P:(t + 1) * P]
                        ins = pe.matmul(o, a, w[:, k, :], start=(k == 0), stop=(k == DT - 1))
                    fill_turn(ins, key)
                last_turn[f"out{c}"] = key

            for t in range(TT):
                pe.wait_ge(hn_ready, t + 1)
                for c in range(2):
                    transposes(("h2", t, c), 2 + (2 * t + c) % 4, HN[:, t, c * 512:(c + 1) * 512], 4)
            pe.wait_ge(router_in, 64)
            o = open_turn(pe, "route", 7)
            E = NG + NE
            for t in range(TT):
                left(pe, ("h2", t, 0))
                left(pe, ("h2", t, 1))
                for k in range(DT):
                    ins = pe.matmul(o[:, t * E:(t + 1) * E], HT[:, k, t * P:(t + 1) * P], WR[:, k, :],
                                    start=(k == 0), stop=(k == DT - 1))
            fill_turn(ins, "route")
            pe.wait_ge(oh_ready, 1)
            o = open_turn(pe, "rank", 6)
            for t in range(TT + 1):
                for j in range(min(t + 1, TT)):
                    ins = pe.matmul(o[:, t * NE:(t + 1) * NE], UPPER if j == t else ones[:, :],
                                    OHS[:, j, :], start=(j == 0), stop=(j == min(t, TT - 1)))
            fill_turn(ins, "rank")

            def turn_rows(g, a):
                if a == 0:
                    until(pe, rows_in, g * 16 + 16)
                for k in range(4):
                    ins = pe.matmul(ps[:, 6 + a, k * 2 * BLK:(k + 1) * 2 * BLK],
                                    XG[:, (4 * a + k) * P:(4 * a + k + 1) * P], SUM2[0:BLK, :], start=True, stop=True)
                if a == 1:
                    ins.then_inc(xt_full, 1)

            def expert_block(e, g, odd, last, ahead):
                raw = expert_slots(odd)

                def product(u, part):
                    until(pe, w_lo if part else w_hi, e * 6 + (2 * u + 2))
                    w = (ring_r[raw[u]] if part else HI[u])[:, :].rearrange("p (k c) -> p k c", k=DT)
                    for k in range(DT):
                        ins = pe.matmul(ps[:, u, :], XTS[:, k, :, :].rearrange("p s b -> p (s b)"), w[:, k, :],
                                        start=(part == 0 and k == 0), stop=(part == 1 and k == DT - 1))
                    return ins

                def summed(u):
                    until(pe, gu_out, g * 2 + (u + 1))
                    for f in range(FT):
                        ins = pe.matmul(ps[:, 2 + u, f * P:(f + 1) * P], GUS[:, u, f * P:(f + 1) * P], SUM2,
                                        start=True, stop=True)
                    ins.then_inc(sum_full, 1)

                until(pe, xt_lo, g + 1)
                product(0, 0)
                product(0, 1).then_inc(gate_full, 1)
                product(1, 0)
                summed(0)
                product(1, 1).then_inc(up_full, 1)
                turn_rows(g + 1, 0)
                summed(1)
                turn_rows(g + 1, 1)
                until(pe, y_left, g * 2 + 1)
                until(pe, hid_hi, g + 1)
                for c in range(2):
                    for n, (a, part) in enumerate(((0, 0), (1, 0), (0, 1))):
                        if c == 0 and n == 1:
                            until(pe, hid_ready, g + 1)
                        if c == 0 and n == 2:
                            until(pe, w_lo, e * 6 + 6)
                        w = (ring_r[raw[2]] if part else HI[2])[:, :].rearrange("p (k c) -> p k c", k=FT)
                        for f in range(FT):
                            ins = pe.matmul(ps[0:BLK, 4 + c, :], HIDS[:, a, f, :], w[:, f, c * 512:(c + 1) * 512],
                                            start=(n == 0 and f == 0), stop=(n == 2 and f == FT - 1))
                    ins.then_inc(y_full, 1)

            pe.wait_ge(tab_ready, 1)
            pe.wait_ge(consts2, N_CONSTS2)
            turn_rows(0, 0)
            turn_rows(0, 1)
            each_expert(pe, expert_block)

            for t in range(TT):
                pe.wait_ge(x3_ready, t + 1)
                for c in range(2):
                    transposes(("x3", t, c), 2 + (2 * t + c) % 4, X[:, t, c * 512:(c + 1) * 512], 4)
            for t in range(TT):
                left(pe, ("x3", t, 0))
                left(pe, ("x3", t, 1))

            w = unit(pe, "q2").rearrange("p (k c) -> p k c", k=DT)
            for n in range(PAIRS):
                o = open_turn(pe, ("q2", n), n % 2)
                for k in range(DT):
                    ins = pe.matmul(o, w[:, k, n * P:(n + 1) * P], HT[:, k, :], start=(k == 0), stop=(k == DT - 1))
                fill_turn(ins, ("q2", n))
            last_turn["q2"] = ("q2", 3)
            w = unit(pe, "kv2")[:, 0:DT * 2 * P].rearrange("p (k c) -> p k c", k=DT)
            o = open_turn(pe, "k2", 0)
            for k in range(DT):
                ins = pe.matmul(o, w[:, k, 0:P], HT[:, k, :], start=(k == 0), stop=(k == DT - 1))
            fill_turn(ins, "k2")
            o = open_turn(pe, "v2", 1)
            for t in range(TT):
                for k in range(DT):
                    ins = pe.matmul(o[:, t * P:(t + 1) * P], HT[:, k, t * P:(t + 1) * P], w[:, k, P:2 * P],
                                    start=(k == 0), stop=(k == DT - 1))
            fill_turn(ins, "v2")
            last_turn["kv2"] = "v2"
            w = unit(pe, "pool2").rearrange("p (k c) -> p k c", k=DT)
            for n in range(4):
                o = open_turn(pe, ("u2", n), n % 2)
                for k in range(DT):
                    ins = pe.matmul(o, w[:, k, n * P:(n + 1) * P], HT[:, k, :], start=(k == 0), stop=(k == DT - 1))
                fill_turn(ins, ("u2", n))
            last_turn["pool2"] = ("u2", 3)

            def scores2(n):
                i, j = divmod(n, PAIRS)
                lo = P if i == 0 else 0
                for a in range(2):
                    r = slice(a * QK, (a + 1) * QK)
                    o = open_turn(pe, ("S2", n, a), 2 + 2 * (n % 2) + a)
                    fill_turn(pe.matmul(o[:, lo:2 * P], Q2[r, j, i * P:(i + 1) * P],
                                        K2[r, (i - 1) * P + lo:(i + 1) * P], start=True, stop=True),
                              ("S2", n, a))

            def turned2(n):
                i, j = divmod(n, PAIRS)
                pe.wait_ge(pr2_ready, 2 * n + 2)
                o = open_turn(pe, ("PT", n), 6)
                for a in range(2):
                    for b in range(1 if i == 0 else 0, 2):
                        ins = pe.transpose(o[:, (2 * a + b) * P:(2 * a + b + 1) * P],
                                           SC2[:, n % 2, a, b * P:(b + 1) * P], ident[:, :])
                fill_turn(ins, ("PT", n))

            def outputs2(n):
                i, j = divmod(n, PAIRS)
                left(pe, ("PT", n))
                if n == 0:
                    left(pe, "v2")
                if j == 0:
                    open_turn(pe, ("O2", i), 7)
                b0 = 1 if i == 0 else 0
                for a in range(2):
                    for b in range(b0, 2):
                        ins = pe.matmul(ps[a * QK:(a + 1) * QK, 7, j * P:(j + 1) * P],
                                        V2[:, i - 1 + b, a * QK:(a + 1) * QK],
                                        PT2[:, n % 2, (2 * a + b) * P:(2 * a + b + 1) * P],
                                        start=(b == b0), stop=(b == 1))
                if j == PAIRS - 1:
                    fill_turn(ins, ("O2", i))

            left(pe, ("q2", 3))
            left(pe, ("q2", 2))
            left(pe, "k2")
            for n in range(18):
                if n < 16:
                    scores2(n)
                if 1 <= n <= 16:
                    turned2(n - 1)
                if n >= 2:
                    outputs2(n - 2)
            pe.wait_ge(wp_in, 16)
            for g in range(4):
                pe.wait_ge(pool_ready, g + 1)
                o = open_turn(pe, ("pw", g), g % 2)
                fill_turn(pe.matmul(o, WP2[:, g, :], DP[:, g, :], start=True, stop=True), ("pw", g))
            for g in range(2, 4):
                left(pe, ("pw", g))
            left(pe, ("O2", 3))
            for c in range(2):
                w = unit(pe, f"mix{c}").rearrange("p (k c) -> p k c", k=DT)
                for t in range(TT):
                    key = ("o2", c, t)
                    o = open_turn(pe, key, 2 + (c * TT + t) % 4)
                    for k in range(DT):
                        ins = pe.matmul(o, MIX2[:, k, t * P:(t + 1) * P], w[:, k, :],
                                        start=(k == 0), stop=(k == DT - 1))
                    fill_turn(ins, key)
                last_turn[f"mix{c}"] = key

            for t in range(TT):
                pe.wait_ge(ln_ready, t + 1)
                for c in range(2):
                    transposes(("h1", t, c), 2 + (2 * t + c) % 4, X[:, t, c * 512:(c + 1) * 512], 4)
            for t in range(TT):
                left(pe, ("h1", t, 0))
                left(pe, ("h1", t, 1))
            for n in range(8):
                w = unit(pe, f"up{n}").rearrange("p (k c) -> p k c", k=DT)
                for f in range(4):
                    key = ("up", 4 * n + f)
                    o = open_turn(pe, key, (4 * n + f) % 4)
                    for k in range(DT):
                        ins = pe.matmul(o, w[:, k, f * P:(f + 1) * P], HT[:, k, :],
                                        start=(k == 0), stop=(k == DT - 1))
                    fill_turn(ins, key)
                last_turn[f"up{n}"] = key
            pe.wait_ge(late_in, 64)
            for t in range(TT):
                transposes(("pt", t), 4 + t % 4, PIN[:, t, :], 2)
            for t in range(TT):
                for c in range(2):
                    open_turn(pe, ("dn", t, c), 2 * t + c)
            pe.wait_ge(at_ready, FFT)
            for n in range(8):
                w = unit(pe, f"down{n}").rearrange("p (k c) -> p k c", k=4)

                def product(k, t, c):
                    return pe.matmul(ps[:, 2 * t + c, :], AT[:, 4 * n + k, t * P:(t + 1) * P],
                                     w[:, k, c * 512:(c + 1) * 512], start=(n == 0 and k == 0),
                                     stop=(n == 7 and k == 3))
                if n < 7:
                    for k in range(4):
                        for t in range(TT):
                            for c in range(2):
                                ins = product(k, t, c)
                    pe.drain().then_inc(unit_used, 1)
                else:
                    for t in range(TT):
                        for c in range(2):
                            for k in range(4):
                                ins = product(k, t, c)
                            fill_turn(ins, ("dn", t, c))
                    last_turn["down7"] = ("dn", TT - 1, 1)
            for t in range(TT):
                pe.wait_ge(ln_ready, TT + t + 1)
                for c in range(2):
                    transposes(("h5", t, c), 2 * t + c, X[:, t, c * 512:(c + 1) * 512], 4)
            for t in range(TT):
                left(pe, ("pt", t))
                left(pe, ("h5", t, 0))
                left(pe, ("h5", t, 1))
            wl = unit(pe, "ple")[:, 0:2 * D].rearrange("p (k c) -> p k c", k=2)
            for c in range(2):
                w = unit(pe, f"gate{c}").rearrange("p (k c) -> p k c", k=DT)
                for t in range(TT):
                    n = c * TT + t
                    o = open_turn(pe, ("gt", n), n % 4)
                    for k in range(DT):
                        ins = pe.matmul(o, H5T[:, k, t * P:(t + 1) * P], w[:, k, :],
                                        start=(k == 0), stop=(k == DT - 1))
                    fill_turn(ins, ("gt", n))
                    o = open_turn(pe, ("pl", n), 4 + n % 4)
                    for k in range(2):
                        ins = pe.matmul(o, PET[:, k, t * P:(t + 1) * P], wl[:, k, c * 512:(c + 1) * 512],
                                        start=(k == 0), stop=(k == 1))
                    fill_turn(ins, ("pl", n))

        @block.sync
        def _(sp):
            W1, W2, RT_ = A["w_in"][0], A["w_in_2"][0], None
            cols_of = {"mq": C_MQ, "mk": C_MK, "mo": C_MO, "aq": C_AQ, "ak": C_AK, "av": C_AV, "mv": C_MV}

            def load(u):
                s = place[u][0]
                dst = ring[:, s, :]
                k8 = dst.rearrange("p (k c) -> p k c", k=DT)

                def put(d, src):
                    sp.dma_start(d, src).then_inc(slot_in[s], 16)

                def columns(w, a, n):
                    return w[:, a:a + n].rearrange("(k p) c -> p k c", p=P)

                if u in cols_of:
                    put(k8, columns(W1, cols_of[u], 512))
                elif u.startswith("out"):
                    put(k8, columns(A["w_out"][0], 512 * int(u[3]), 512))
                elif u == "q2":
                    for h in range(W2_HEADS):
                        c = P * (h % PAIRS) + QK * (h // PAIRS)
                        put(k8[:, :, c:c + QK], columns(W2, 512 + QK * h, QK))
                elif u == "kv2":
                    put(dst[:, 0:DT * 2 * P].rearrange("p (k c) -> p k c", k=DT), columns(W2, 1024, 256))
                elif u == "pool2":
                    put(k8, columns(W2, 0, 512))
                elif u.startswith("mix"):
                    w = A["w_out_2"][0][:, 512 * int(u[3]):512 * int(u[3]) + 512]
                    put(k8[:, 0:4, :], w[0:512].rearrange("(k p) c -> p k c", p=P))
                    for a in range(2):
                        rows_ = w[512 + 256 * a:768 + 256 * a].rearrange("(j d) c -> d j c", d=QK)
                        put(k8[a * QK:(a + 1) * QK, 4:8, :], rows_)
                elif u.startswith("up"):
                    put(k8, columns(A["w_ff1_2"][0], 512 * int(u[2:]), 512))
                elif u.startswith("down"):
                    n = int(u[4:])
                    put(dst.rearrange("p (k c) -> p k c", k=4),
                        A["w_ff2_2"][0][512 * n:512 * n + 512].rearrange("(k p) c -> p k c", p=P))
                elif u == "ple":
                    put(dst[:, 0:2 * D].rearrange("p (k c) -> p k c", k=2),
                        A["w_ple_2"][0].rearrange("(k p) c -> p k c", p=P))
                else:
                    put(k8, columns(A["w_ple_gate_2"][0], 512 * int(u[4]), 512))

            def used_up(u):
                if u in last_turn:
                    filled(sp, last_turn[u])
                else:
                    sp.wait_ge(unit_used, int(u[4:]) + 1)

            def load_expert(e, odd):
                for s, w, k in zip(expert_slots(odd), ("w_gate", "w_up", "w_down"), (DT, DT, FT)):
                    src = A[w][0, bass.ds(e, 1)].rearrange("e (k p) c -> p (e k) c", p=P)
                    yield s, ring[:, s, :].rearrange("p (k c) -> p k c", k=k), src

            for n, u in enumerate(UNITS_1):
                if n >= RING:
                    used_up(UNITS_1[n - RING])
                load(u)
            for odd in range(2):
                for k, (s, dst, src) in enumerate(load_expert(odd, odd)):
                    used_up(UNITS_1[len(UNITS_1) - RING + 3 * odd + k])
                    sp.dma_start(dst, src).then_inc(slot_in[s], 16)
            sp.wait_ge(tab_ready, 1)

            def freed(e, k):
                end = sp.value_load(tab[0:1, 0, bass.ds(e + 1, 1)], min_val=1, max_val=BLOCKS_MAX)
                sp.wait_ge((gate_full, up_full, y_full)[k], end * 2 if k == 2 else end)

            with sp.Fori(1, NE // 2) as ii:
                for odd in range(2):
                    for k, (s, dst, src) in enumerate(load_expert(2 * ii + odd, odd)):
                        freed(2 * ii + (odd - 2), k)
                        sp.dma_start(dst, src).then_inc(slot_in[s], 16)
            for n, u in enumerate(UNITS_2):
                if n < RING:
                    freed(NE - 2 + n // 3, n % 3)
                else:
                    used_up(UNITS_2[n - RING])
                load(u)
            res = out[0].rearrange("(t p) c -> p t c", p=P)
            for n in range(2 * TT):
                c, t = divmod(n, TT)
                sp.wait_ge(out_ready, n + 1)
                sp.dma_start(res[:, t, c * 512:(c + 1) * 512], OUT2[:, t, c * 512:(c + 1) * 512]).then_inc(stored, 16)
            sp.wait_ge(stored, 16 * 2 * TT)

        @block.gpsimd
        def _(pool):
            made = [0]

            def const(ins, wait=False):
                ins.then_inc(consts, 1)
                made[0] += 1
                if wait:
                    pool.wait_ge(consts, made[0])

            def select(t, pattern, base, mult, op, fill, wait=False):
                const(pool.affine_select(out=t, in_=t, pattern=pattern, base=base, channel_multiplier=mult,
                                         compare_op=op, fill=fill), wait)

            const(pool.memset(ident[:, :], 0.0))
            const(pool.memset(identb[:, :], 0.0))
            const(pool.memset(maskc[:, :], 0.0))
            const(pool.memset(headsel[:, :, :], 0.0))
            const(pool.memset(maskk[:, :], 0.0))
            const(pool.memset(ones[:, :], 1.0))
            const(pool.memset(half[:, :], -0.5))
            const(pool.memset(unheld[:, :, :], NO_ROW))
            const(pool.memset(idx[:, 1, :], NO_ROW))
            const(pool.memset(tab[:, 0, 0:1], 0))
            const(pool.iota(inv16[:, :], [[1, 16]], base=1, channel_multiplier=0,
                            allow_small_or_imprecise_dtypes=True))
            for k in range(2):
                const(pool.iota(tokid[:, k, :, 0], [[P, TT]], base=0, channel_multiplier=1))
                const(pool.iota(tokid[:, k, :, 1], [[P, TT]], base=k * T, channel_multiplier=1), k == 1)
            select(ident[:, :], [[-1, P]], 0, 1, ALU.not_equal, 1.0)
            select(identb[:, :], [[-1, P]], 0, 1, ALU.not_equal, 1.0)
            select(maskc[:, :], [[-1, P]], 0, 1, ALU.is_ge, NEG)
            select(headsel[:, :, :], [[-1, HEADS], [0, P]], 0, 1, ALU.not_equal, 1.0)
            const(pool.memset(maskk[0:QK, QK:P], NEG))
            assert made[0] == N_CONSTS

            def roots(names, width):
                for nm in names:
                    r = root(*nm)
                    pool.wait_ge(ms_ready, r + 1)
                    pool.tensor_tensor(rsv[:, r, 0:width], msv[:, r, 0:width], half[:, 0:width],
                                       ALU.pow).then_inc(root_done, 1)

            roots([("n1", t) for t in range(TT)], 1)
            roots([(u, t) for u in ("aq", "ak") for t in range(TT)], 8)
            roots([(k, t) for t in range(TT) for k in ("fd", "fm")], HEADS)

            filled(pool, ("O", TT - 1, "m"))
            filled(pool, ("F", TT - 1, "d"))
            pool.memset(XG, 0.0).then_inc(consts2, 1)
            pool.memset(YB, 0.0).then_inc(y_left, 1)
            pool.memset(UPPER, 1.0).then_inc(consts2, 1)
            pool.iota(DISTI, [[-1, 2 * P]], base=P, channel_multiplier=1,
                      allow_small_or_imprecise_dtypes=True).then_inc(consts2, 1)
            pool.iota(IOG, [[0, TT], [1, NG]], base=0, channel_multiplier=0,
                      allow_small_or_imprecise_dtypes=True).then_inc(consts2, 1)
            pool.iota(IO8, [[0, TT], [1, EG]], base=0, channel_multiplier=0,
                      allow_small_or_imprecise_dtypes=True).then_inc(consts2, 1)
            pool.iota(TH, [[0, NE], [BLK, PER_EXPERT_MAX - 1]], base=BLK, channel_multiplier=0,
                      allow_small_or_imprecise_dtypes=True).then_inc(consts2, 1)
            pool.memset(SUM2, 0.0).then_inc(consts2, 1)
            pool.wait_ge(consts2, 7)
            for k in range(-1, 2):
                pool.affine_select(out=SUM2, in_=SUM2, pattern=[[-1, 2 * BLK]], base=k * BLK, channel_multiplier=1,
                                   compare_op=ALU.not_equal, fill=1.0).then_inc(consts2, 1)
                pool.wait_ge(consts2, 9 + k)
            pool.affine_select(out=UPPER, in_=UPPER, pattern=[[1, P]], base=0, channel_multiplier=-1,
                               compare_op=ALU.is_gt, fill=0.0).then_inc(consts2, 1)
            roots([("n2", t) for t in range(TT)], 1)
            for h in range(W2_HEADS):
                pool.tensor_scalar(BM[:, h, :], DISTI, -(2.0 ** -(h + 1)), None, ALU.mult).then_inc(consts2, 1)
            pool.wait_ge(consts2, 11 + W2_HEADS)
            pool.affine_select(out=BM, in_=BM, pattern=[[0, W2_HEADS], [-1, 2 * P]], base=P, channel_multiplier=1,
                               compare_op=ALU.is_ge, fill=NEG).then_inc(consts2, 1)
            pool.wait_ge(consts2, 12 + W2_HEADS)
            pool.affine_select(out=BM, in_=BM, pattern=[[0, W2_HEADS], [1, 2 * P]], base=-1, channel_multiplier=-1,
                               compare_op=ALU.is_ge, fill=NEG).then_inc(consts2, 1)

            pool.wait_ge(table_in, 16)
            pool.wait_ge(dest_ready, 1)
            for k in range(2):
                for t in range(TT):
                    pool.indirect_dma_start(
                        out=slot_tokens, out_offset=bass.IndirectOffsetOnAxis(dest[:, k, t:t + 1], 0),
                        in_=tokid[:, k, t, :], in_offset=None).then_inc(ids_out, 16)
            pool.wait_ge(ids_out, 16 * 2 * TT)
            pool.wait_ge(h_out, 16 * TT)
            pool.wait_ge(tab_ready, 1)

            def pick(k, g):
                pool.tensor_copy(idx[:, k, :], ids[:, bass.ds(g, 1), k]).then_inc(idx_kept[k], 1)

            def gather_rows():
                pool.indirect_dma_start(
                    out=XG, out_offset=None, in_=h_rows,
                    in_offset=bass.IndirectOffsetOnAxis(idx[:, 0, 0:1], 0),
                    bounds_check=T - 1, oob_is_err=False).then_inc(rows_in, 16)

            def scatter_results():
                pool.indirect_dma_start(
                    out=results, out_offset=bass.IndirectOffsetOnAxis(idx[:, 1, 0:1], 0),
                    in_=YB.rearrange("p c n -> p (c n)"), in_offset=None,
                    bounds_check=NO_ROW - 1, oob_is_err=False).then_inc(y_out, 16)

            def move_rows(e, g, odd, last, ahead):
                until(pool, xt_full, g + 1)
                pick(0, g + 1)
                until(pool, idx_kept[0], g + 2)
                gather_rows()
                until(pool, y_left, g * 2 + 1)
                scatter_results()
                until(pool, y_out, g * 16 + 16)
                pick(1, g)
                until(pool, idx_kept[1], g + 1)

            pool.dma_start(ids, slot_tokens.rearrange("(n p) o -> p n o", p=BLK)).then_inc(idx_in, 16)
            pool.wait_ge(idx_in, 16)
            pick(0, 0)
            pool.wait_ge(idx_kept[0], 1)
            gather_rows()
            each_expert(pool, move_rows)
            blocks = pool.value_load(tab[0:1, 0, NE:NE + 1], min_val=0, max_val=BLOCKS_MAX)
            until(pool, y_left, blocks * 2 + 1)
            scatter_results()

            done = [0]

            def step(ins, wait=True):
                ins.then_inc(pool_step, 1)
                done[0] += 1
                if wait:
                    pool.wait_ge(pool_step, done[0])

            for g, w in enumerate(POOL_WINDOWS):
                left(pool, ("u2", g))
                src, k, sh = U2[:, g, :], 0, 1
                while sh < w:
                    dst = PW[:, k, :]
                    step(pool.tensor_copy(dst[:, 0:sh], src[:, 0:sh]), False)
                    step(pool.tensor_tensor(dst[:, sh:T], src[:, sh:T], src[:, 0:T - sh], ALU.add))
                    src, k, sh = dst, 1 - k, 2 * sh
                dst = PW[:, k, :]
                step(pool.tensor_tensor(dst[:, 0:w], src[:, 0:w], inv16[:, 0:w], ALU.mult), False)
                step(pool.tensor_scalar(dst[:, w:T], src[:, w:T], 1.0 / w, None, ALU.mult))
                pool.tensor_tensor(DP[:, g, :], dst, U2[:, g, :], ALU.subtract).then_inc(pool_ready, 1)
                pool.wait_ge(pool_ready, g + 1)
            roots([("l1", t) for t in range(TT)] + [("l2", t) for t in range(TT)], 1)

        @block.scalar
        def _(act):
            xt = A["x"][0].rearrange("(t p) c -> p t c", p=P)

            def small(dst, src, s=small_in):
                act.dma_start(dst, src).then_inc(s, 16)

            def row(name, q):
                return A[name][0].rearrange("(q c) -> q c", q=q)

            for t in range(TT):
                act.dma_start(X[:, t, :], xt[:, t, :]).then_inc(x_in[t], 16)
            small(PROWS[R_N1:R_N1 + 8], row("norm1_w", 8))
            small(PROWS[R_N2:R_N2 + 8], row("norm2_w", 8))
            small(PROWS[R_CB:R_CB + 8], row("conv_b", 8))
            small(PROWS[R_CW:R_CW + 32], A["conv_w"][0].rearrange("w (c p) -> (w c) p", p=P))
            small(PROWS[R_MN:R_MN + 1], A["m_norm_w"])
            small(PROWS[R_AN:R_AN + 1], A["a_norm_w"])
            small(PROWS[R_PS:R_PS + 4], row("pool_scale_2", 4))
            for c in range(2):
                small(PROWS[R_QN:R_QN + 1, c * QK:(c + 1) * QK], A["q_norm_w"])
                small(PROWS[R_KN:R_KN + 1, c * QK:(c + 1) * QK], A["k_norm_w"])
            small(wgates[:, :, :], A["w_in"][0][:, C_GATES:C_GATES + 8].rearrange("(k p) c -> p k c", p=P), wgates_in)
            for k, nm in enumerate(("lambda_q1", "lambda_k1", "lambda_q2", "lambda_k2")):
                small(LAMIN[:, k, :], A[nm])
            small(rg[:, 0:1], A["b_igate"].rearrange("o h -> h o"))
            small(rg[:, 1:2], A["b_fgate"].rearrange("o h -> h o"))
            act.dma_start(sink[:, :], A["attn_sinks_2"].to_broadcast([P, W2_HEADS])).then_inc(sink_in, 16)
            act.wait_ge(consts, N_CONSTS)
            act.dma_start(slot_tokens.rearrange("(p n) o -> p (n o)", p=BLK),
                          unheld[:, :, :].rearrange("p n o -> p (n o)")).then_inc(table_in, 16)

            for t in range(TT):
                act.wait_ge(x_in[t], 16)
                if t >= 2:
                    act.wait_ge(sumsq, t - 1)
                act.activation(JUNK2[:, t % 2, :], X[:, t, :], ACT.Square, accum_out=st[:, t:t + 1]).then_inc(sumsq, 1)
            filled(act, "lam")
            leave(act.activation(lamc[:, 0:2], ps[:, 7, 0:2], ACT.Exp), "lam")

            def silu(c):
                left(act, ("mq", c) if c < 4 else ("mk", c - 4))
                act.activation(QKM[:, c, :], EE[:, c % 2, :], ACT.Silu).then_inc(silu_done, 1)

            silu(0)
            silu(1)
            act.wait_ge(row_dve, 1)
            act.activation(RT, RT, ACT.Exp).then_inc(row_act, 1)
            act.wait_ge(row_act, 1)
            act.activation(RT, RT, ACT.Ln, bias=1.0).then_inc(row_act, 1)
            silu(2)
            act.wait_ge(row_dve, 2)
            act.wait_ge(table_in, 16)
            act.activation(REM, RM, ACT.Exp, scale=-1.0).then_inc(row_act, 1)
            for c in range(3, 8):
                silu(c)
            for t in range(TT):
                leave(act.activation(MO[:, t, :], filled(act, ("mo", t)), ACT.Sigmoid), ("mo", t))
            names = [(u, n) for u in ("aq", "ak", "av", "mv") for n in range(4)]
            filled(act, "gcols")
            for k, nm in enumerate(names):
                p = filled(act, nm)
                if k < 8:
                    if k >= 2:
                        act.wait_ge(ms_ready, root(*names[k - 2]) + 1)
                    act.activation(SQS[k % 2], p, ACT.Square).then_inc(sumsq, 1)
                else:
                    leave(act.activation((AV if nm[0] == "av" else MV)[:, nm[1], :], p, ACT.Copy), nm)
                if 1 <= k <= 8:
                    u, n = names[k - 1]
                    key = ("T", u, n)
                    q = filled(act, key).rearrange("p (h t) -> p h t", h=HEADS)
                    dst, gain = (QA, R_QN) if u == "aq" else (KA, R_KN)
                    leave(act.activation(dst[:, :, n * P:(n + 1) * P], q, ACT.Copy, scale=prm[:, gain:gain + 1]), key)

            def exps(n):
                i, h, kind = ITEMS[n]
                k, W = n // 2, (i + 1) * P
                if kind == "d":
                    act.wait_ge(nmax_ready, k + 1)
                    if k:
                        act.wait_ge(ad_ready, k)
                    for c in range(2):
                        leave(act.activation(EE[:, c, 0:W], filled(act, ("S", n, c))[:, 0:W], ACT.Exp,
                                       bias=st[:, 18 + 8 * (k % 2) + c:19 + 8 * (k % 2) + c], scale=QK ** -0.5,
                                       accum_out=st[:, 20 + 8 * (k % 2) + c:21 + 8 * (k % 2) + c]), ("S", n, c))
                else:
                    p = filled(act, ("S", n, 0))
                    if k:
                        left(act, ("S", n - 2, 1))
                    if k == 0:
                        left(act, "gcols")
                    leave(act.activation(DD[:, 0:W], p[:, 0:W], ACT.Exp, bias=cols[:, 0, i, h:h + 1]), ("S", n, 0))

            def finals(i):
                act.activation(SQD, filled(act, ("O", i, "d")), ACT.Square).then_inc(fin_sq, 1)
                act.wait_ge(fin_in, i + 1)
                act.activation(SQM, NM, ACT.Square).then_inc(fin_sq, 1)

            def final_out(i):
                for kind, dst, gain in (("d", MIXA, R_AN), ("m", HT, R_MN)):
                    key = ("F", i, kind)
                    q = filled(act, key).rearrange("p (h t) -> p h t", h=HEADS)
                    leave(act.activation(dst[:, 0:HEADS, i * P:(i + 1) * P], q, ACT.Copy, scale=prm[:, gain:gain + 1]), key)

            for n in range(len(ITEMS) + 1):
                if n < len(ITEMS):
                    exps(n)
                if n >= 1 and ITEMS[n - 1][2] == "d":
                    key, W = ("AT", n - 1), (ITEMS[n - 1][0] + 1) * P
                    leave(act.activation(ATD[:, 0:W], filled(act, key)[:, 0:W], ACT.Copy), key)
                if n >= 9 and (n - 9) % 8 == 0:
                    finals((n - 9) // 8)
                if n >= FIN_STEP and (n - FIN_STEP) % 8 == 0:
                    final_out((n - FIN_STEP) // 8)
            finals(TT - 1)
            for t in range(TT):
                act.dma_start(X[:, t, :], xt[:, t, :]).then_inc(x_in[t], 16)
            final_out(TT - 1)
            small(WR[:, :, 0:NG], A["w_group"][0].rearrange("(k p) c -> p k c", p=P), router_in)
            small(WR[:, :, NG:NG + NE], A["w_expert"][0].rearrange("(k p) c -> p k c", p=P), router_in)
            small(BR[:, 0:NG], A["b_group"].to_broadcast([P, NG]), router_in)
            small(BR[:, NG:NG + NE], A["b_expert"].to_broadcast([P, NE]), router_in)
            for t in range(TT):
                left(act, ("o", 0, t))
                left(act, ("o", 1, t))
                if t >= 2:
                    act.wait_ge(sumsq, TT + 8 + t - 1)
                act.activation(JUNK3[:, t % 2, :], X[:, t, :], ACT.Square, accum_out=st[:, 4 + t:5 + t]).then_inc(sumsq, 1)
            for t in range(TT):
                act.wait_ge(hn_ready, t + 1)
                act.dma_start(h_rows[t * P:(t + 1) * P, :], HN[:, t, :]).then_inc(h_out, 16)
            act.wait_ge(r_dve, 1)
            act.activation(EXPG, D4, ACT.Exp).then_inc(r_act, 1)
            act.wait_ge(r_dve, 2)
            act.activation(P2, DM, ACT.Exp).then_inc(r_act, 1)

            def weights_hi(e, u, half_, odd):
                s = expert_slots(odd)[u]
                if half_ == 0:
                    act.wait_ge(slot_in[s], raw_loads(e, odd, s))
                c = slice(half_ * UNIT // 2, (half_ + 1) * UNIT // 2)
                act.activation(HI[u][:, c], ring[:, s, c], ACT.Copy).then_inc(w_hi, 1)

            def rows_hi(g):
                act.wait_ge(xt_gained, g + 1)
                act.activation(XTS[:, :, 0, :], XTG, ACT.Copy).then_inc(xt_hi, 1)

            def block_act(e, g, odd, last, ahead):
                def gate_or_up(u):
                    act.wait_ge((gate_full, up_full)[u], g + 1)
                    act.activation(GUS[:, u, :], ps[:, u, :], ACT.Copy).then_inc(gu_out, 1)

                gate_or_up(0)
                if ahead:
                    weights_hi(e + 1, 0, 0, 1 - odd)
                act.wait_ge(sum_full, g * 2 + 1)
                act.activation(SG, ps[:, 2, :].rearrange("p (f b) -> p f b", f=FT)[:, :, 0:BLK],
                               ACT.Silu).then_inc(sg_ready, 1)
                gate_or_up(1)
                act.wait_ge(hid_gated, g + 1)
                act.activation(HIDS[:, 0, :, :], HIDG, ACT.Copy).then_inc(hid_hi, 1)
                rows_hi(g + 1)
                if ahead:
                    weights_hi(e + 1, 0, 1, 1 - odd)
                    weights_hi(e + 1, 1, 0, 1 - odd)
                    weights_hi(e + 1, 1, 1, 1 - odd)
                act.wait_ge(y_out, g * 16 + 16)
                for c in range(2):
                    act.wait_ge(y_full, g * 2 + (c + 1))
                    act.activation(YB[:, c, :], ps[0:BLK, 4 + c, :], ACT.Copy).then_inc(y_left, 1)
                if ahead:
                    for half_ in range(2):
                        weights_hi(e + 1, 2, half_, 1 - odd)

            filled(act, "route")
            act.wait_ge(h_out, 16 * TT)
            for u in range(3):
                if u == 2:
                    act.wait_ge(dest_ready, 1)
                for half_ in range(2):
                    weights_hi(0, u, half_, 0)
            act.wait_ge(tab_ready, 1)
            rows_hi(0)
            act.preload_act_table(ACT.Silu)
            each_expert(act, block_act)

            blocks = act.value_load(tab[0:1, 0, NE:NE + 1], min_val=0, max_val=BLOCKS_MAX)
            act.wait_ge(y_out, blocks * 16 + 16)
            for t in range(TT):
                for k in range(2):
                    act.dma_start(YG[:, k, t, :], results[k * T + t * P:k * T + (t + 1) * P, :]).then_inc(yg_in[t], 16)

            for t in range(TT):
                leave(act.activation(HT[:, 0:4, t * P:(t + 1) * P],
                                     filled(act, ("x3", t, 0)).rearrange("p (k t) -> p k t", k=4), ACT.Copy), ("x3", t, 0))
            act.dma_start(WP2, A["w_pool_2"][0].rearrange("g c d -> c g d")).then_inc(wp_in, 16)
            for n in range(PAIRS):
                leave(act.activation(Q2[:, n, :], filled(act, ("q2", n)), ACT.Copy), ("q2", n))
            leave(act.activation(K2, filled(act, "k2"), ACT.Copy), "k2")
            leave(act.activation(V2, filled(act, "v2").rearrange("p (t d) -> p t d", t=TT), ACT.Copy), "v2")
            for n in range(4):
                leave(act.activation(U2[:, n, :], filled(act, ("u2", n)), ACT.Copy), ("u2", n))

            def pt_out(n):
                lo = 1 if n < PAIRS else 0
                dst, src = (v.rearrange("p (a b q) -> p a b q", a=2, b=2)[:, :, lo:2, :]
                            for v in (PT2[:, n % 2, :], filled(act, ("PT", n))))
                leave(act.activation(dst, src, ACT.Copy), ("PT", n))

            for n in range(18):
                if n < 16:
                    lo = P if n < PAIRS else 0
                    b = 32 + 8 * (n % 2)
                    act.wait_ge(nmax2, n + 1)
                    for a in range(2):
                        act.activation(SC2[:, n % 2, a, lo:], SC2[:, n % 2, a, lo:], ACT.Exp,
                                       bias=st[:, b + 2 + a:b + 3 + a], accum_out=st[:, b + 4 + a:b + 5 + a]).then_inc(exp2, 1)
                    act.activation(st[:, b + 6:b + 8], st[:, b + 6:b + 8], ACT.Exp).then_inc(exp2, 1)
                if 1 <= n <= 16:
                    pt_out(n - 1)
                if n >= 5 and (n - 5) % 4 == 0:
                    i = (n - 5) // 4
                    leave(act.activation(MIX2[:, 4:8, i * P:(i + 1) * P],
                                         filled(act, ("O2", i)).rearrange("p (j q) -> p j q", j=PAIRS), ACT.Copy), ("O2", i))
            act.dma_start(LNB1, A["ln1_b_2"].to_broadcast([P, D])).then_inc(ln_in, 16)
            for g in range(4):
                leave(act.activation(MIX2[:, g, :], filled(act, ("pw", g)), ACT.Copy, scale=prm[:, R_PS + g:R_PS + g + 1]), ("pw", g))
            act.dma_start(LNG1, A["ln1_g_2"].to_broadcast([P, D])).then_inc(ln_in, 16)
            for t in range(TT):
                for c in range(2):
                    key = ("h1", t, c)
                    leave(act.activation(HT[:, 4 * c:4 * c + 4, t * P:(t + 1) * P],
                                         filled(act, key).rearrange("p (k t) -> p k t", k=4), ACT.Copy), key)
            for f in range(FFT):
                leave(act.activation(AT[:, f, :], filled(act, ("up", f)), ACT.Relu), ("up", f))
            for dst, nm in ((LNG2, "ln2_g_2"), (LNB2, "ln2_b_2"), (BG, "b_ple_gate_2")):
                act.dma_start(dst, A[nm].to_broadcast([P, D])).then_inc(late_in, 16)
            act.dma_start(PIN, A["p_2"][0, 0].rearrange("(t p) c -> p t c", p=P)).then_inc(late_in, 16)
            for t in range(TT):
                leave(act.activation(PET[:, :, t * P:(t + 1) * P],
                                     filled(act, ("pt", t))[:, 0:2 * P].rearrange("p (k t) -> p k t", k=2), ACT.Copy), ("pt", t))
            for t in range(TT):
                for c in range(2):
                    key = ("h5", t, c)
                    leave(act.activation(H5T[:, 4 * c:4 * c + 4, t * P:(t + 1) * P],
                                         filled(act, key).rearrange("p (k t) -> p k t", k=4), ACT.Copy), key)
            for n in range(2 * TT):
                left(act, ("gt", n))
                act.activation(GT[:, n % 2, :], GT[:, n % 2, :], ACT.Sigmoid).then_inc(gate_act, 1)

        @block.vector
        def _(vec):
            steps = [0]

            def step(ins):
                ins.then_inc(dve_step, 1)
                steps[0] += 1
                vec.wait_ge(dve_step, steps[0])

            def mean_square(r, src, n, width=1, eps=EPS):
                vec.tensor_scalar(msv[:, r, 0:width], src, 1.0 / n, eps, ALU.mult, ALU.add).then_inc(ms_ready, 1)

            def rooted(r):
                vec.wait_ge(root_done, r + 1)
                return rsv[:, r, :]

            vec.wait_ge(consts, N_CONSTS)
            step(vec.reciprocal(inv16[:, :], inv16[:, :]))

            def ms1(t):
                vec.wait_ge(sumsq, t + 1)
                mean_square(t, st[:, t:t + 1], D)

            ms1(0)
            for t in range(TT):
                if t + 1 < TT:
                    ms1(t + 1)
                vec.tensor_scalar(X[:, t, :], X[:, t, :], rooted(t)[:, 0:1], None, ALU.mult).then_inc(xn_ready, 1)
            vec.wait_ge(small_in, 16 * N_SMALL)
            leave(vec.tensor_copy(prm[:, :], filled(vec, "prm")[:, 0:N_PARAMS]), "prm")
            left(vec, "prm")
            step(vec.tensor_scalar(prm[:, R_AN:R_AN + 1], prm[:, R_AN:R_AN + 1], 1.0 - LAMBDA_INIT, None, ALU.mult))

            def gained(key, t, c, first):
                w = prm[:, first + 4 * c:first + 4 * c + 4].unsqueeze(2).to_broadcast([P, 4, P])
                leave(vec.tensor_tensor(HT[:, 4 * c:4 * c + 4, t * P:(t + 1) * P],
                                        filled(vec, key).rearrange("p (k t) -> p k t", k=4), w, ALU.mult), key)

            for t in range(TT):
                for c in range(2):
                    gained(("h", t, c), t, c, R_N1)
            for k in range(2):
                step(vec.tensor_tensor_reduce(LAMP[:, 2:2 + QK], LAMIN[:, 2 * k, :], LAMIN[:, 2 * k + 1, :], 1.0, 0.0,
                                              ALU.mult, ALU.add, LAMP[:, k:k + 1]))
            vec.tensor_copy(LAMP[:, 66:67], LAMP[:, 0:1]).then_inc(lam_prod, 1)
            leave(vec.tensor_copy(GTOK, filled(vec, "gates")[:, 0:TT * 8].rearrange("p (t g) -> p t g", t=TT)), "gates")
            left(vec, "lam")
            step(vec.tensor_tensor(lamc[:, 3:4], lamc[:, 1:2], lamc[:, 0:1], ALU.subtract))
            step(vec.tensor_scalar(lamc[:, 2:3], lamc[:, 3:4], -LAMBDA_INIT, None, ALU.add))

            def conv(c):
                key = ("mq", c) if c < 4 else ("mk", c - 4)
                p, e = filled(vec, key), EE[:, c % 2, :]
                if c >= 2:
                    vec.wait_ge(silu_done, c - 1)
                w = [prm[:, R_CW + 8 * j + c:R_CW + 8 * j + c + 1] for j in range(4)]
                step(vec.tensor_scalar(e, p, w[3], prm[:, R_CB + c:R_CB + c + 1], ALU.mult, ALU.add))
                for s in (1, 2, 3):
                    ins = vec.scalar_tensor_tensor(out=e[:, s:T], in0=p[:, 0:T - s], scalar=w[3 - s], in1=e[:, s:T],
                                                   op0=ALU.mult, op1=ALU.add)
                    step(ins) if s < 3 else leave(ins, key)

            conv(0)
            conv(1)
            leave(vec.tensor_scalar(RI, filled(vec, ("grow", 0))[0:HEADS], rg[:, 0:1], None, ALU.add), ("grow", 0))
            leave(vec.tensor_scalar(RF, filled(vec, ("grow", 1))[0:HEADS], rg[:, 1:2], None, ALU.add), ("grow", 1))
            left(vec, ("grow", 1))
            vec.scalar_tensor_tensor(out=RT, in0=RF, scalar=-1.0, in1=RF, op0=ALU.mult, op1=ALU.min).then_inc(row_dve, 1)
            conv(2)
            vec.wait_ge(row_act, 2)
            step(vec.scalar_tensor_tensor(out=RF, in0=RF, scalar=0.0, in1=RT, op0=ALU.min, op1=ALU.subtract))
            for j in range(TT):
                s = slice(j * P, (j + 1) * P)
                step(vec.tensor_tensor_scan(RB[:, s], ones[0:HEADS, :], RF[:, s], 0.0, ALU.mult, ALU.add))
            step(vec.tensor_copy(rg[:, 8:8 + TT], RB[:, P - 1:T:P]))
            step(vec.tensor_tensor(wrow[:, :], RI, RB, ALU.subtract))
            step(vec.memset(rg[:, 2:6], 0.0))
            for i in range(TT):
                s = slice(i * P, (i + 1) * P)
                if i:
                    e = rg[:, 7 + i:8 + i]
                    step(vec.tensor_reduce(rg[:, 4:5], wrow[:, (i - 1) * P:i * P], AX, ALU.max))
                    if i > 1:
                        step(vec.tensor_tensor(rg[:, 4:5], rg[:, 4:5], rg[:, 3:4], ALU.max))
                    step(vec.tensor_tensor(rg[:, 3:4], rg[:, 4:5], e, ALU.add))
                    step(vec.tensor_tensor(rg[:, 2:3], rg[:, 2:3], e, ALU.add))
                    step(vec.tensor_tensor(rg[:, 5:6], rg[:, 2:3], rg[:, 3:4], ALU.max))
                step(vec.tensor_tensor_scan(RR[:, s], wrow[:, s], wrow[:, s], rg[:, 5:6], ALU.max, ALU.max))
            vec.tensor_tensor(RM, RB, RR, ALU.add).then_inc(row_dve, 1)
            conv(3)
            vec.wait_ge(row_act, 3)
            vec.wait_ge(row_dve, 2)
            vec.tensor_scalar(RR, RR, -1.0, None, ALU.mult).then_inc(rows_done, 1)
            for c in range(4, 8):
                conv(c)
            leave(vec.tensor_copy(cols[:, :, :, :].rearrange("p a t h -> p (a t h)"), filled(vec, "gcols")[:, 0:2 * TT * HEADS]), "gcols")

            names = [(u, n) for u in ("aq", "ak") for n in range(4)]
            for k, nm in enumerate(names):
                vec.wait_ge(sumsq, TT + k + 1)
                p = filled(vec, nm).rearrange("p (g d) -> p g d", g=8)
                step(vec.tensor_reduce(st[:, 8:16], SQS[k % 2].rearrange("p (g d) -> p g d", g=8), AX, ALU.add))
                mean_square(root(*nm), st[:, 8:16], QK, 8)
                if k >= 2:
                    filled(vec, ("T",) + names[k - 2])
                r = rooted(root(*nm)).unsqueeze(2).to_broadcast([P, 8, QK])
                dst = (ND, NM)[k % 2].rearrange("p (g d) -> p g d", g=8)
                leave(vec.tensor_tensor(dst, p, r, ALU.mult), nm)

            def maximum(n):
                i, h, _ = ITEMS[n]
                k, W = n // 2, (i + 1) * P
                b = 16 + 8 * (k % 2)
                if h == 0 and i:
                    filled(vec, ("S", n - 1, 0))
                    vec.tensor_scalar(wrow[:, 0:i * P], wrow[:, 0:i * P], rg[:, 7 + i:8 + i], None, ALU.add).then_inc(w_ready, 1)
                filled(vec, ("S", n, 0))
                filled(vec, ("S", n, 1))
                step(vec.tensor_reduce(st[:, b:b + 2], ps[:, 2:4, 0:W], AX, ALU.max))
                vec.tensor_scalar(st[:, b + 2:b + 4], st[:, b:b + 2], -QK ** -0.5, None, ALU.mult).then_inc(nmax_ready, 1)

            def decayed(n):
                i, h, _ = ITEMS[n]
                W = (i + 1) * P
                left(vec, ("S", n, 0))
                if n >= 2:
                    filled(vec, ("AT", n - 2))
                d = 64 + 4 * (i % 2) + h
                leave(vec.tensor_tensor_reduce(AM[:, 0:W], filled(vec, ("S", n, 1))[:, 0:W], DD[:, 0:W], HD ** -0.5, 0.0,
                                               ALU.mult, ALU.add, st[:, d:d + 1]), ("S", n, 1))

            def mixed(n):
                i, h, _ = ITEMS[n]
                k, W = n // 2, (i + 1) * P
                b = 16 + 8 * (k % 2)
                for c in range(2):
                    left(vec, ("S", n, c))
                step(vec.reciprocal(st[:, b + 6:b + 8], st[:, b + 4:b + 6]))
                vec.tensor_scalar(EE[:, 0, 0:W], EE[:, 0, 0:W], st[:, b + 6:b + 7], None, ALU.mult).then_inc(dve_step, 1)
                steps[0] += 1
                step(vec.tensor_tensor(st[:, 81:82], st[:, b + 7:b + 8], lamc[:, 2:3], ALU.mult))
                if n >= 2:
                    filled(vec, ("AT", n - 2))
                vec.scalar_tensor_tensor(out=AD[:, 0:W], in0=EE[:, 1, 0:W], scalar=st[:, 81:82], in1=EE[:, 0, 0:W],
                                         op0=ALU.mult, op1=ALU.add).then_inc(ad_ready, 1)

            def at_out(n):
                key, W = ("AT", n), (ITEMS[n][0] + 1) * P
                leave(vec.tensor_copy(ATM[:, 0:W], filled(vec, key)[:, 0:W]), key)

            def heads_of(v):
                return v.rearrange("p (h d) -> p h d", h=HEADS)

            def final(i):
                d = 64 + 4 * (i % 2)
                step(vec.scalar_tensor_tensor(out=st[:, 72:76], in0=st[:, d:d + 4], scalar=-1.0, in1=st[:, d:d + 4],
                                              op0=ALU.mult, op1=ALU.max))
                step(vec.tensor_tensor(st[:, 72:76], st[:, 72:76], cols[:, 1, i, :], ALU.max))
                step(vec.reciprocal(st[:, 76:80], st[:, 72:76]))
                r = st[:, 76:80].unsqueeze(2).to_broadcast([P, HEADS, HD])
                p = filled(vec, ("O", i, "m"))
                if i:
                    filled(vec, ("F", i - 1, "m"))
                leave(vec.tensor_tensor(heads_of(NM), heads_of(p), r, ALU.mult), ("O", i, "m"))
                left(vec, ("O", i, "m"))
                left(vec, ("mo", i))
                vec.tensor_tensor(NM, NM, MO[:, i, :], ALU.mult).then_inc(fin_in, 1)
                for k, (kind, sq, dst) in enumerate((("d", SQD, ND), ("m", SQM, NM))):
                    r = root("f" + kind, i)
                    vec.wait_ge(fin_sq, 2 * i + k + 1)
                    step(vec.tensor_reduce(st[:, 84:88], heads_of(sq), AX, ALU.add))
                    mean_square(r, st[:, 84:88], HD, HEADS)
                    v = rooted(r)[:, 0:HEADS].unsqueeze(2).to_broadcast([P, HEADS, HD])
                    if kind == "d":
                        if i:
                            filled(vec, ("F", i - 1, "d"))
                        leave(vec.tensor_tensor(heads_of(ND), heads_of(filled(vec, ("O", i, "d"))), v, ALU.mult), ("O", i, "d"))
                    else:
                        vec.tensor_tensor(heads_of(NM), heads_of(NM), v, ALU.mult).then_inc(fin_ready, 1)

            for q in range(len(ITEMS) // 2):
                maximum(2 * q)
                if q:
                    at_out(2 * q - 1)
                decayed(2 * q + 1)
                mixed(2 * q)
                if q >= 4 and q % 4 == 0:
                    final(q // 4 - 1)
            at_out(len(ITEMS) - 1)
            final(TT - 1)

            for c in range(2):
                for t in range(TT):
                    vec.wait_ge(x_in[t], 32)
                    s = slice(c * 512, (c + 1) * 512)
                    leave(vec.tensor_tensor(X[:, t, s], X[:, t, s], filled(vec, ("o", c, t)), ALU.add), ("o", c, t))

            def ms2(t):
                vec.wait_ge(sumsq, TT + 8 + t + 1)
                mean_square(root("n2", t), st[:, 4 + t:5 + t], D)

            ms2(0)
            for t in range(TT):
                if t + 1 < TT:
                    ms2(t + 1)
                vec.tensor_scalar(HN[:, t, :], X[:, t, :], rooted(root("n2", t))[:, 0:1], None, ALU.mult).then_inc(hn_ready, 1)
            for t in range(TT):
                for c in range(2):
                    gained(("h2", t, c), t, c, R_N2)

            def over(v, *shape):
                return v.to_broadcast([P] + list(shape))

            E = NG + NE
            vec.wait_ge(router_in, 64)
            leave(vec.tensor_tensor(LG, filled(vec, "route")[:, 0:TT * E].rearrange("p (t e) -> p t e", t=TT),
                                    over(BR.unsqueeze(1), TT, E), ALU.add), "route")
            left(vec, "route")
            vec.wait_ge(consts2, 11)
            step(vec.tensor_reduce(RS[:, 0, :], LG[:, :, 0:NG], AX, ALU.max))
            vec.tensor_tensor(D4, LG[:, :, 0:NG], over(RS[:, 0, :].unsqueeze(2), TT, NG), ALU.subtract).then_inc(r_dve, 1)

            def first_of(dst, hit, iota, n):
                step(vec.scalar_tensor_tensor(out=C8[:, :, 0:n], in0=hit, scalar=-100.0, in1=iota, op0=ALU.mult, op1=ALU.add))
                step(vec.tensor_reduce(RS[:, 1, :], C8[:, :, 0:n], AX, ALU.min))
                step(vec.tensor_tensor(dst, C8[:, :, 0:n], over(RS[:, 1, :].unsqueeze(2), TT, n), ALU.is_equal))

            vec.wait_ge(r_dve, 1)
            step(vec.tensor_scalar(H8[:, :, 0:NG], D4, 0.0, None, ALU.is_equal))
            first_of(OHG, H8[:, :, 0:NG], IOG4, NG)
            le = LG[:, :, NG:E].rearrange("p t (g j) -> p t g j", g=NG)
            step(vec.tensor_tensor(T32, le, over(OHG.unsqueeze(3), TT, NG, EG), ALU.mult))
            step(vec.tensor_reduce(E8, T32.rearrange("p t g j -> p t j g"), AX, ALU.add))
            for k, oh in enumerate((OH1, OH2)):
                step(vec.tensor_reduce(RS[:, 2 + k, :], E8, AX, ALU.max))
                step(vec.tensor_tensor(H8, E8, over(RS[:, 2 + k, :].unsqueeze(2), TT, EG), ALU.is_equal))
                first_of(oh, H8, IO88, EG)
                if k == 0:
                    step(vec.scalar_tensor_tensor(out=E8, in0=oh, scalar=NEG, in1=E8, op0=ALU.mult, op1=ALU.add))
            for o, oh in ((O1, OH1), (O2, OH2)):
                step(vec.tensor_tensor(o, over(OHG.unsqueeze(3), TT, NG, EG), over(oh.unsqueeze(2), TT, NG, EG), ALU.mult))
            O1F, O2F = (o.rearrange("p t g j -> p t (g j)") for o in (O1, O2))
            vec.tensor_tensor(OHS, O1F, O2F, ALU.add).then_inc(oh_ready, 1)
            vec.tensor_tensor(DM, RS[:, 3, :], RS[:, 2, :], ALU.subtract).then_inc(r_dve, 1)
            vec.wait_ge(r_act, 2)
            step(vec.tensor_reduce(RS[:, 4, :], EXPG, AX, ALU.add))
            step(vec.scalar_tensor_tensor(out=RS[:, 5, :], in0=P2, scalar=1.0, in1=RS[:, 4, :], op0=ALU.add, op1=ALU.mult))
            step(vec.reciprocal(wts[:, 0, :], RS[:, 5, :]))
            step(vec.tensor_tensor(wts[:, 1, :], wts[:, 0, :], P2, ALU.mult))
            leave(vec.tensor_copy(RANK, filled(vec, "rank")[:, 0:(TT + 1) * NE].rearrange("p (t e) -> p t e", e=NE)), "rank")
            left(vec, "rank")
            th = TH.rearrange("p (e q) -> p e q", e=NE)
            q7 = PER_EXPERT_MAX - 1
            step(vec.tensor_tensor(th, over(RANK[:, TT, :].unsqueeze(2), NE, q7), th, ALU.is_gt))
            step(vec.tensor_reduce(NB, th, AX, ALU.add))
            step(vec.tensor_copy(tab[:, 1, 0:NE], NB[0:1]))
            step(vec.tensor_scalar(NB, NB, 1.0, None, ALU.add))
            step(vec.tensor_tensor_scan(BEF, ones[:, 0:NE], NB, 0.0, ALU.mult, ALU.add))
            vec.tensor_copy(tab[:, 0, 1:NE + 1], BEF[0:1]).then_inc(tab_ready, 1)
            vec.wait_ge(tab_ready, 1)
            step(vec.tensor_tensor(BEF, BEF, NB, ALU.subtract))
            step(vec.tensor_scalar(NB, BEF, float(BLK), None, ALU.mult))
            step(vec.tensor_tensor(RANK[:, 0:TT, :], RANK[:, 0:TT, :], over(NB.unsqueeze(1), TT, NE), ALU.add))
            for k, o in enumerate((O1F, O2F)):
                step(vec.tensor_tensor(o, o, RANK[:, 0:TT, :], ALU.mult))
                step(vec.tensor_reduce(RS[:, 6 + k, :], o, AX, ALU.add))
            vec.tensor_copy(dest[:, :, :], RS[:, 6:8, :]).then_inc(dest_ready, 1)

            gain = prm[:, R_N2:R_N2 + DT].rearrange("p (a k) -> p a k", a=2).unsqueeze(3).to_broadcast([P, 2, 4, BLK])

            def weights_lo(e, u, odd, half_):
                s = expert_slots(odd)[u]
                c = slice(half_ * UNIT // 2, (half_ + 1) * UNIT // 2)
                vec.wait_ge(w_hi, e * 6 + (2 * u + half_ + 1))
                vec.tensor_tensor(ring_r[s][:, c], ring[:, s, c], HI[u][:, c].bitcast(F32),
                                  ALU.subtract).then_inc(w_lo, 1)

            def rows_gained(g):
                vec.wait_ge(xt_full, g + 1)
                turned = ps[:, 6:8, :].rearrange("p a (k b) -> p a k b", k=4)[:, :, :, 0:BLK]
                vec.tensor_tensor(XTG.rearrange("p (a k) b -> p a k b", a=2), turned, gain,
                                  ALU.mult).then_inc(xt_gained, 1)

            def rows_lo(g):
                vec.wait_ge(xt_hi, g + 1)
                vec.tensor_tensor(XTS[:, :, 1, :], XTG, XTS[:, :, 0, :].bitcast(F32), ALU.subtract).then_inc(xt_lo, 1)

            def block_vec(e, g, odd, last, ahead):
                vec.wait_ge(sg_ready, g + 1)
                vec.wait_ge(sum_full, g * 2 + 2)
                vec.tensor_tensor(HIDG, SG, ps[:, 3, :].rearrange("p (f b) -> p f b", f=FT)[:, :, 0:BLK],
                                  ALU.mult).then_inc(hid_gated, 1)
                vec.wait_ge(hid_hi, g + 1)
                vec.tensor_tensor(HIDS[:, 1, :, :], HIDG, HIDS[:, 0, :, :].bitcast(F32), ALU.subtract).then_inc(hid_ready, 1)
                rows_gained(g + 1)
                rows_lo(g + 1)
                if ahead:
                    for u in range(2):
                        for half_ in range(2):
                            weights_lo(e + 1, u, 1 - odd, half_)

            def down_lo(e, odd):
                for half_ in range(2):
                    weights_lo(e, 2, odd, half_)

            for u in range(2):
                for half_ in range(2):
                    weights_lo(0, u, 0, half_)
            vec.wait_ge(consts2, N_CONSTS2)
            rows_gained(0)
            rows_lo(0)
            each_expert(vec, block_vec, down_lo)

            for t in range(TT):
                vec.wait_ge(yg_in[t], 32)
                step(vec.scalar_tensor_tensor(out=X[:, t, :], in0=YG[:, 0, t, :], scalar=wts[:, 0, t:t + 1], in1=X[:, t, :],
                                              op0=ALU.mult, op1=ALU.add))
                vec.scalar_tensor_tensor(out=X[:, t, :], in0=YG[:, 1, t, :], scalar=wts[:, 1, t:t + 1], in1=X[:, t, :],
                                         op0=ALU.mult, op1=ALU.add).then_inc(x3_ready, 1)

            for t in range(TT):
                leave(vec.tensor_copy(HT[:, 4:8, t * P:(t + 1) * P],
                                      filled(vec, ("x3", t, 1)).rearrange("p (k t) -> p k t", k=4)), ("x3", t, 1))
            vec.wait_ge(sink_in, 16)
            vec.wait_ge(consts2, N_CONSTS2)

            def biased(n):
                i, j = divmod(n, PAIRS)
                lo, b = (P if i == 0 else 0), 32 + 8 * (n % 2)
                if n >= 2:
                    filled(vec, ("PT", n - 2))
                for a in range(2):
                    leave(vec.scalar_tensor_tensor(out=SC2[:, n % 2, a, lo:], in0=filled(vec, ("S2", n, a))[:, lo:2 * P],
                                                   scalar=QK ** -0.5, in1=BM[:, j + PAIRS * a, lo:], op0=ALU.mult, op1=ALU.add),
                          ("S2", n, a))
                left(vec, ("S2", n, 0))
                left(vec, ("S2", n, 1))
                snk = sink[:, j:j + PAIRS + 1:PAIRS]
                step(vec.tensor_reduce(st[:, b:b + 2], SC2[:, n % 2, :, lo:], AX, ALU.max))
                step(vec.tensor_tensor(st[:, b:b + 2], st[:, b:b + 2], snk, ALU.max))
                step(vec.tensor_scalar(st[:, b + 2:b + 4], st[:, b:b + 2], -1.0, None, ALU.mult))
                vec.tensor_tensor(st[:, b + 6:b + 8], snk, st[:, b:b + 2], ALU.subtract).then_inc(nmax2, 1)

            def probabilities(n):
                lo, b = (P if n < PAIRS else 0), 32 + 8 * (n % 2)
                vec.wait_ge(exp2, 3 * n + 3)
                step(vec.tensor_tensor(st[:, b + 4:b + 6], st[:, b + 4:b + 6], st[:, b + 6:b + 8], ALU.add))
                step(vec.reciprocal(st[:, b + 4:b + 6], st[:, b + 4:b + 6]))
                for a in range(2):
                    vec.tensor_scalar(SC2[:, n % 2, a, lo:], SC2[:, n % 2, a, lo:], st[:, b + 4 + a:b + 5 + a], None,
                                      ALU.mult).then_inc(pr2_ready, 1)

            for n in range(17):
                if n < 16:
                    biased(n)
                if n:
                    probabilities(n - 1)

            def residual(c, t, key):
                s = slice(c * 512, (c + 1) * 512)
                leave(vec.scalar_tensor_tensor(out=X[:, t, s], in0=X[:, t, s], scalar=ALPHA, in1=filled(vec, key),
                                               op0=ALU.mult, op1=ALU.add), key)

            def ln_stats(name, t, key):
                b = 48 + 2 * t
                left(vec, (key, 0, t) if key == "o2" else (key, t, 0))
                left(vec, (key, 1, t) if key == "o2" else (key, t, 1))
                for c in range(2):
                    step(vec.bn_stats(bn[:, c, :], X[:, t, c * 512:(c + 1) * 512]))
                step(vec.bn_aggr(st[:, b:b + 2], bn[:, :, :].rearrange("p a b -> p (a b)")))
                mean_square(root(name, t), st[:, b + 1:b + 2], 1, 1, LN_EPS)

            def ln_apply(name, t, g, b_):
                b = 48 + 2 * t
                step(vec.tensor_scalar(X[:, t, :], X[:, t, :], st[:, b:b + 1], rooted(root(name, t))[:, 0:1],
                                       ALU.subtract, ALU.mult))
                step(vec.tensor_tensor(X[:, t, :], X[:, t, :], g, ALU.mult))
                vec.tensor_tensor(X[:, t, :], X[:, t, :], b_, ALU.add).then_inc(ln_ready, 1)

            for c in range(2):
                for t in range(TT):
                    residual(c, t, ("o2", c, t))
                    if c == 1:
                        ln_stats("l1", t, "o2")
            vec.wait_ge(ln_in, 32)
            for t in range(TT):
                ln_apply("l1", t, LNG1, LNB1)
            for f in range(FFT):
                left(vec, ("up", f))
                vec.tensor_tensor(AT[:, f, :], AT[:, f, :], AT[:, f, :], ALU.mult).then_inc(at_ready, 1)
            vec.wait_ge(late_in, 64)
            for t in range(TT):
                for c in range(2):
                    residual(c, t, ("dn", t, c))
                ln_stats("l2", t, "dn")
                ln_apply("l2", t, LNG2, LNB2)

            def gate_in_(n):
                c, t = divmod(n, TT)
                if n >= 2:
                    vec.wait_ge(out_ready, n - 1)
                leave(vec.tensor_tensor(GT[:, n % 2, :], filled(vec, ("gt", n)), BG[:, c * 512:(c + 1) * 512], ALU.add), ("gt", n))

            gate_in_(0)
            for n in range(2 * TT):
                c, t = divmod(n, TT)
                s = slice(c * 512, (c + 1) * 512)
                if n + 1 < 2 * TT:
                    gate_in_(n + 1)
                vec.wait_ge(gate_act, n + 1)
                leave(vec.tensor_tensor(GT[:, n % 2, :], GT[:, n % 2, :], filled(vec, ("pl", n)), ALU.mult), ("pl", n))
                left(vec, ("pl", n))
                vec.tensor_tensor(OUT2[:, t, s], GT[:, n % 2, :], X[:, t, s], ALU.add).then_inc(out_ready, 1)


_OUT = (1, T, D)


def kernel(**inputs):
    from concourse import bacc
    from concourse.bass_utils import run_bass_kernel_spmd

    nc = bacc.Bacc("TRN2", target_bir_lowering=False, num_devices=1)
    arrays, args = {}, {}
    for name, value in inputs.items():
        a = np.ascontiguousarray(value)
        arrays[f"in_{name}"] = a
        args[name] = nc.dram_tensor(f"in_{name}", a.shape, mybir.dt.from_np(a.dtype), kind="ExternalInput").ap()
    out = nc.dram_tensor("result", _OUT, F32, kind="ExternalOutput").ap()
    build(nc, args, out)
    r = run_bass_kernel_spmd(nc, [arrays], core_ids=[0])
    return r.results[0]["result"]
```

```python
from contextlib import ExitStack

import numpy as np

import concourse.bass as bass
from concourse import mybir

F32 = mybir.dt.float32
BF16 = mybir.dt.bfloat16
F32R = mybir.dt.float32r
I32 = mybir.dt.int32
ALU = mybir.AluOpType
ACT = mybir.ActivationFunctionType
AX = mybir.AxisListType.X

P = 128
T = 512
D = 1024
TT = T // P
DT = D // P
RING = 6
UNIT = 4096
NEG = -1e30
EPS = 1e-6
LN_EPS = 1e-5
HEADS = 4
HD = 128
QK = 64
LAMBDA_INIT = 0.8 - 0.6
NE = 32
NG = 4
EG = NE // NG
FT = 4
BLK = 64
PER_EXPERT_MAX = -(-T // BLK)
BLOCKS_MAX = 2 * T // BLK + NE
BLOCKS_HELD = BLOCKS_MAX + PER_EXPERT_MAX + 1
SLOTS = BLOCKS_HELD * BLK
NO_ROW = 2 * T
W2_HEADS = 8
PAIRS = W2_HEADS // 2
WINDOW = 128
POOL_STEP = 3
FFT = 4 * D // P
POOL_WINDOWS = (2, 4, 8, 16)
ALPHA = 2.0 ** 0.25

C_MQ, C_MK, C_MV, C_MO, C_GATES, C_AQ, C_AK, C_AV = 0, 512, 1024, 1536, 2048, 2056, 2568, 3080
R_N1, R_N2, R_CB, R_CW, R_MN, R_AN, R_PS, R_QN, R_KN = 0, 8, 16, 24, 56, 57, 58, 62, 63
N_PARAMS = 64
N_CONSTS2 = 22
N_SMALL = 17
N_CONSTS = 20

UNITS_1 = ["mq", "mk", "mo", "aq", "ak", "av", "mv", "out0", "out1"]
FF_UNITS = [f"{u}{4 * h + n}" for h in range(2) for u in ("up", "down") for n in range(4)]
SPLIT_2 = FF_UNITS + ["gate0", "gate1"]
UNITS_2 = ["q2", "kv2", "pool2", "mix0", "mix1"] + FF_UNITS + ["gate0", "gate1", "ple"]
DMAS_OF = {"q2": 8, "mix0": 3, "mix1": 3}
SECOND = len(UNITS_1) + 3 * NE

RAW_SLOTS = (2, 3, 4)
HI_SLOTS = (0, 1)
X_SLOT = 5
SPLIT_1 = UNITS_1[:7]

ROOTS = ([("n1", t) for t in range(TT)] + [("aq", t) for t in range(TT)]
         + [("ak", t) for t in range(TT)]
         + [(k, t) for t in range(TT) for k in ("fd", "fm")] + [("n2", t) for t in range(TT)]
         + [("l1", t) for t in range(TT)] + [("l2", t) for t in range(TT)])

ITEMS = [(i, h, kind) for i in range(TT) for h in range(HEADS) for kind in "dm"]
FIN_STEP = 13
BANKS = {"d": (2, 3, 6, 7), "m": (4, 5, 1, 0)}


def build(nc, A, out):
    ctx = ExitStack()

    def sb(name, shape, dt=F32):
        return ctx.enter_context(nc.sbuf_tensor(name, shape, dt))

    def sem(name):
        return ctx.enter_context(nc.semaphore(name))

    with ctx:
        base = -(-nc.sbuf_base // 32) * 32
        ring = sb("ring", [P, RING, UNIT])
        X = sb("X", [P, TT, D])
        HT = sb("HT", [P, DT, T])
        M = sb("M", [P, 17920])
        def as_r(name, a, *shape):
            return nc.alloc_sbuf_tensor_at(name, [P] + list(shape), F32R, offset=base + 4 * a)

        HT_AT = RING * UNIT + TT * D
        M_AT = HT_AT + DT * T
        ring_r = [as_r(f"ring_r{s}", s * UNIT, UNIT) for s in range(RING)]
        ident = sb("ident", [P, P])
        identb = sb("identb", [P, P], BF16)
        maskc = sb("maskc", [P, P], BF16)
        maskk = sb("maskk", [P, P], BF16)
        ones = sb("ones", [P, P])
        headsel = sb("headsel", [HEADS, HEADS, P])
        wrow = sb("wrow", [HEADS, T])
        prm = sb("prm", [P, N_PARAMS])
        wgates = sb("wgates", [P, DT, 8])
        msv = sb("msv", [P, len(ROOTS), 8])
        rsv = sb("rsv", [P, len(ROOTS), 8])
        half = sb("half", [P, 8])
        st = sb("st", [P, 96])
        cols = sb("cols", [P, 2, TT, HEADS])
        rg = sb("rg", [HEADS, 12])
        lamc = sb("lamc", [P, 4])
        wts = sb("wts", [P, 2, TT])
        dest = sb("dest", [P, 2, TT], I32)
        tokid = sb("tokid", [P, 2, TT, 2], I32)
        tab = sb("tab", [1, 2, NE + 1], I32)
        idx = sb("idx", [BLK, 2, 1], I32)
        sink = sb("sink", [P, W2_HEADS])
        bn = sb("bn", [P, 2, 6])
        inv16 = sb("inv16", [P, 16])

        def m(a, *shape):
            v = M[:, a:a + int(np.prod(shape))]
            if len(shape) == 2:
                v = v.rearrange("p (a b) -> p a b", a=shape[0])
            if len(shape) == 3:
                v = v.rearrange("p (a b c) -> p a b c", a=shape[0], b=shape[1])
            return v

        MV, MO = m(0, TT, 512), m(2048, TT, 512)
        QA, KA, AV = m(4096, HEADS, T), m(6144, HEADS, T), m(8192, TT, 512)
        MIXA = m(10240, HEADS, T)
        JUNK3 = m(15872, 2, D)
        JUNK2 = m(0, 2, D)
        PROWS = m(12288, P)[0:N_PARAMS]
        EE = m(12288, 2, 512)
        AD, ATD = m(13312, 512), m(13824, 512)
        DD, AM, ATM = m(14336, 512), m(14848, 512), m(15360, 512)
        ND, SQD, NM, SQM = m(15872, 512), m(16384, 512), m(16896, 512), m(17408, 512)
        RI, RF, RT, RB, RR, RM, REM = (m(14336 + 512 * k, T)[0:HEADS] for k in range(7))
        GTOK = m(13312, TT, 8)
        LAMIN = m(13376, 4, QK)[0:1]
        LAMP = m(13632, 2 * QK)[0:1]
        unheld = m(17408, 2 * BLOCKS_HELD)[0:BLK].bitcast(I32).rearrange("p (n o) -> p n o", o=2)
        QKM = X[:, :, :].rearrange("p t d -> p (t d)").rearrange("p (c t) -> p c t", c=8)
        HN = m(4096, TT, D)
        WR = m(8192, DT, NG + NE)
        BR = m(8480, NG + NE)
        SQS = (SQD, SQM)
        UPPER, ONESB = m(8576, P // 2).bitcast(BF16), m(8640, P // 2).bitcast(BF16)
        LG = m(8704, TT, NG + NE)
        OHG, D4, EXPG = m(8848, TT, NG), m(8864, TT, NG), m(8880, TT, NG)
        E8, C8, H8, OH1, OH2 = (m(8896 + 32 * k, TT, EG) for k in range(5))
        T32, O1, O2 = (m(9056 + 128 * k, TT, NG, EG) for k in range(3))
        OHS = m(9440, TT * NE // 2).bitcast(BF16).rearrange("p (t e) -> p t e", t=TT)
        NB, BEF = m(9568, NE), m(9600, NE)
        TH = m(9632, NE * (PER_EXPERT_MAX - 1))
        IOG, IO8 = m(9856, TT * NG), m(9872, TT * EG)
        IOG4, IO88 = m(9856, TT, NG), m(9872, TT, EG)
        RS = m(9904, 8, TT)
        P2, DM = m(9936, TT), m(9940, TT)
        RANK = m(9952, TT + 1, NE)
        XG, XTG = m(0, D)[0:BLK], m(1024, DT, BLK)
        XTS = as_r("XTS", M_AT + 1536, DT, 2, BLK)
        YB = m(2560, 2, 512)[0:BLK]
        SG, HIDG = m(3584, FT, BLK), m(3840, FT, BLK)
        ids = m(15232, 2 * BLOCKS_HELD)[0:BLK].bitcast(I32).rearrange("p (n o) -> p n o", o=2)
        SUM2 = m(14592, 2 * BLK)
        HIDS = as_r("HIDS", M_AT + 14720, 2, FT, BLK)
        GUS = m(15872, 2, 512)
        HI = [as_r(f"hi{u}", a, UNIT) for u, a in enumerate((HT_AT, M_AT + UNIT, M_AT + 2 * UNIT))]
        YG = m(4096, 2, TT, D)
        BM = m(12288, W2_HEADS, 2 * P)
        DISTI = m(14336, 2 * P)
        Q2, K2, V2, U2, DP = m(0, PAIRS, T), m(2048, T), m(2560, TT, P), m(3072, 4, T), m(5120, 4, T)
        MIX2 = m(7168, DT, T)
        PW = m(11264, 2, T)
        SC2 = m(14336, 3, 2 * 2 * P).rearrange("p n (a k) -> p n a k", a=2)
        PT2 = m(15872, 2, 512)
        ATS = [as_r(f"ats{k}", M_AT + 8192 * k, FFT // 2, T) for k in range(2)]
        SQR = m(16384, 2, T)
        split_hi = [ring_r[k] for k in HI_SLOTS]
        HTS = [v[:, :].rearrange("p (k t) -> p k t", k=DT) for v in (ring_r[X_SLOT], HI[0])]
        LNB1, LNG1 = m(0, D), m(16384, D)
        WP2 = m(16896, 4, P)
        LNG2, LNB2, BG = (HT[:, 2 * k:2 * k + 2, :].rearrange("p a b -> p (a b)") for k in range(3))
        PIN = HT[:, 6:8, :].rearrange("p a b -> p (a b)").rearrange("p (t c) -> p t c", t=TT)
        PET = m(16384, 2, T)
        H5 = m(12288, DT, T)
        H5S = [as_r(f"h5s{k}", M_AT + a, DT, T) for k, a in enumerate((0, 12288))]
        GT = m(4096, 2, 512)
        OUT2 = m(8192, TT, D)

        ps = ctx.enter_context(nc.psum_tensor("ps", [P, 8, 512], F32))
        h_rows = nc.dram_tensor("h_rows", [T, D], F32, kind="Internal").ap()
        slot_tokens = nc.dram_tensor("slot_tokens", [SLOTS, 2], I32, kind="Internal").ap()
        results = nc.dram_tensor("results", [NO_ROW, D], F32, kind="Internal").ap()

        full = [sem(f"bank_full{b}") for b in range(8)]
        empty = [sem(f"bank_empty{b}") for b in range(8)]
        slot_in = [sem(f"slot_in{s}") for s in range(RING)]
        unit_used = sem("unit_used")
        x_in = [sem(f"x_in{t}") for t in range(TT)]
        small_in = sem("small_in")
        wgates_in = sem("wgates_in")
        sink_in = sem("sink_in")
        router_in = sem("router_in")
        consts = sem("consts")
        sumsq = sem("sumsq")
        ms_ready = sem("ms_ready")
        root_done = sem("root_done")
        xn_ready = sem("xn_ready")
        dve_step = sem("dve_step")
        silu_done = sem("silu_done")
        row_dve = sem("row_dve")
        row_act = sem("row_act")
        rows_done = sem("rows_done")
        lam_prod = sem("lam_prod")
        nmax_ready = sem("nmax_ready")
        ad_ready = sem("ad_ready")
        w_ready = sem("w_ready")
        fin_sq = sem("fin_sq")
        fin_in = sem("fin_in")
        fin_ready = sem("fin_ready")
        hn_ready = sem("hn_ready")
        h_out = sem("h_out")
        r_dve = sem("r_dve")
        r_act = sem("r_act")
        oh_ready = sem("oh_ready")
        tab_ready = sem("tab_ready")
        ids_out = sem("ids_out")
        table_in = sem("table_in")
        idx_kept = [sem(f"idx_kept{k}") for k in range(2)]
        waits_met = sem("waits_met")
        idx_in = sem("idx_in")
        rows_in = sem("rows_in")
        xt_full = sem("xt_full")
        xt_gained = sem("xt_gained")
        xt_hi = sem("xt_hi")
        xt_lo = sem("xt_lo")
        w_hi = sem("w_hi")
        w_lo = sem("w_lo")
        gate_full = sem("gate_full")
        up_full = sem("up_full")
        gu_out = sem("gu_out")
        sum_full = sem("sum_full")
        sg_ready = sem("sg_ready")
        hid_gated = sem("hid_gated")
        hid_hi = sem("hid_hi")
        hid_ready = sem("hid_ready")
        y_full = sem("y_full")
        y_left = sem("y_left")
        y_out = sem("y_out")
        yg_in = [sem(f"yg_in{t}") for t in range(TT)]
        x3_ready = sem("x3_ready")
        consts2 = sem("consts2")
        dest_ready = sem("dest_ready")
        pool_step = sem("pool_step")
        wp_in = sem("wp_in")
        pool_ready = sem("pool_ready")
        nmax2 = sem("nmax2")
        exp2 = sem("exp2")
        pr2_ready = sem("pr2_ready")
        ln_in = sem("ln_in")
        ln_ready = sem("ln_ready")
        gates_read = sem("gates_read")
        x1_hi = sem("x1_hi")
        x1_lo = sem("x1_lo")
        w1_hi = sem("w1_hi")
        w1_lo = sem("w1_lo")
        h5_lo = sem("h5_lo")
        h1_hi = sem("h1_hi")
        ff_w_hi = sem("ff_w_hi")
        ff_w_lo = sem("ff_w_lo")
        sqr_ready = sem("sqr_ready")
        at_hi = sem("at_hi")
        at_ready = sem("at_ready")
        late_in = sem("late_in")
        gate_act = sem("gate_act")
        out_ready = sem("out_ready")
        stored = sem("stored")

        turn, turns_of = {}, [0] * 8
        last_turn = {}

        def open_turn(pe, key, bank):
            turn[key] = (bank, turns_of[bank])
            if turns_of[bank]:
                pe.wait_ge(empty[bank], turns_of[bank])
            turns_of[bank] += 1
            return ps[:, bank, :]

        def fill_turn(ins, key):
            ins.then_inc(full[turn[key][0]], 1)

        def filled(eng, key):
            eng.wait_ge(full[turn[key][0]], turn[key][1] + 1)
            return ps[:, turn[key][0], :]

        def leave(ins, key):
            ins.then_inc(empty[turn[key][0]], 1)

        def left(eng, key):
            eng.wait_ge(empty[turn[key][0]], turn[key][1] + 1)

        place, slot_total = {}, [0] * RING
        for n, u in enumerate(UNITS_1):
            s = RAW_SLOTS[n % len(RAW_SLOTS)]
            slot_total[s] += 16
            place[u] = (s, slot_total[s])
        expert_base = list(slot_total)
        slot_total = [c + 16 * NE // 2 for c in slot_total]
        before_in_slot = {}
        last_in_slot = {}
        for n, u in enumerate(UNITS_2):
            if u == "ple":
                s = X_SLOT
            elif n < RING:
                s = (SECOND + n) % RING
            else:
                s = RAW_SLOTS[(n - RING + 1) % len(RAW_SLOTS)]
            before_in_slot[u] = last_in_slot.get(s)
            last_in_slot[s] = u
            slot_total[s] += 16 * DMAS_OF.get(u, 1)
            place[u] = (s, slot_total[s])

        def unit(pe, u):
            pe.wait_ge(slot_in[place[u][0]], place[u][1])
            return ring[:, place[u][0], :]

        def raw_loads(e, odd, s):
            return (e - odd) * 8 + (expert_base[s] + 16)

        def expert_slots(odd):
            return [(len(UNITS_1) + 3 * odd + k) % RING for k in range(3)]

        def each_expert(eng, work, start=None):
            def one(e, odd, ahead):
                before = eng.value_load(tab[0:1, 0, bass.ds(e, 1)], min_val=0, max_val=BLOCKS_MAX)
                extra = eng.value_load(tab[0:1, 1, bass.ds(e, 1)], min_val=0, max_val=PER_EXPERT_MAX - 1)
                if start:
                    start(e, odd)
                with eng.If(extra > 0):
                    with eng.Fori(0, extra) as j:
                        work(e, before + j, odd, False, False)
                work(e, before + extra, odd, True, ahead)

            with eng.Fori(0, NE // 2 - 1) as ii:
                for odd in range(2):
                    one(2 * ii + odd, odd, True)
            one(NE - 2, 0, True)
            one(NE - 1, 1, False)

        def root(name, t):
            return ROOTS.index((name, t))

        def used_up(eng, u):
            if u in last_turn:
                filled(eng, last_turn[u])
            else:
                eng.wait_ge(unit_used, units_counted.index(u) + 1)

        units_counted = [u for u in FF_UNITS if u[:-1] == "down" and u not in ("down3", "down7")]

        def until(eng, s, value):
            eng.wait_ge(s, value)
            eng.sem_inc(waits_met, 1)

        block = ctx.enter_context(nc.Block())

        @block.tensor
        def _(pe):
            def transposes(key, bank, src, n, width=P, idn=None):
                o = open_turn(pe, key, bank)
                idn = ident[:, :] if idn is None else idn
                for c in range(n):
                    ins = pe.transpose(o[:, c * width:(c + 1) * width], src[:, c * P:(c + 1) * P], idn)
                fill_turn(ins, key)

            pe.wait_ge(consts, N_CONSTS)
            pe.wait_ge(small_in, 16 * N_SMALL)
            transposes("prm", 7, PROWS, 1, N_PARAMS, ident[0:N_PARAMS, 0:N_PARAMS])
            for t in range(TT):
                pe.wait_ge(xn_ready, t + 1)
                for c in range(2):
                    transposes(("h", t, c), 2 + (2 * t + c) % 4, X[:, t, c * 512:(c + 1) * 512], 4)

            pe.wait_ge(wgates_in, 16)
            o = open_turn(pe, "gates", 6)
            for t in range(TT):
                left(pe, ("h", t, 0))
                left(pe, ("h", t, 1))
                for k in range(DT):
                    ins = pe.matmul(o[:, t * 8:t * 8 + 8], HT[:, k, t * P:(t + 1) * P],
                                    wgates[:, k, :], start=(k == 0), stop=(k == DT - 1))
                if t < TT - 1:
                    ins.then_inc(gates_read, 1)
            fill_turn(ins, "gates")
            pe.wait_ge(lam_prod, 1)
            o = open_turn(pe, "lam", 7)
            fill_turn(pe.matmul(o[:, 0:2], ones[0:1, :], LAMP[:, 0:2], start=True, stop=True), "lam")

            jobs = [0]

            def project(u, n, key, channel_major):
                j = SPLIT_1.index(u)
                if n == 0:
                    pe.wait_ge(w1_hi, j + 1)
                    pe.wait_ge(w1_lo, j + 1)
                w = [v[:, :].rearrange("p (k c) -> p k c", k=DT) for v in (split_hi[j % 2], ring_r[place[u][0]])]
                o = open_turn(pe, key, jobs[0] % 2)
                jobs[0] += 1
                for i, (wp, xp) in enumerate(((0, 0), (1, 0), (0, 1))):
                    if jobs[0] == 1 and i != 1:
                        pe.wait_ge(x1_lo if xp else x1_hi, TT)
                    for k in range(DT):
                        a, b = w[wp][:, k, n * P:(n + 1) * P], HTS[xp][:, k, :]
                        if not channel_major:
                            a, b = HTS[xp][:, k, n * P:(n + 1) * P], w[wp][:, k, :]
                        ins = pe.matmul(o, a, b, start=(i == 0 and k == 0), stop=(i == 2 and k == DT - 1))
                fill_turn(ins, key)
                last_turn[u] = key

            for n in range(4):
                project("mq", n, ("mq", n), True)
                if n == 0:
                    left(pe, "gates")
                    for g, bank in ((0, 4), (1, 5)):
                        o = open_turn(pe, ("grow", g), bank)
                        for t in range(TT):
                            ins = pe.transpose(o[0:HEADS, t * P:(t + 1) * P],
                                               GTOK[:, t, g * HEADS:(g + 1) * HEADS], ident[:, :])
                        fill_turn(ins, ("grow", g))
            for n in range(4):
                project("mk", n, ("mk", n), True)
            for n in range(4):
                project("mo", n, ("mo", n), False)
            pe.wait_ge(rows_done, 1)
            o = open_turn(pe, "gcols", 4)
            for g, src in ((0, RR), (1, REM)):
                for t in range(TT):
                    ins = pe.transpose(o[:, (g * TT + t) * HEADS:(g * TT + t + 1) * HEADS],
                                       src[:, t * P:(t + 1) * P], ident[0:HEADS, 0:HEADS])
            fill_turn(ins, "gcols")
            names = [(u, n) for u in ("aq", "ak", "av", "mv") for n in range(4)]
            for k, (u, n) in enumerate(names):
                project(u, n, (u, n), False)
                if 1 <= k <= 8:
                    left(pe, names[k - 1])
                    transposes(("T",) + names[k - 1], 6 + k % 2, (ND, NM)[(k - 1) % 2], HEADS)

            def scores(n):
                i, h, kind = ITEMS[n]
                W = (i + 1) * P
                b0, b1, _, _ = BANKS[kind]
                if kind == "d":
                    if h == 0:
                        left(pe, ("T", "aq", i))
                        left(pe, ("T", "ak", i))
                    for c, bank in ((0, b0), (1, b1)):
                        r = slice(c * QK, (c + 1) * QK)
                        o = open_turn(pe, ("S", n, c), bank)
                        pe.matmul(o[:, 0:W], QA[r, h, i * P:W], KA[r, h, 0:W], start=True, stop=False)
                        fill_turn(pe.matmul(o[:, i * P:W], identb[:, :], maskk[:, :],
                                            start=False, stop=True), ("S", n, c))
                else:
                    if h == 0 and i:
                        pe.wait_ge(w_ready, i)
                    o = open_turn(pe, ("S", n, 0), b0)
                    pe.matmul(o[:, 0:W], headsel[:, h, :], wrow[:, 0:W], start=True, stop=False)
                    fill_turn(pe.matmul(o[:, i * P:W], identb[:, :], maskc[:, :],
                                        start=False, stop=True), ("S", n, 0))
                    if n == 1:
                        pe.wait_ge(silu_done, 8)
                    o = open_turn(pe, ("S", n, 1), b1)
                    fill_turn(pe.matmul(o[:, 0:W], QKM[:, h, i * P:W], QKM[:, HEADS + h, 0:W],
                                        start=True, stop=True), ("S", n, 1))

            def turned(n):
                i, h, kind = ITEMS[n]
                if kind == "d":
                    pe.wait_ge(ad_ready, n // 2 + 1)
                else:
                    left(pe, ("S", n, 1))
                transposes(("AT", n), BANKS[kind][2], AD if kind == "d" else AM, i + 1)

            def outputs(n):
                i, h, kind = ITEMS[n]
                left(pe, ("AT", n))
                a, v = (ATD, AV) if kind == "d" else (ATM, MV)
                if n < 2:
                    for t in range(TT):
                        left(pe, ("av" if kind == "d" else "mv", t))
                if h == 0:
                    open_turn(pe, ("O", i, kind), BANKS[kind][3])
                o = ps[:, BANKS[kind][3], :]
                for j in range(i + 1):
                    ins = pe.matmul(o[:, h * P:(h + 1) * P], a[:, j * P:(j + 1) * P],
                                    v[:, j, h * P:(h + 1) * P], start=(j == 0), stop=(j == i))
                if h == HEADS - 1:
                    fill_turn(ins, ("O", i, kind))

            def final(i):
                left(pe, ("O", i, "d"))
                pe.wait_ge(fin_ready, i + 1)
                for kind in "dm":
                    transposes(("F", i, kind), BANKS[kind][2], ND if kind == "d" else NM, HEADS)

            for n in range(len(ITEMS) + 3):
                if n < len(ITEMS):
                    scores(n)
                if 2 <= n <= len(ITEMS) + 1:
                    turned(n - 2)
                if n >= 3:
                    outputs(n - 3)
                if n >= FIN_STEP and (n - FIN_STEP) % 8 == 0:
                    final((n - FIN_STEP) // 8)
            final(TT - 1)

            for i in range(TT):
                for kind in "dm":
                    left(pe, ("F", i, kind))
            for c in range(2):
                w = unit(pe, f"out{c}").rearrange("p (k c) -> p k c", k=DT)
                for t in range(TT):
                    key = ("o", c, t)
                    o = open_turn(pe, key, 2 + (c * TT + t) % 4)
                    for k in range(DT):
                        a = HT[:, k, t * P:(t + 1) * P] if k < HEADS else MIXA[:, k - HEADS, t * P:(t + 1) * P]
                        ins = pe.matmul(o, a, w[:, k, :], start=(k == 0), stop=(k == DT - 1))
                    fill_turn(ins, key)
                last_turn[f"out{c}"] = key

            for t in range(TT):
                pe.wait_ge(hn_ready, t + 1)
                for c in range(2):
                    transposes(("h2", t, c), 2 + (2 * t + c) % 4, HN[:, t, c * 512:(c + 1) * 512], 4)
            pe.wait_ge(router_in, 64)
            o = open_turn(pe, "route", 7)
            E = NG + NE
            for t in range(TT):
                left(pe, ("h2", t, 0))
                left(pe, ("h2", t, 1))
                for k in range(DT):
                    ins = pe.matmul(o[:, t * E:(t + 1) * E], HT[:, k, t * P:(t + 1) * P], WR[:, k, :],
                                    start=(k == 0), stop=(k == DT - 1))
            fill_turn(ins, "route")
            pe.wait_ge(oh_ready, 1)
            o = open_turn(pe, "rank", 6)
            for t in range(TT + 1):
                for j in range(min(t + 1, TT)):
                    ins = pe.matmul(o[:, t * NE:(t + 1) * NE], UPPER if j == t else ONESB,
                                    OHS[:, j, :], start=(j == 0), stop=(j == min(t, TT - 1)))
            fill_turn(ins, "rank")

            def turn_rows(g, a):
                if a == 0:
                    until(pe, rows_in, g * 16 + 16)
                for k in range(4):
                    ins = pe.matmul(ps[:, 6 + a, k * 2 * BLK:(k + 1) * 2 * BLK],
                                    XG[:, (4 * a + k) * P:(4 * a + k + 1) * P], SUM2[0:BLK, :], start=True, stop=True)
                if a == 1:
                    ins.then_inc(xt_full, 1)

            def expert_block(e, g, odd, last, ahead):
                raw = expert_slots(odd)

                def product(u, part):
                    until(pe, w_lo if part else w_hi, e * 6 + (2 * u + 2))
                    w = (ring_r[raw[u]] if part else HI[u])[:, :].rearrange("p (k c) -> p k c", k=DT)
                    for k in range(DT):
                        ins = pe.matmul(ps[:, u, :], XTS[:, k, :, :].rearrange("p s b -> p (s b)"), w[:, k, :],
                                        start=(part == 0 and k == 0), stop=(part == 1 and k == DT - 1))
                    return ins

                def summed(u):
                    until(pe, gu_out, g * 2 + (u + 1))
                    for f in range(FT):
                        ins = pe.matmul(ps[:, 2 + u, f * P:(f + 1) * P], GUS[:, u, f * P:(f + 1) * P], SUM2,
                                        start=True, stop=True)
                    ins.then_inc(sum_full, 1)

                until(pe, xt_lo, g + 1)
                product(0, 0)
                product(0, 1).then_inc(gate_full, 1)
                product(1, 0)
                summed(0)
                product(1, 1).then_inc(up_full, 1)
                turn_rows(g + 1, 0)
                summed(1)
                turn_rows(g + 1, 1)
                until(pe, y_left, g * 2 + 1)
                until(pe, hid_hi, g + 1)
                for c in range(2):
                    for n, (a, part) in enumerate(((0, 0), (1, 0), (0, 1))):
                        if c == 0 and n == 1:
                            until(pe, hid_ready, g + 1)
                        if c == 0 and n == 2:
                            until(pe, w_lo, e * 6 + 6)
                        w = (ring_r[raw[2]] if part else HI[2])[:, :].rearrange("p (k c) -> p k c", k=FT)
                        for f in range(FT):
                            ins = pe.matmul(ps[0:BLK, 4 + c, :], HIDS[:, a, f, :], w[:, f, c * 512:(c + 1) * 512],
                                            start=(n == 0 and f == 0), stop=(n == 2 and f == FT - 1))
                    ins.then_inc(y_full, 1)

            pe.wait_ge(tab_ready, 1)
            pe.wait_ge(consts2, N_CONSTS2)
            turn_rows(0, 0)
            turn_rows(0, 1)
            each_expert(pe, expert_block)

            for t in range(TT):
                pe.wait_ge(x3_ready, t + 1)
                for c in range(2):
                    transposes(("x3", t, c), 2 + (2 * t + c) % 4, X[:, t, c * 512:(c + 1) * 512], 4)
            for t in range(TT):
                left(pe, ("x3", t, 0))
                left(pe, ("x3", t, 1))

            w = unit(pe, "q2").rearrange("p (k c) -> p k c", k=DT)
            for n in range(PAIRS):
                o = open_turn(pe, ("q2", n), n % 2)
                for k in range(DT):
                    ins = pe.matmul(o, w[:, k, n * P:(n + 1) * P], HT[:, k, :], start=(k == 0), stop=(k == DT - 1))
                fill_turn(ins, ("q2", n))
            last_turn["q2"] = ("q2", 3)
            w = unit(pe, "kv2")[:, 0:DT * 2 * P].rearrange("p (k c) -> p k c", k=DT)
            o = open_turn(pe, "k2", 0)
            for k in range(DT):
                ins = pe.matmul(o, w[:, k, 0:P], HT[:, k, :], start=(k == 0), stop=(k == DT - 1))
            fill_turn(ins, "k2")
            o = open_turn(pe, "v2", 1)
            for t in range(TT):
                for k in range(DT):
                    ins = pe.matmul(o[:, t * P:(t + 1) * P], HT[:, k, t * P:(t + 1) * P], w[:, k, P:2 * P],
                                    start=(k == 0), stop=(k == DT - 1))
            fill_turn(ins, "v2")
            last_turn["kv2"] = "v2"
            def pooled(n):
                for q in range(POOL_STEP * n, min(POOL_STEP * (n + 1), 4 * DT)):
                    c, k = divmod(q, DT)
                    if q == 0:
                        unit(pe, "pool2")
                    w = ring[:, place["pool2"][0], :].rearrange("p (k c) -> p k c", k=DT)
                    if k == 0:
                        open_turn(pe, ("u2", c), c % 2)
                    ins = pe.matmul(ps[:, c % 2, :], w[:, k, c * P:(c + 1) * P], HT[:, k, :],
                                    start=(k == 0), stop=(k == DT - 1))
                    if k == DT - 1:
                        fill_turn(ins, ("u2", c))
            last_turn["pool2"] = ("u2", 3)

            def scores2(n):
                i, j = divmod(n, PAIRS)
                lo = P if i == 0 else 0
                for a in range(2):
                    r = slice(a * QK, (a + 1) * QK)
                    o = open_turn(pe, ("S2", n, a), 2 + 2 * (n % 2) + a)
                    fill_turn(pe.matmul(o[:, lo:2 * P], Q2[r, j, i * P:(i + 1) * P],
                                        K2[r, (i - 1) * P + lo:(i + 1) * P], start=True, stop=True),
                              ("S2", n, a))

            def turned2(n):
                i, j = divmod(n, PAIRS)
                pe.wait_ge(pr2_ready, 2 * n + 2)
                o = open_turn(pe, ("PT", n), 6)
                for a in range(2):
                    for b in range(1 if i == 0 else 0, 2):
                        ins = pe.transpose(o[:, (2 * a + b) * P:(2 * a + b + 1) * P],
                                           SC2[:, n % 3, a, b * P:(b + 1) * P], ident[:, :])
                fill_turn(ins, ("PT", n))

            def outputs2(n):
                i, j = divmod(n, PAIRS)
                left(pe, ("PT", n))
                if n == 0:
                    left(pe, "v2")
                if j == 0:
                    open_turn(pe, ("O2", i), 7)
                b0 = 1 if i == 0 else 0
                for a in range(2):
                    for b in range(b0, 2):
                        ins = pe.matmul(ps[a * QK:(a + 1) * QK, 7, j * P:(j + 1) * P],
                                        V2[:, i - 1 + b, a * QK:(a + 1) * QK],
                                        PT2[:, n % 2, (2 * a + b) * P:(2 * a + b + 1) * P],
                                        start=(b == b0), stop=(b == 1))
                if j == PAIRS - 1:
                    fill_turn(ins, ("O2", i))

            left(pe, ("q2", 3))
            left(pe, ("q2", 2))
            left(pe, "k2")
            for n in range(19):
                if n < 16:
                    scores2(n)
                if 2 <= n <= 17:
                    turned2(n - 2)
                if n < 16:
                    pooled(n)
                if n >= 3:
                    outputs2(n - 3)
            pe.wait_ge(wp_in, 16)
            for g in range(4):
                pe.wait_ge(pool_ready, g + 1)
                o = open_turn(pe, ("pw", g), g % 2)
                fill_turn(pe.matmul(o, WP2[:, g, :], DP[:, g, :], start=True, stop=True), ("pw", g))
            for g in range(2, 4):
                left(pe, ("pw", g))
            left(pe, ("O2", 3))
            for c in range(2):
                w = unit(pe, f"mix{c}").rearrange("p (k c) -> p k c", k=DT)
                for t in range(TT):
                    key = ("o2", c, t)
                    o = open_turn(pe, key, 2 + (c * TT + t) % 4)
                    for k in range(DT):
                        ins = pe.matmul(o, MIX2[:, k, t * P:(t + 1) * P], w[:, k, :],
                                        start=(k == 0), stop=(k == DT - 1))
                    fill_turn(ins, key)
                last_turn[f"mix{c}"] = key

            for t in range(TT):
                pe.wait_ge(ln_ready, t + 1)
                for c in range(2):
                    transposes(("h1", t, c), 2 + (2 * t + c) % 4, X[:, t, c * 512:(c + 1) * 512], 4)
            for t in range(TT):
                left(pe, ("h1", t, 0))
                left(pe, ("h1", t, 1))
            for j, u in enumerate(FF_UNITS):
                n = int(u[-1])
                half_ = n // 4
                w = [v[:, :] for v in (split_hi[j % 2], ring_r[place[u][0]])]
                if u[:-1] == "up":
                    w = [v.rearrange("p (k c) -> p k c", k=DT) for v in w]
                    pe.wait_ge(ff_w_hi, j + 1)
                    pe.wait_ge(ff_w_lo, j + 1)
                    for f in range(4):
                        key = ("up", 4 * n + f)
                        o = open_turn(pe, key, f)
                        for i, (a, b) in enumerate(((0, 0), (1, 0), (0, 1))):
                            for k in range(DT):
                                ins = pe.matmul(o, w[a][:, k, f * P:(f + 1) * P], HTS[b][:, k, :],
                                                start=(i == 0 and k == 0), stop=(i == 2 and k == DT - 1))
                        fill_turn(ins, key)
                    last_turn[u] = key
                    continue
                w = [v.rearrange("p (k c) -> p k c", k=4) for v in w]
                if u == "down4":
                    pe.wait_ge(late_in, 64)
                    for t in range(TT):
                        transposes(("pt", t), 4 + t % 4, PIN[:, t, :], 2)
                if n % 4 == 0:
                    for t in range(TT):
                        for c in range(2):
                            open_turn(pe, ("dn", half_, t, c), 2 * t + c)
                    pe.wait_ge(at_ready, 16 * half_ + 16)
                pe.wait_ge(ff_w_hi, j + 1)
                pe.wait_ge(ff_w_lo, j + 1)

                def products(t, c):
                    for i, (a, b) in enumerate(((0, 0), (1, 0), (0, 1))):
                        for k in range(4):
                            ins = pe.matmul(ps[:, 2 * t + c, :], ATS[a][:, 4 * (n % 4) + k, t * P:(t + 1) * P],
                                            w[b][:, k, c * 512:(c + 1) * 512], start=(n % 4 == 0 and i == 0 and k == 0),
                                            stop=(n % 4 == 3 and i == 2 and k == 3))
                    return ins

                for t in range(TT):
                    for c in range(2):
                        ins = products(t, c)
                        if n % 4 == 3:
                            fill_turn(ins, ("dn", half_, t, c))
                if n % 4 == 3:
                    last_turn[u] = ("dn", half_, TT - 1, 1)
                else:
                    ins.then_inc(unit_used, 1)
            for t in range(TT):
                pe.wait_ge(ln_ready, TT + t + 1)
                for c in range(2):
                    transposes(("h5", t, c), 2 * t + c, X[:, t, c * 512:(c + 1) * 512], 4)
            for t in range(TT):
                left(pe, ("pt", t))
            pe.wait_ge(h5_lo, 2 * TT)
            wl = unit(pe, "ple")[:, 0:2 * D].rearrange("p (k c) -> p k c", k=2)
            for c in range(2):
                j = SPLIT_2.index(f"gate{c}")
                pe.wait_ge(ff_w_hi, j + 1)
                pe.wait_ge(ff_w_lo, j + 1)
                w = [v[:, :].rearrange("p (k c) -> p k c", k=DT) for v in (split_hi[j % 2], ring_r[place[f"gate{c}"][0]])]
                for t in range(TT):
                    n = c * TT + t
                    o = open_turn(pe, ("gt", n), n % 4)
                    for i, (a, b) in enumerate(((0, 0), (0, 1), (1, 0))):
                        for k in range(DT):
                            ins = pe.matmul(o, H5S[a][:, k, t * P:(t + 1) * P], w[b][:, k, :],
                                            start=(i == 0 and k == 0), stop=(i == 2 and k == DT - 1))
                    fill_turn(ins, ("gt", n))
                    o = open_turn(pe, ("pl", n), 4 + n % 4)
                    for k in range(2):
                        ins = pe.matmul(o, PET[:, k, t * P:(t + 1) * P], wl[:, k, c * 512:(c + 1) * 512],
                                        start=(k == 0), stop=(k == 1))
                    fill_turn(ins, ("pl", n))

        @block.sync
        def _(sp):
            W1, W2 = A["w_in"][0], A["w_in_2"][0]
            cols_of = {"mq": C_MQ, "mk": C_MK, "mo": C_MO, "aq": C_AQ, "ak": C_AK, "av": C_AV, "mv": C_MV}

            def load(u):
                s = place[u][0]
                dst = ring[:, s, :]
                k8 = dst.rearrange("p (k c) -> p k c", k=DT)

                def put(d, src):
                    sp.dma_start(d, src).then_inc(slot_in[s], 16)

                def columns(w, a, n):
                    return w[:, a:a + n].rearrange("(k p) c -> p k c", p=P)

                if u in cols_of:
                    put(k8, columns(W1, cols_of[u], 512))
                elif u.startswith("out"):
                    put(k8, columns(A["w_out"][0], 512 * int(u[3]), 512))
                elif u == "q2":
                    for h in range(W2_HEADS):
                        c = P * (h % PAIRS) + QK * (h // PAIRS)
                        put(k8[:, :, c:c + QK], columns(W2, 512 + QK * h, QK))
                elif u == "kv2":
                    put(dst[:, 0:DT * 2 * P].rearrange("p (k c) -> p k c", k=DT), columns(W2, 1024, 256))
                elif u == "pool2":
                    put(k8, columns(W2, 0, 512))
                elif u.startswith("mix"):
                    w = A["w_out_2"][0][:, 512 * int(u[3]):512 * int(u[3]) + 512]
                    put(k8[:, 0:4, :], w[0:512].rearrange("(k p) c -> p k c", p=P))
                    for a in range(2):
                        rows_ = w[512 + 256 * a:768 + 256 * a].rearrange("(j d) c -> d j c", d=QK)
                        put(k8[a * QK:(a + 1) * QK, 4:8, :], rows_)
                elif u.startswith("up"):
                    put(k8, columns(A["w_ff1_2"][0], 512 * int(u[2:]), 512))
                elif u.startswith("down"):
                    n = int(u[4:])
                    put(dst.rearrange("p (k c) -> p k c", k=4),
                        A["w_ff2_2"][0][512 * n:512 * n + 512].rearrange("(k p) c -> p k c", p=P))
                elif u == "ple":
                    put(dst[:, 0:2 * D].rearrange("p (k c) -> p k c", k=2),
                        A["w_ple_2"][0].rearrange("(k p) c -> p k c", p=P))
                else:
                    put(k8, columns(A["w_ple_gate_2"][0], 512 * int(u[4]), 512))

            def load_expert(e, odd):
                for s, w, k in zip(expert_slots(odd), ("w_gate", "w_up", "w_down"), (DT, DT, FT)):
                    src = A[w][0, bass.ds(e, 1)].rearrange("e (k p) c -> p (e k) c", p=P)
                    yield s, ring[:, s, :].rearrange("p (k c) -> p k c", k=k), src

            def small(dst, src, s=small_in):
                sp.dma_start(dst, src).then_inc(s, 16)

            def row(name, q):
                return A[name][0].rearrange("(q c) -> q c", q=q)

            small(PROWS[R_N1:R_N1 + 8], row("norm1_w", 8))
            small(PROWS[R_N2:R_N2 + 8], row("norm2_w", 8))
            small(PROWS[R_CB:R_CB + 8], row("conv_b", 8))
            small(PROWS[R_CW:R_CW + 32], A["conv_w"][0].rearrange("w (c p) -> (w c) p", p=P))
            small(PROWS[R_MN:R_MN + 1], A["m_norm_w"])
            small(PROWS[R_AN:R_AN + 1], A["a_norm_w"])
            small(PROWS[R_PS:R_PS + 4], row("pool_scale_2", 4))
            for c in range(2):
                small(PROWS[R_QN:R_QN + 1, c * QK:(c + 1) * QK], A["q_norm_w"])
                small(PROWS[R_KN:R_KN + 1, c * QK:(c + 1) * QK], A["k_norm_w"])
            small(wgates[:, :, :], A["w_in"][0][:, C_GATES:C_GATES + 8].rearrange("(k p) c -> p k c", p=P), wgates_in)
            for k, nm in enumerate(("lambda_q1", "lambda_k1", "lambda_q2", "lambda_k2")):
                small(LAMIN[:, k, :], A[nm])
            small(rg[:, 0:1], A["b_igate"].rearrange("o h -> h o"))
            small(rg[:, 1:2], A["b_fgate"].rearrange("o h -> h o"))
            sp.dma_start(sink[:, :], A["attn_sinks_2"].to_broadcast([P, W2_HEADS])).then_inc(sink_in, 16)
            sp.wait_ge(consts, N_CONSTS)
            sp.dma_start(slot_tokens.rearrange("(p n) o -> p (n o)", p=BLK),
                          unheld[:, :, :].rearrange("p n o -> p (n o)")).then_inc(table_in, 16)

            for n, u in enumerate(UNITS_1):
                if n >= len(RAW_SLOTS):
                    used_up(sp, UNITS_1[n - len(RAW_SLOTS)])
                load(u)
            last_use = {0: "mv", 1: "av", 2: "mv", 5: "mv", 3: "out0", 4: "out1"}
            first_loads = {s: (dst, src) for odd in range(2) for s, dst, src in load_expert(odd, odd)}
            for s, u in last_use.items():
                used_up(sp, u)
                dst, src = first_loads[s]
                sp.dma_start(dst, src).then_inc(slot_in[s], 16)
            sp.wait_ge(tab_ready, 1)

            def freed(e, k):
                end = sp.value_load(tab[0:1, 0, bass.ds(e + 1, 1)], min_val=1, max_val=BLOCKS_MAX)
                sp.wait_ge((gate_full, up_full, y_full)[k], end * 2 if k == 2 else end)

            with sp.Fori(1, NE // 2) as ii:
                for odd in range(2):
                    for k, (s, dst, src) in enumerate(load_expert(2 * ii + odd, odd)):
                        freed(2 * ii + (odd - 2), k)
                        sp.dma_start(dst, src).then_inc(slot_in[s], 16)
            for n, u in enumerate(UNITS_2):
                if n < RING:
                    if n == 3:
                        sp.wait_ge(yg_in[TT - 1], 32)
                    freed(NE - 2 + n // 3, n % 3)
                else:
                    used_up(sp, before_in_slot[u])
                if u == "ple":
                    used_up(sp, "up7")
                load(u)
            res = out[0].rearrange("(t p) c -> p t c", p=P)
            for n in range(2 * TT):
                c, t = divmod(n, TT)
                sp.wait_ge(out_ready, n + 1)
                sp.dma_start(res[:, t, c * 512:(c + 1) * 512], OUT2[:, t, c * 512:(c + 1) * 512]).then_inc(stored, 16)
            sp.wait_ge(stored, 16 * 2 * TT)

        @block.gpsimd
        def _(pool):
            made = [0]

            def const(ins, wait=False):
                ins.then_inc(consts, 1)
                made[0] += 1
                if wait:
                    pool.wait_ge(consts, made[0])

            def select(t, pattern, base, mult, op, fill, wait=False):
                const(pool.affine_select(out=t, in_=t, pattern=pattern, base=base, channel_multiplier=mult,
                                         compare_op=op, fill=fill), wait)

            const(pool.memset(ident[:, :], 0.0))
            const(pool.memset(identb[:, :], 0.0))
            const(pool.memset(maskc[:, :], 0.0))
            const(pool.memset(headsel[:, :, :], 0.0))
            const(pool.memset(maskk[:, :], 0.0))
            const(pool.memset(ones[:, :], 1.0))
            const(pool.memset(half[:, :], -0.5))
            const(pool.memset(unheld[:, :, :], NO_ROW))
            const(pool.memset(idx[:, 1, :], NO_ROW))
            const(pool.memset(tab[:, 0, 0:1], 0))
            const(pool.iota(inv16[:, :], [[1, 16]], base=1, channel_multiplier=0,
                            allow_small_or_imprecise_dtypes=True))
            for k in range(2):
                const(pool.iota(tokid[:, k, :, 0], [[P, TT]], base=0, channel_multiplier=1))
                const(pool.iota(tokid[:, k, :, 1], [[P, TT]], base=k * T, channel_multiplier=1), k == 1)
            select(ident[:, :], [[-1, P]], 0, 1, ALU.not_equal, 1.0)
            select(identb[:, :], [[-1, P]], 0, 1, ALU.not_equal, 1.0)
            select(maskc[:, :], [[-1, P]], 0, 1, ALU.is_ge, NEG)
            select(headsel[:, :, :], [[-1, HEADS], [0, P]], 0, 1, ALU.not_equal, 1.0)
            const(pool.memset(maskk[0:QK, QK:P], NEG))
            assert made[0] == N_CONSTS

            def roots(names, width):
                for nm in names:
                    r = root(*nm)
                    pool.wait_ge(ms_ready, r + 1)
                    pool.tensor_tensor(rsv[:, r, 0:width], msv[:, r, 0:width], half[:, 0:width],
                                       ALU.pow).then_inc(root_done, 1)

            roots([("n1", t) for t in range(TT)], 1)
            roots([(u, t) for u in ("aq", "ak") for t in range(TT)], 8)
            roots([(k, t) for t in range(TT) for k in ("fd", "fm")], HEADS)

            filled(pool, ("O", TT - 1, "m"))
            filled(pool, ("F", TT - 1, "d"))
            pool.memset(XG, 0.0).then_inc(consts2, 1)
            pool.memset(YB, 0.0).then_inc(y_left, 1)
            pool.memset(UPPER, 1.0).then_inc(consts2, 1)
            pool.memset(ONESB, 1.0).then_inc(consts2, 1)
            pool.iota(DISTI, [[-1, 2 * P]], base=P, channel_multiplier=1,
                      allow_small_or_imprecise_dtypes=True).then_inc(consts2, 1)
            pool.iota(IOG, [[0, TT], [1, NG]], base=0, channel_multiplier=0,
                      allow_small_or_imprecise_dtypes=True).then_inc(consts2, 1)
            pool.iota(IO8, [[0, TT], [1, EG]], base=0, channel_multiplier=0,
                      allow_small_or_imprecise_dtypes=True).then_inc(consts2, 1)
            pool.iota(TH, [[0, NE], [BLK, PER_EXPERT_MAX - 1]], base=BLK, channel_multiplier=0,
                      allow_small_or_imprecise_dtypes=True).then_inc(consts2, 1)
            pool.memset(SUM2, 0.0).then_inc(consts2, 1)
            pool.wait_ge(consts2, 8)
            for k in range(-1, 2):
                pool.affine_select(out=SUM2, in_=SUM2, pattern=[[-1, 2 * BLK]], base=k * BLK, channel_multiplier=1,
                                   compare_op=ALU.not_equal, fill=1.0).then_inc(consts2, 1)
                pool.wait_ge(consts2, 10 + k)
            pool.affine_select(out=UPPER, in_=UPPER, pattern=[[1, P]], base=0, channel_multiplier=-1,
                               compare_op=ALU.is_gt, fill=0.0).then_inc(consts2, 1)
            roots([("n2", t) for t in range(TT)], 1)
            for h in range(W2_HEADS):
                pool.tensor_scalar(BM[:, h, :], DISTI, -(2.0 ** -(h + 1)), None, ALU.mult).then_inc(consts2, 1)
            pool.wait_ge(consts2, 12 + W2_HEADS)
            pool.affine_select(out=BM, in_=BM, pattern=[[0, W2_HEADS], [-1, 2 * P]], base=P, channel_multiplier=1,
                               compare_op=ALU.is_ge, fill=NEG).then_inc(consts2, 1)
            pool.wait_ge(consts2, 13 + W2_HEADS)
            pool.affine_select(out=BM, in_=BM, pattern=[[0, W2_HEADS], [1, 2 * P]], base=-1, channel_multiplier=-1,
                               compare_op=ALU.is_ge, fill=NEG).then_inc(consts2, 1)

            pool.wait_ge(table_in, 16)
            pool.wait_ge(dest_ready, 1)
            for k in range(2):
                for t in range(TT):
                    pool.indirect_dma_start(
                        out=slot_tokens, out_offset=bass.IndirectOffsetOnAxis(dest[:, k, t:t + 1], 0),
                        in_=tokid[:, k, t, :], in_offset=None).then_inc(ids_out, 16)
            pool.wait_ge(ids_out, 16 * 2 * TT)
            pool.wait_ge(h_out, 16 * TT)
            pool.wait_ge(tab_ready, 1)

            def pick(k, g):
                pool.tensor_copy(idx[:, k, :], ids[:, bass.ds(g, 1), k]).then_inc(idx_kept[k], 1)

            def gather_rows():
                pool.indirect_dma_start(
                    out=XG, out_offset=None, in_=h_rows,
                    in_offset=bass.IndirectOffsetOnAxis(idx[:, 0, 0:1], 0),
                    bounds_check=T - 1, oob_is_err=False).then_inc(rows_in, 16)

            def scatter_results():
                pool.indirect_dma_start(
                    out=results, out_offset=bass.IndirectOffsetOnAxis(idx[:, 1, 0:1], 0),
                    in_=YB.rearrange("p c n -> p (c n)"), in_offset=None,
                    bounds_check=NO_ROW - 1, oob_is_err=False).then_inc(y_out, 16)

            def move_rows(e, g, odd, last, ahead):
                until(pool, xt_full, g + 1)
                pick(0, g + 1)
                until(pool, idx_kept[0], g + 2)
                gather_rows()
                until(pool, y_left, g * 2 + 1)
                scatter_results()
                until(pool, y_out, g * 16 + 16)
                pick(1, g)
                until(pool, idx_kept[1], g + 1)

            pool.dma_start(ids, slot_tokens.rearrange("(n p) o -> p n o", p=BLK)).then_inc(idx_in, 16)
            pool.wait_ge(idx_in, 16)
            pick(0, 0)
            pool.wait_ge(idx_kept[0], 1)
            gather_rows()
            each_expert(pool, move_rows)
            blocks = pool.value_load(tab[0:1, 0, NE:NE + 1], min_val=0, max_val=BLOCKS_MAX)
            until(pool, y_left, blocks * 2 + 1)
            scatter_results()

            done = [0]

            def step(ins, wait=True):
                ins.then_inc(pool_step, 1)
                done[0] += 1
                if wait:
                    pool.wait_ge(pool_step, done[0])

            for g, w in enumerate(POOL_WINDOWS):
                left(pool, ("u2", g))
                src, k, sh = U2[:, g, :], 0, 1
                while sh < w:
                    dst = PW[:, k, :]
                    step(pool.tensor_copy(dst[:, 0:sh], src[:, 0:sh]), False)
                    step(pool.tensor_tensor(dst[:, sh:T], src[:, sh:T], src[:, 0:T - sh], ALU.add))
                    src, k, sh = dst, 1 - k, 2 * sh
                dst = PW[:, k, :]
                step(pool.tensor_tensor(dst[:, 0:w], src[:, 0:w], inv16[:, 0:w], ALU.mult), False)
                step(pool.tensor_scalar(dst[:, w:T], src[:, w:T], 1.0 / w, None, ALU.mult))
                pool.tensor_tensor(DP[:, g, :], dst, U2[:, g, :], ALU.subtract).then_inc(pool_ready, 1)
                pool.wait_ge(pool_ready, g + 1)
            roots([("l1", t) for t in range(TT)] + [("l2", t) for t in range(TT)], 1)
            for t in range(TT):
                for c in range(2):
                    left(pool, ("h5", t, c))
                    a = (slice(None), slice(4 * c, 4 * c + 4), slice(t * P, (t + 1) * P))
                    pool.tensor_tensor(H5S[1][a], H5[a], H5S[0][a].bitcast(F32), ALU.subtract).then_inc(h5_lo, 1)

        @block.scalar
        def _(act):
            xt = A["x"][0].rearrange("(t p) c -> p t c", p=P)

            def small(dst, src, s):
                act.dma_start(dst, src).then_inc(s, 16)


            for t in range(TT):
                act.dma_start(X[:, t, :], xt[:, t, :]).then_inc(x_in[t], 16)
            for t in range(TT):
                act.wait_ge(x_in[t], 16)
                if t >= 2:
                    act.wait_ge(sumsq, t - 1)
                act.activation(JUNK2[:, t % 2, :], X[:, t, :], ACT.Square, accum_out=st[:, t:t + 1]).then_inc(sumsq, 1)
            def unit_hi(units, j, before, s_hi):
                if before:
                    used_up(act, before)
                s, loads = place[units[j]]
                act.wait_ge(slot_in[s], loads)
                act.activation(split_hi[j % 2][:, :], ring[:, s, :], ACT.Copy).then_inc(s_hi, 1)

            def hi_1(j):
                unit_hi(SPLIT_1, j, SPLIT_1[j - 2] if j >= 2 else None, w1_hi)

            hi_1(0)
            for t in range(TT):
                if t < TT - 1:
                    act.wait_ge(gates_read, t + 1)
                else:
                    filled(act, "gates")
                act.activation(HTS[0][:, :, t * P:(t + 1) * P], HT[:, :, t * P:(t + 1) * P], ACT.Copy).then_inc(x1_hi, 1)
            hi_1(1)
            filled(act, "lam")
            leave(act.activation(lamc[:, 0:2], ps[:, 7, 0:2], ACT.Exp), "lam")

            def silu(c):
                left(act, ("mq", c) if c < 4 else ("mk", c - 4))
                act.activation(QKM[:, c, :], EE[:, c % 2, :], ACT.Silu).then_inc(silu_done, 1)

            silu(0)
            silu(1)
            act.wait_ge(row_dve, 1)
            act.activation(RT, RT, ACT.Exp).then_inc(row_act, 1)
            act.wait_ge(row_act, 1)
            act.activation(RT, RT, ACT.Ln, bias=1.0).then_inc(row_act, 1)
            silu(2)
            act.wait_ge(row_dve, 2)
            act.wait_ge(table_in, 16)
            act.activation(REM, RM, ACT.Exp, scale=-1.0).then_inc(row_act, 1)
            silu(3)
            hi_1(2)
            for c in range(4, 8):
                silu(c)
            hi_1(3)
            for t in range(TT):
                leave(act.activation(MO[:, t, :], filled(act, ("mo", t)), ACT.Sigmoid), ("mo", t))
            names = [(u, n) for u in ("aq", "ak", "av", "mv") for n in range(4)]
            hi_1(4)
            filled(act, "gcols")
            for k, nm in enumerate(names):
                if k in (4, 8):
                    hi_1(4 + k // 4)
                p = filled(act, nm)
                if k < 8:
                    if k >= 2:
                        act.wait_ge(ms_ready, root(*names[k - 2]) + 1)
                    act.activation(SQS[k % 2], p, ACT.Square).then_inc(sumsq, 1)
                else:
                    leave(act.activation((AV if nm[0] == "av" else MV)[:, nm[1], :], p, ACT.Copy), nm)
                if 1 <= k <= 8:
                    u, n = names[k - 1]
                    key = ("T", u, n)
                    q = filled(act, key).rearrange("p (h t) -> p h t", h=HEADS)
                    dst, gain = (QA, R_QN) if u == "aq" else (KA, R_KN)
                    leave(act.activation(dst[:, :, n * P:(n + 1) * P], q, ACT.Copy, scale=prm[:, gain:gain + 1]), key)

            def exps(n):
                i, h, kind = ITEMS[n]
                k, W = n // 2, (i + 1) * P
                if kind == "d":
                    act.wait_ge(nmax_ready, k + 1)
                    if k:
                        act.wait_ge(ad_ready, k)
                    for c in range(2):
                        leave(act.activation(EE[:, c, 0:W], filled(act, ("S", n, c))[:, 0:W], ACT.Exp,
                                       bias=st[:, 18 + 8 * (k % 2) + c:19 + 8 * (k % 2) + c], scale=QK ** -0.5,
                                       accum_out=st[:, 20 + 8 * (k % 2) + c:21 + 8 * (k % 2) + c]), ("S", n, c))
                else:
                    p = filled(act, ("S", n, 0))
                    if k:
                        left(act, ("S", n - 2, 1))
                    if k == 0:
                        left(act, "gcols")
                    leave(act.activation(DD[:, 0:W], p[:, 0:W], ACT.Exp, bias=cols[:, 0, i, h:h + 1]), ("S", n, 0))

            def finals(i):
                act.activation(SQD, filled(act, ("O", i, "d")), ACT.Square).then_inc(fin_sq, 1)
                act.wait_ge(fin_in, i + 1)
                act.activation(SQM, NM, ACT.Square).then_inc(fin_sq, 1)

            def final_out(i):
                for kind, dst, gain in (("d", MIXA, R_AN), ("m", HT, R_MN)):
                    key = ("F", i, kind)
                    q = filled(act, key).rearrange("p (h t) -> p h t", h=HEADS)
                    leave(act.activation(dst[:, 0:HEADS, i * P:(i + 1) * P], q, ACT.Copy, scale=prm[:, gain:gain + 1]), key)

            for n in range(len(ITEMS) + 1):
                if n < len(ITEMS):
                    exps(n)
                if n >= 2 and ITEMS[n - 2][2] == "d":
                    key, W = ("AT", n - 2), (ITEMS[n - 2][0] + 1) * P
                    leave(act.activation(ATD[:, 0:W], filled(act, key)[:, 0:W], ACT.Copy), key)
                if n >= 9 and (n - 9) % 8 == 0:
                    finals((n - 9) // 8)
                if n >= FIN_STEP and (n - FIN_STEP) % 8 == 0:
                    final_out((n - FIN_STEP) // 8)
            finals(TT - 1)
            for t in range(TT):
                act.dma_start(X[:, t, :], xt[:, t, :]).then_inc(x_in[t], 16)
            final_out(TT - 1)
            small(WR[:, :, 0:NG], A["w_group"][0].rearrange("(k p) c -> p k c", p=P), router_in)
            small(WR[:, :, NG:NG + NE], A["w_expert"][0].rearrange("(k p) c -> p k c", p=P), router_in)
            small(BR[:, 0:NG], A["b_group"].to_broadcast([P, NG]), router_in)
            small(BR[:, NG:NG + NE], A["b_expert"].to_broadcast([P, NE]), router_in)
            for t in range(TT):
                left(act, ("o", 0, t))
                left(act, ("o", 1, t))
                if t >= 2:
                    act.wait_ge(sumsq, TT + 8 + t - 1)
                act.activation(JUNK3[:, t % 2, :], X[:, t, :], ACT.Square, accum_out=st[:, 4 + t:5 + t]).then_inc(sumsq, 1)
            for t in range(TT):
                act.wait_ge(hn_ready, t + 1)
                act.dma_start(h_rows[t * P:(t + 1) * P, :], HN[:, t, :]).then_inc(h_out, 16)
            act.wait_ge(r_dve, 1)
            act.activation(EXPG, D4, ACT.Exp).then_inc(r_act, 1)
            act.wait_ge(r_dve, 2)
            act.activation(P2, DM, ACT.Exp).then_inc(r_act, 1)

            def weights_hi(e, u, half_, odd):
                s = expert_slots(odd)[u]
                if half_ == 0:
                    act.wait_ge(slot_in[s], raw_loads(e, odd, s))
                c = slice(half_ * UNIT // 2, (half_ + 1) * UNIT // 2)
                act.activation(HI[u][:, c], ring[:, s, c], ACT.Copy).then_inc(w_hi, 1)

            def rows_hi(g):
                act.wait_ge(xt_gained, g + 1)
                act.activation(XTS[:, :, 0, :], XTG, ACT.Copy).then_inc(xt_hi, 1)

            def block_act(e, g, odd, last, ahead):
                def gate_or_up(u):
                    act.wait_ge((gate_full, up_full)[u], g + 1)
                    act.activation(GUS[:, u, :], ps[:, u, :], ACT.Copy).then_inc(gu_out, 1)

                gate_or_up(0)
                if ahead:
                    weights_hi(e + 1, 0, 0, 1 - odd)
                act.wait_ge(sum_full, g * 2 + 1)
                act.activation(SG, ps[:, 2, :].rearrange("p (f b) -> p f b", f=FT)[:, :, 0:BLK],
                               ACT.Silu).then_inc(sg_ready, 1)
                gate_or_up(1)
                act.wait_ge(hid_gated, g + 1)
                act.activation(HIDS[:, 0, :, :], HIDG, ACT.Copy).then_inc(hid_hi, 1)
                rows_hi(g + 1)
                if ahead:
                    weights_hi(e + 1, 0, 1, 1 - odd)
                    weights_hi(e + 1, 1, 0, 1 - odd)
                    weights_hi(e + 1, 1, 1, 1 - odd)
                act.wait_ge(y_out, g * 16 + 16)
                for c in range(2):
                    act.wait_ge(y_full, g * 2 + (c + 1))
                    act.activation(YB[:, c, :], ps[0:BLK, 4 + c, :], ACT.Copy).then_inc(y_left, 1)
                if ahead:
                    for half_ in range(2):
                        weights_hi(e + 1, 2, half_, 1 - odd)

            filled(act, "route")
            act.wait_ge(h_out, 16 * TT)
            for u in range(3):
                if u == 2:
                    act.wait_ge(dest_ready, 1)
                for half_ in range(2):
                    weights_hi(0, u, half_, 0)
            act.wait_ge(tab_ready, 1)
            rows_hi(0)
            act.preload_act_table(ACT.Silu)
            each_expert(act, block_act)

            blocks = act.value_load(tab[0:1, 0, NE:NE + 1], min_val=0, max_val=BLOCKS_MAX)
            act.wait_ge(y_out, blocks * 16 + 16)
            for t in range(TT):
                for k in range(2):
                    act.dma_start(YG[:, k, t, :], results[k * T + t * P:k * T + (t + 1) * P, :]).then_inc(yg_in[t], 16)

            for t in range(TT):
                leave(act.activation(HT[:, 0:4, t * P:(t + 1) * P],
                                     filled(act, ("x3", t, 0)).rearrange("p (k t) -> p k t", k=4), ACT.Copy), ("x3", t, 0))
            act.dma_start(WP2, A["w_pool_2"][0].rearrange("g c d -> c g d")).then_inc(wp_in, 16)
            for n in range(PAIRS):
                leave(act.activation(Q2[:, n, :], filled(act, ("q2", n)), ACT.Copy), ("q2", n))
            leave(act.activation(K2, filled(act, "k2"), ACT.Copy), "k2")
            leave(act.activation(V2, filled(act, "v2").rearrange("p (t d) -> p t d", t=TT), ACT.Copy), "v2")

            def pt_out(n):
                lo = 1 if n < PAIRS else 0
                dst, src = (v.rearrange("p (a b q) -> p a b q", a=2, b=2)[:, :, lo:2, :]
                            for v in (PT2[:, n % 2, :], filled(act, ("PT", n))))
                leave(act.activation(dst, src, ACT.Copy), ("PT", n))

            for n in range(19):
                if n < 16:
                    lo = P if n < PAIRS else 0
                    b = 32 + 8 * (n % 3)
                    act.wait_ge(nmax2, n + 1)
                    for a in range(2):
                        act.activation(SC2[:, n % 3, a, lo:], SC2[:, n % 3, a, lo:], ACT.Exp,
                                       bias=st[:, b + 2 + a:b + 3 + a], accum_out=st[:, b + 4 + a:b + 5 + a]).then_inc(exp2, 1)
                    act.activation(st[:, b + 6:b + 8], st[:, b + 6:b + 8], ACT.Exp).then_inc(exp2, 1)
                if 2 <= n <= 17:
                    pt_out(n - 2)
                for c in range(4):
                    if n == (DT * c + DT - 1) // POOL_STEP + 1:
                        leave(act.activation(U2[:, c, :], filled(act, ("u2", c)), ACT.Copy), ("u2", c))
                if n >= 6 and (n - 6) % 4 == 0:
                    i = (n - 6) // 4
                    leave(act.activation(MIX2[:, 4:8, i * P:(i + 1) * P],
                                         filled(act, ("O2", i)).rearrange("p (j q) -> p j q", j=PAIRS), ACT.Copy), ("O2", i))
            act.dma_start(LNB1, A["ln1_b_2"].to_broadcast([P, D])).then_inc(ln_in, 16)
            for g in range(4):
                leave(act.activation(MIX2[:, g, :], filled(act, ("pw", g)), ACT.Copy, scale=prm[:, R_PS + g:R_PS + g + 1]), ("pw", g))
            act.dma_start(LNG1, A["ln1_g_2"].to_broadcast([P, D])).then_inc(ln_in, 16)
            def ff_unit_hi(j):
                unit_hi(SPLIT_2, j, FF_UNITS[j - 2] if j >= 2 else f"mix{j}", ff_w_hi)

            ff_unit_hi(0)
            for t in range(TT):
                for c in range(2):
                    act.activation(HTS[0][:, 4 * c:4 * c + 4, t * P:(t + 1) * P],
                                   filled(act, ("h1", t, c)).rearrange("p (k t) -> p k t", k=4), ACT.Copy).then_inc(h1_hi, 1)
            for j, u in enumerate(FF_UNITS):
                ff_unit_hi(j + 1)
                if u[:-1] == "up":
                    for f in range(4 * int(u[-1]), 4 * int(u[-1]) + 4):
                        if f >= 2:
                            act.wait_ge(at_ready, f - 1)
                        leave(act.activation(SQR[:, f % 2, :], filled(act, ("up", f)), ACT.Relu), ("up", f))
                        act.wait_ge(sqr_ready, f + 1)
                        act.activation(ATS[0][:, f % 16, :], SQR[:, f % 2, :], ACT.Copy).then_inc(at_hi, 1)
                if u == "up7":
                    for dst, nm in ((LNG2, "ln2_g_2"), (LNB2, "ln2_b_2"), (BG, "b_ple_gate_2")):
                        act.dma_start(dst, A[nm].to_broadcast([P, D])).then_inc(late_in, 16)
                    act.dma_start(PIN, A["p_2"][0, 0].rearrange("(t p) c -> p t c", p=P)).then_inc(late_in, 16)
                    act.wait_ge(at_ready, FFT)
                    for t in range(TT):
                        leave(act.activation(PET[:, :, t * P:(t + 1) * P],
                                             filled(act, ("pt", t))[:, 0:2 * P].rearrange("p (k t) -> p k t", k=2), ACT.Copy), ("pt", t))
            for t in range(TT):
                for c in range(2):
                    key = ("h5", t, c)
                    a = (slice(None), slice(4 * c, 4 * c + 4), slice(t * P, (t + 1) * P))
                    o = filled(act, key).rearrange("p (k t) -> p k t", k=4)
                    act.activation(H5[a], o, ACT.Copy)
                    leave(act.activation(H5S[0][a], o, ACT.Copy), key)
            ff_unit_hi(len(FF_UNITS) + 1)
            for n in range(2 * TT):
                left(act, ("gt", n))
                act.activation(GT[:, n % 2, :], GT[:, n % 2, :], ACT.Sigmoid).then_inc(gate_act, 1)

        @block.vector
        def _(vec):
            steps = [0]

            def step(ins):
                ins.then_inc(dve_step, 1)
                steps[0] += 1
                vec.wait_ge(dve_step, steps[0])

            def mean_square(r, src, n, width=1, eps=EPS):
                vec.tensor_scalar(msv[:, r, 0:width], src, 1.0 / n, eps, ALU.mult, ALU.add).then_inc(ms_ready, 1)

            def rooted(r):
                vec.wait_ge(root_done, r + 1)
                return rsv[:, r, :]

            vec.wait_ge(consts, N_CONSTS)
            step(vec.reciprocal(inv16[:, :], inv16[:, :]))

            def ms1(t):
                vec.wait_ge(sumsq, t + 1)
                mean_square(t, st[:, t:t + 1], D)

            ms1(0)
            for t in range(TT):
                if t + 1 < TT:
                    ms1(t + 1)
                vec.tensor_scalar(X[:, t, :], X[:, t, :], rooted(t)[:, 0:1], None, ALU.mult).then_inc(xn_ready, 1)
            vec.wait_ge(small_in, 16 * N_SMALL)
            leave(vec.tensor_copy(prm[:, :], filled(vec, "prm")[:, 0:N_PARAMS]), "prm")
            left(vec, "prm")
            step(vec.tensor_scalar(prm[:, R_AN:R_AN + 1], prm[:, R_AN:R_AN + 1], 1.0 - LAMBDA_INIT, None, ALU.mult))

            def gained(key, t, c, first):
                w = prm[:, first + 4 * c:first + 4 * c + 4].unsqueeze(2).to_broadcast([P, 4, P])
                leave(vec.tensor_tensor(HT[:, 4 * c:4 * c + 4, t * P:(t + 1) * P],
                                        filled(vec, key).rearrange("p (k t) -> p k t", k=4), w, ALU.mult), key)

            for t in range(TT):
                for c in range(2):
                    gained(("h", t, c), t, c, R_N1)
            for k in range(2):
                step(vec.tensor_tensor_reduce(LAMP[:, 2:2 + QK], LAMIN[:, 2 * k, :], LAMIN[:, 2 * k + 1, :], 1.0, 0.0,
                                              ALU.mult, ALU.add, LAMP[:, k:k + 1]))
            vec.tensor_copy(LAMP[:, 66:67], LAMP[:, 0:1]).then_inc(lam_prod, 1)

            def unit_lo(units, j, s_hi, s_lo):
                s = place[units[j]][0]
                vec.wait_ge(s_hi, j + 1)
                vec.tensor_tensor(ring_r[s][:, :], ring[:, s, :], split_hi[j % 2][:, :].bitcast(F32),
                                  ALU.subtract).then_inc(s_lo, 1)

            def lo_1(j):
                unit_lo(SPLIT_1, j, w1_hi, w1_lo)

            lo_1(0)
            for t in range(TT):
                vec.wait_ge(x1_hi, t + 1)
                a = (slice(None), slice(None), slice(t * P, (t + 1) * P))
                vec.tensor_tensor(HTS[1][a], HT[a], HTS[0][a].bitcast(F32), ALU.subtract).then_inc(x1_lo, 1)
            leave(vec.tensor_copy(GTOK, filled(vec, "gates")[:, 0:TT * 8].rearrange("p (t g) -> p t g", t=TT)), "gates")
            left(vec, "lam")
            step(vec.tensor_tensor(lamc[:, 3:4], lamc[:, 1:2], lamc[:, 0:1], ALU.subtract))
            step(vec.tensor_scalar(lamc[:, 2:3], lamc[:, 3:4], -LAMBDA_INIT, None, ALU.add))
            lo_1(1)

            def conv(c):
                key = ("mq", c) if c < 4 else ("mk", c - 4)
                p, e = filled(vec, key), EE[:, c % 2, :]
                if c >= 2:
                    vec.wait_ge(silu_done, c - 1)
                w = [prm[:, R_CW + 8 * j + c:R_CW + 8 * j + c + 1] for j in range(4)]
                step(vec.tensor_scalar(e, p, w[3], prm[:, R_CB + c:R_CB + c + 1], ALU.mult, ALU.add))
                for s in (1, 2, 3):
                    ins = vec.scalar_tensor_tensor(out=e[:, s:T], in0=p[:, 0:T - s], scalar=w[3 - s], in1=e[:, s:T],
                                                   op0=ALU.mult, op1=ALU.add)
                    step(ins) if s < 3 else leave(ins, key)

            conv(0)
            conv(1)
            leave(vec.tensor_scalar(RI, filled(vec, ("grow", 0))[0:HEADS], rg[:, 0:1], None, ALU.add), ("grow", 0))
            leave(vec.tensor_scalar(RF, filled(vec, ("grow", 1))[0:HEADS], rg[:, 1:2], None, ALU.add), ("grow", 1))
            left(vec, ("grow", 1))
            vec.scalar_tensor_tensor(out=RT, in0=RF, scalar=-1.0, in1=RF, op0=ALU.mult, op1=ALU.min).then_inc(row_dve, 1)
            conv(2)
            vec.wait_ge(row_act, 2)
            step(vec.scalar_tensor_tensor(out=RF, in0=RF, scalar=0.0, in1=RT, op0=ALU.min, op1=ALU.subtract))
            for j in range(TT):
                s = slice(j * P, (j + 1) * P)
                step(vec.tensor_tensor_scan(RB[:, s], ones[0:HEADS, :], RF[:, s], 0.0, ALU.mult, ALU.add))
            step(vec.tensor_copy(rg[:, 8:8 + TT], RB[:, P - 1:T:P]))
            step(vec.tensor_tensor(wrow[:, :], RI, RB, ALU.subtract))
            step(vec.memset(rg[:, 2:6], 0.0))
            for i in range(TT):
                s = slice(i * P, (i + 1) * P)
                if i:
                    e = rg[:, 7 + i:8 + i]
                    step(vec.tensor_reduce(rg[:, 4:5], wrow[:, (i - 1) * P:i * P], AX, ALU.max))
                    if i > 1:
                        step(vec.tensor_tensor(rg[:, 4:5], rg[:, 4:5], rg[:, 3:4], ALU.max))
                    step(vec.tensor_tensor(rg[:, 3:4], rg[:, 4:5], e, ALU.add))
                    step(vec.tensor_tensor(rg[:, 2:3], rg[:, 2:3], e, ALU.add))
                    step(vec.tensor_tensor(rg[:, 5:6], rg[:, 2:3], rg[:, 3:4], ALU.max))
                step(vec.tensor_tensor_scan(RR[:, s], wrow[:, s], wrow[:, s], rg[:, 5:6], ALU.max, ALU.max))
            vec.tensor_tensor(RM, RB, RR, ALU.add).then_inc(row_dve, 1)
            conv(3)
            vec.wait_ge(row_act, 3)
            vec.wait_ge(row_dve, 2)
            vec.tensor_scalar(RR, RR, -1.0, None, ALU.mult).then_inc(rows_done, 1)
            for c in range(4, 8):
                conv(c)
                if c == 4:
                    lo_1(2)
            lo_1(3)
            leave(vec.tensor_copy(cols[:, :, :, :].rearrange("p a t h -> p (a t h)"), filled(vec, "gcols")[:, 0:2 * TT * HEADS]), "gcols")

            names = [(u, n) for u in ("aq", "ak") for n in range(4)]
            lo_1(4)
            for k, nm in enumerate(names):
                if k == 4:
                    lo_1(5)
                vec.wait_ge(sumsq, TT + k + 1)
                p = filled(vec, nm).rearrange("p (g d) -> p g d", g=8)
                step(vec.tensor_reduce(st[:, 8:16], SQS[k % 2].rearrange("p (g d) -> p g d", g=8), AX, ALU.add))
                mean_square(root(*nm), st[:, 8:16], QK, 8)
                if k >= 2:
                    filled(vec, ("T",) + names[k - 2])
                r = rooted(root(*nm)).unsqueeze(2).to_broadcast([P, 8, QK])
                dst = (ND, NM)[k % 2].rearrange("p (g d) -> p g d", g=8)
                leave(vec.tensor_tensor(dst, p, r, ALU.mult), nm)
            lo_1(6)

            def maximum(n):
                i, h, _ = ITEMS[n]
                k, W = n // 2, (i + 1) * P
                b = 16 + 8 * (k % 2)
                if h == 0 and i:
                    filled(vec, ("S", n - 1, 0))
                    vec.tensor_scalar(wrow[:, 0:i * P], wrow[:, 0:i * P], rg[:, 7 + i:8 + i], None, ALU.add).then_inc(w_ready, 1)
                filled(vec, ("S", n, 0))
                filled(vec, ("S", n, 1))
                step(vec.tensor_reduce(st[:, b:b + 2], ps[:, 2:4, 0:W], AX, ALU.max))
                vec.tensor_scalar(st[:, b + 2:b + 4], st[:, b:b + 2], -QK ** -0.5, None, ALU.mult).then_inc(nmax_ready, 1)

            def decayed(n):
                i, h, _ = ITEMS[n]
                W = (i + 1) * P
                left(vec, ("S", n, 0))
                if n >= 2:
                    filled(vec, ("AT", n - 2))
                d = 64 + 4 * (i % 2) + h
                leave(vec.tensor_tensor_reduce(AM[:, 0:W], filled(vec, ("S", n, 1))[:, 0:W], DD[:, 0:W], HD ** -0.5, 0.0,
                                               ALU.mult, ALU.add, st[:, d:d + 1]), ("S", n, 1))

            def mixed(n):
                i, h, _ = ITEMS[n]
                k, W = n // 2, (i + 1) * P
                b = 16 + 8 * (k % 2)
                for c in range(2):
                    left(vec, ("S", n, c))
                step(vec.reciprocal(st[:, b + 6:b + 8], st[:, b + 4:b + 6]))
                vec.tensor_scalar(EE[:, 0, 0:W], EE[:, 0, 0:W], st[:, b + 6:b + 7], None, ALU.mult).then_inc(dve_step, 1)
                steps[0] += 1
                step(vec.tensor_tensor(st[:, 81:82], st[:, b + 7:b + 8], lamc[:, 2:3], ALU.mult))
                if n >= 2:
                    filled(vec, ("AT", n - 2))
                vec.scalar_tensor_tensor(out=AD[:, 0:W], in0=EE[:, 1, 0:W], scalar=st[:, 81:82], in1=EE[:, 0, 0:W],
                                         op0=ALU.mult, op1=ALU.add).then_inc(ad_ready, 1)

            def at_out(n):
                key, W = ("AT", n), (ITEMS[n][0] + 1) * P
                leave(vec.tensor_copy(ATM[:, 0:W], filled(vec, key)[:, 0:W]), key)

            def heads_of(v):
                return v.rearrange("p (h d) -> p h d", h=HEADS)

            def final(i):
                d = 64 + 4 * (i % 2)
                step(vec.scalar_tensor_tensor(out=st[:, 72:76], in0=st[:, d:d + 4], scalar=-1.0, in1=st[:, d:d + 4],
                                              op0=ALU.mult, op1=ALU.max))
                step(vec.tensor_tensor(st[:, 72:76], st[:, 72:76], cols[:, 1, i, :], ALU.max))
                step(vec.reciprocal(st[:, 76:80], st[:, 72:76]))
                r = st[:, 76:80].unsqueeze(2).to_broadcast([P, HEADS, HD])
                p = filled(vec, ("O", i, "m"))
                if i:
                    filled(vec, ("F", i - 1, "m"))
                leave(vec.tensor_tensor(heads_of(NM), heads_of(p), r, ALU.mult), ("O", i, "m"))
                left(vec, ("O", i, "m"))
                left(vec, ("mo", i))
                vec.tensor_tensor(NM, NM, MO[:, i, :], ALU.mult).then_inc(fin_in, 1)
                for k, (kind, sq, dst) in enumerate((("d", SQD, ND), ("m", SQM, NM))):
                    r = root("f" + kind, i)
                    vec.wait_ge(fin_sq, 2 * i + k + 1)
                    step(vec.tensor_reduce(st[:, 84:88], heads_of(sq), AX, ALU.add))
                    mean_square(r, st[:, 84:88], HD, HEADS)
                    v = rooted(r)[:, 0:HEADS].unsqueeze(2).to_broadcast([P, HEADS, HD])
                    if kind == "d":
                        if i:
                            filled(vec, ("F", i - 1, "d"))
                        leave(vec.tensor_tensor(heads_of(ND), heads_of(filled(vec, ("O", i, "d"))), v, ALU.mult), ("O", i, "d"))
                    else:
                        vec.tensor_tensor(heads_of(NM), heads_of(NM), v, ALU.mult).then_inc(fin_ready, 1)

            for q in range(len(ITEMS) // 2):
                maximum(2 * q)
                if q:
                    at_out(2 * q - 1)
                decayed(2 * q + 1)
                mixed(2 * q)
                if q >= 4 and q % 4 == 0:
                    final(q // 4 - 1)
            at_out(len(ITEMS) - 1)
            final(TT - 1)

            for c in range(2):
                for t in range(TT):
                    vec.wait_ge(x_in[t], 32)
                    s = slice(c * 512, (c + 1) * 512)
                    leave(vec.tensor_tensor(X[:, t, s], X[:, t, s], filled(vec, ("o", c, t)), ALU.add), ("o", c, t))

            def ms2(t):
                vec.wait_ge(sumsq, TT + 8 + t + 1)
                mean_square(root("n2", t), st[:, 4 + t:5 + t], D)

            ms2(0)
            for t in range(TT):
                if t + 1 < TT:
                    ms2(t + 1)
                vec.tensor_scalar(HN[:, t, :], X[:, t, :], rooted(root("n2", t))[:, 0:1], None, ALU.mult).then_inc(hn_ready, 1)
            for t in range(TT):
                for c in range(2):
                    gained(("h2", t, c), t, c, R_N2)

            def over(v, *shape):
                return v.to_broadcast([P] + list(shape))

            E = NG + NE
            vec.wait_ge(router_in, 64)
            leave(vec.tensor_tensor(LG, filled(vec, "route")[:, 0:TT * E].rearrange("p (t e) -> p t e", t=TT),
                                    over(BR.unsqueeze(1), TT, E), ALU.add), "route")
            left(vec, "route")
            vec.wait_ge(consts2, 12)
            step(vec.tensor_reduce(RS[:, 0, :], LG[:, :, 0:NG], AX, ALU.max))
            vec.tensor_tensor(D4, LG[:, :, 0:NG], over(RS[:, 0, :].unsqueeze(2), TT, NG), ALU.subtract).then_inc(r_dve, 1)

            def first_of(dst, hit, iota, n):
                step(vec.scalar_tensor_tensor(out=C8[:, :, 0:n], in0=hit, scalar=-100.0, in1=iota, op0=ALU.mult, op1=ALU.add))
                step(vec.tensor_reduce(RS[:, 1, :], C8[:, :, 0:n], AX, ALU.min))
                step(vec.tensor_tensor(dst, C8[:, :, 0:n], over(RS[:, 1, :].unsqueeze(2), TT, n), ALU.is_equal))

            vec.wait_ge(r_dve, 1)
            step(vec.tensor_scalar(H8[:, :, 0:NG], D4, 0.0, None, ALU.is_equal))
            first_of(OHG, H8[:, :, 0:NG], IOG4, NG)
            le = LG[:, :, NG:E].rearrange("p t (g j) -> p t g j", g=NG)
            step(vec.tensor_tensor(T32, le, over(OHG.unsqueeze(3), TT, NG, EG), ALU.mult))
            step(vec.tensor_reduce(E8, T32.rearrange("p t g j -> p t j g"), AX, ALU.add))
            for k, oh in enumerate((OH1, OH2)):
                step(vec.tensor_reduce(RS[:, 2 + k, :], E8, AX, ALU.max))
                step(vec.tensor_tensor(H8, E8, over(RS[:, 2 + k, :].unsqueeze(2), TT, EG), ALU.is_equal))
                first_of(oh, H8, IO88, EG)
                if k == 0:
                    step(vec.scalar_tensor_tensor(out=E8, in0=oh, scalar=NEG, in1=E8, op0=ALU.mult, op1=ALU.add))
            for o, oh in ((O1, OH1), (O2, OH2)):
                step(vec.tensor_tensor(o, over(OHG.unsqueeze(3), TT, NG, EG), over(oh.unsqueeze(2), TT, NG, EG), ALU.mult))
            O1F, O2F = (o.rearrange("p t g j -> p t (g j)") for o in (O1, O2))
            vec.tensor_tensor(OHS, O1F, O2F, ALU.add).then_inc(oh_ready, 1)
            vec.tensor_tensor(DM, RS[:, 3, :], RS[:, 2, :], ALU.subtract).then_inc(r_dve, 1)
            vec.wait_ge(r_act, 2)
            step(vec.tensor_reduce(RS[:, 4, :], EXPG, AX, ALU.add))
            step(vec.scalar_tensor_tensor(out=RS[:, 5, :], in0=P2, scalar=1.0, in1=RS[:, 4, :], op0=ALU.add, op1=ALU.mult))
            step(vec.reciprocal(wts[:, 0, :], RS[:, 5, :]))
            step(vec.tensor_tensor(wts[:, 1, :], wts[:, 0, :], P2, ALU.mult))
            leave(vec.tensor_copy(RANK, filled(vec, "rank")[:, 0:(TT + 1) * NE].rearrange("p (t e) -> p t e", e=NE)), "rank")
            left(vec, "rank")
            th = TH.rearrange("p (e q) -> p e q", e=NE)
            q7 = PER_EXPERT_MAX - 1
            step(vec.tensor_tensor(th, over(RANK[:, TT, :].unsqueeze(2), NE, q7), th, ALU.is_gt))
            step(vec.tensor_reduce(NB, th, AX, ALU.add))
            step(vec.tensor_copy(tab[:, 1, 0:NE], NB[0:1]))
            step(vec.tensor_scalar(NB, NB, 1.0, None, ALU.add))
            step(vec.tensor_tensor_scan(BEF, ones[:, 0:NE], NB, 0.0, ALU.mult, ALU.add))
            vec.tensor_copy(tab[:, 0, 1:NE + 1], BEF[0:1]).then_inc(tab_ready, 1)
            vec.wait_ge(tab_ready, 1)
            step(vec.tensor_tensor(BEF, BEF, NB, ALU.subtract))
            step(vec.tensor_scalar(NB, BEF, float(BLK), None, ALU.mult))
            step(vec.tensor_tensor(RANK[:, 0:TT, :], RANK[:, 0:TT, :], over(NB.unsqueeze(1), TT, NE), ALU.add))
            for k, o in enumerate((O1F, O2F)):
                step(vec.tensor_tensor(o, o, RANK[:, 0:TT, :], ALU.mult))
                step(vec.tensor_reduce(RS[:, 6 + k, :], o, AX, ALU.add))
            vec.tensor_copy(dest[:, :, :], RS[:, 6:8, :]).then_inc(dest_ready, 1)

            gain = prm[:, R_N2:R_N2 + DT].rearrange("p (a k) -> p a k", a=2).unsqueeze(3).to_broadcast([P, 2, 4, BLK])

            def weights_lo(e, u, odd, half_):
                s = expert_slots(odd)[u]
                c = slice(half_ * UNIT // 2, (half_ + 1) * UNIT // 2)
                vec.wait_ge(w_hi, e * 6 + (2 * u + half_ + 1))
                vec.tensor_tensor(ring_r[s][:, c], ring[:, s, c], HI[u][:, c].bitcast(F32),
                                  ALU.subtract).then_inc(w_lo, 1)

            def rows_gained(g):
                vec.wait_ge(xt_full, g + 1)
                turned = ps[:, 6:8, :].rearrange("p a (k b) -> p a k b", k=4)[:, :, :, 0:BLK]
                vec.tensor_tensor(XTG.rearrange("p (a k) b -> p a k b", a=2), turned, gain,
                                  ALU.mult).then_inc(xt_gained, 1)

            def rows_lo(g):
                vec.wait_ge(xt_hi, g + 1)
                vec.tensor_tensor(XTS[:, :, 1, :], XTG, XTS[:, :, 0, :].bitcast(F32), ALU.subtract).then_inc(xt_lo, 1)

            def block_vec(e, g, odd, last, ahead):
                vec.wait_ge(sg_ready, g + 1)
                vec.wait_ge(sum_full, g * 2 + 2)
                vec.tensor_tensor(HIDG, SG, ps[:, 3, :].rearrange("p (f b) -> p f b", f=FT)[:, :, 0:BLK],
                                  ALU.mult).then_inc(hid_gated, 1)
                vec.wait_ge(hid_hi, g + 1)
                vec.tensor_tensor(HIDS[:, 1, :, :], HIDG, HIDS[:, 0, :, :].bitcast(F32), ALU.subtract).then_inc(hid_ready, 1)
                rows_gained(g + 1)
                rows_lo(g + 1)
                if ahead:
                    for u in range(2):
                        for half_ in range(2):
                            weights_lo(e + 1, u, 1 - odd, half_)

            def down_lo(e, odd):
                for half_ in range(2):
                    weights_lo(e, 2, odd, half_)

            for u in range(2):
                for half_ in range(2):
                    weights_lo(0, u, 0, half_)
            vec.wait_ge(consts2, N_CONSTS2)
            rows_gained(0)
            rows_lo(0)
            each_expert(vec, block_vec, down_lo)

            for t in range(TT):
                vec.wait_ge(yg_in[t], 32)
                step(vec.scalar_tensor_tensor(out=X[:, t, :], in0=YG[:, 0, t, :], scalar=wts[:, 0, t:t + 1], in1=X[:, t, :],
                                              op0=ALU.mult, op1=ALU.add))
                vec.scalar_tensor_tensor(out=X[:, t, :], in0=YG[:, 1, t, :], scalar=wts[:, 1, t:t + 1], in1=X[:, t, :],
                                         op0=ALU.mult, op1=ALU.add).then_inc(x3_ready, 1)

            for t in range(TT):
                leave(vec.tensor_copy(HT[:, 4:8, t * P:(t + 1) * P],
                                      filled(vec, ("x3", t, 1)).rearrange("p (k t) -> p k t", k=4)), ("x3", t, 1))
            vec.wait_ge(sink_in, 16)
            vec.wait_ge(consts2, N_CONSTS2)

            def biased(n):
                i, j = divmod(n, PAIRS)
                lo, b = (P if i == 0 else 0), 32 + 8 * (n % 3)
                if n >= 3:
                    filled(vec, ("PT", n - 3))
                for a in range(2):
                    leave(vec.scalar_tensor_tensor(out=SC2[:, n % 3, a, lo:], in0=filled(vec, ("S2", n, a))[:, lo:2 * P],
                                                   scalar=QK ** -0.5, in1=BM[:, j + PAIRS * a, lo:], op0=ALU.mult, op1=ALU.add),
                          ("S2", n, a))
                left(vec, ("S2", n, 0))
                left(vec, ("S2", n, 1))
                snk = sink[:, j:j + PAIRS + 1:PAIRS]
                step(vec.tensor_reduce(st[:, b:b + 2], SC2[:, n % 3, :, lo:], AX, ALU.max))
                step(vec.tensor_tensor(st[:, b:b + 2], st[:, b:b + 2], snk, ALU.max))
                step(vec.tensor_scalar(st[:, b + 2:b + 4], st[:, b:b + 2], -1.0, None, ALU.mult))
                vec.tensor_tensor(st[:, b + 6:b + 8], snk, st[:, b:b + 2], ALU.subtract).then_inc(nmax2, 1)

            def probabilities(n):
                lo, b = (P if n < PAIRS else 0), 32 + 8 * (n % 3)
                vec.wait_ge(exp2, 3 * n + 3)
                step(vec.tensor_tensor(st[:, b + 4:b + 6], st[:, b + 4:b + 6], st[:, b + 6:b + 8], ALU.add))
                step(vec.reciprocal(st[:, b + 4:b + 6], st[:, b + 4:b + 6]))
                for a in range(2):
                    vec.tensor_scalar(SC2[:, n % 3, a, lo:], SC2[:, n % 3, a, lo:], st[:, b + 4 + a:b + 5 + a], None,
                                      ALU.mult).then_inc(pr2_ready, 1)

            for n in range(17):
                if n < 16:
                    biased(n)
                if n:
                    probabilities(n - 1)

            def residual(c, t, key, scale=ALPHA):
                s = slice(c * 512, (c + 1) * 512)
                leave(vec.scalar_tensor_tensor(out=X[:, t, s], in0=X[:, t, s], scalar=scale, in1=filled(vec, key),
                                               op0=ALU.mult, op1=ALU.add), key)

            def ln_stats(name, t, key):
                b = 48 + 2 * t
                for c in range(2):
                    left(vec, ("o2", c, t) if key == "o2" else ("dn", 1, t, c))
                for c in range(2):
                    step(vec.bn_stats(bn[:, c, :], X[:, t, c * 512:(c + 1) * 512]))
                step(vec.bn_aggr(st[:, b:b + 2], bn[:, :, :].rearrange("p a b -> p (a b)")))
                mean_square(root(name, t), st[:, b + 1:b + 2], 1, 1, LN_EPS)

            def ln_apply(name, t, g, b_):
                b = 48 + 2 * t
                step(vec.tensor_scalar(X[:, t, :], X[:, t, :], st[:, b:b + 1], rooted(root(name, t))[:, 0:1],
                                       ALU.subtract, ALU.mult))
                step(vec.tensor_tensor(X[:, t, :], X[:, t, :], g, ALU.mult))
                vec.tensor_tensor(X[:, t, :], X[:, t, :], b_, ALU.add).then_inc(ln_ready, 1)

            def ff_unit_lo(j):
                unit_lo(SPLIT_2, j, ff_w_hi, ff_w_lo)

            for c in range(2):
                if c == 1:
                    ff_unit_lo(0)
                for t in range(TT):
                    residual(c, t, ("o2", c, t))
                    if c == 1:
                        ln_stats("l1", t, "o2")
            vec.wait_ge(ln_in, 32)
            for t in range(TT):
                ln_apply("l1", t, LNG1, LNB1)
            for t in range(TT):
                for c in range(2):
                    vec.wait_ge(h1_hi, 2 * t + c + 1)
                    a = (slice(None), slice(4 * c, 4 * c + 4), slice(t * P, (t + 1) * P))
                    leave(vec.tensor_tensor(HTS[1][a], filled(vec, ("h1", t, c)).rearrange("p (k t) -> p k t", k=4),
                                            HTS[0][a].bitcast(F32), ALU.subtract), ("h1", t, c))

            for j, u in enumerate(FF_UNITS):
                ff_unit_lo(j + 1)
                n = int(u[-1])
                if u[:-1] == "up":
                    for f in range(4 * n, 4 * n + 4):
                        left(vec, ("up", f))
                        vec.tensor_tensor(SQR[:, f % 2, :], SQR[:, f % 2, :], SQR[:, f % 2, :],
                                          ALU.mult).then_inc(sqr_ready, 1)
                        vec.wait_ge(at_hi, f + 1)
                        vec.tensor_tensor(ATS[1][:, f % 16, :], SQR[:, f % 2, :],
                                          ATS[0][:, f % 16, :].bitcast(F32), ALU.subtract).then_inc(at_ready, 1)
                elif u == "down3":
                    for t in range(TT):
                        for c in range(2):
                            residual(c, t, ("dn", 0, t, c))
            vec.wait_ge(late_in, 64)
            for t in range(TT):
                for c in range(2):
                    left(vec, ("dn", 0, t, c))
                    residual(c, t, ("dn", 1, t, c), 1.0)
                ln_stats("l2", t, "dn")
                ln_apply("l2", t, LNG2, LNB2)

            def gate_in_(n):
                c, t = divmod(n, TT)
                if n >= 2:
                    vec.wait_ge(out_ready, n - 1)
                leave(vec.tensor_tensor(GT[:, n % 2, :], filled(vec, ("gt", n)), BG[:, c * 512:(c + 1) * 512], ALU.add), ("gt", n))

            ff_unit_lo(len(FF_UNITS) + 1)
            gate_in_(0)
            for n in range(2 * TT):
                c, t = divmod(n, TT)
                s = slice(c * 512, (c + 1) * 512)
                if n + 1 < 2 * TT:
                    gate_in_(n + 1)
                vec.wait_ge(gate_act, n + 1)
                leave(vec.tensor_tensor(GT[:, n % 2, :], GT[:, n % 2, :], filled(vec, ("pl", n)), ALU.mult), ("pl", n))
                left(vec, ("pl", n))
                vec.tensor_tensor(OUT2[:, t, s], GT[:, n % 2, :], X[:, t, s], ALU.add).then_inc(out_ready, 1)


_OUT = (1, T, D)


def kernel(**inputs):
    from concourse import bacc
    from concourse.bass_utils import run_bass_kernel_spmd

    nc = bacc.Bacc("TRN2", target_bir_lowering=False, num_devices=1)
    arrays, args = {}, {}
    for name, value in inputs.items():
        a = np.ascontiguousarray(value)
        arrays[f"in_{name}"] = a
        args[name] = nc.dram_tensor(f"in_{name}", a.shape, mybir.dt.from_np(a.dtype), kind="ExternalInput").ap()
    out = nc.dram_tensor("result", _OUT, F32, kind="ExternalOutput").ap()
    build(nc, args, out)
    r = run_bass_kernel_spmd(nc, [arrays], core_ids=[0])
    return r.results[0]["result"]
```
